# Optimizing a Trainium2 kernel written in Bass

```python
import math
import jax, jax.numpy as jnp
from jax import lax
import numpy as np

D_MODEL = 2048
BATCH = 1
SEQ = 256
DEPTH = 1

CTX_LEN = 256
GRID_W = 64
MIX_WIDTH = D_MODEL
MLSTM_HEAD_DIM = 128
MLSTM_HEADS = (MIX_WIDTH // 2) // MLSTM_HEAD_DIM
MLSTM_WIDTH = MLSTM_HEADS * MLSTM_HEAD_DIM
MLSTM_CHUNK = 128
DIFF_V_DIM = 128
DIFF_QK_DIM = DIFF_V_DIM // 2
DIFF_HEADS = (MIX_WIDTH - MLSTM_WIDTH) // DIFF_V_DIM
DIFF_WIDTH = DIFF_HEADS * DIFF_V_DIM
ROPE_FREQS = DIFF_QK_DIM // 4
ROPE_BASE = 10000.0
Q_BLOCK = 128
D_FF = 5632
CONV_W = 3
N_MOD = 6
EPS = 1e-6

OFF_MQ = 0
OFF_MK = MLSTM_WIDTH
OFF_MV = 2 * MLSTM_WIDTH
OFF_MO = 3 * MLSTM_WIDTH
OFF_MG = 4 * MLSTM_WIDTH
OFF_DQ = OFF_MG + 4 * MLSTM_HEADS
OFF_DK = OFF_DQ + DIFF_HEADS * 2 * DIFF_QK_DIM
OFF_DV = OFF_DK + DIFF_HEADS * 2 * DIFF_QK_DIM
IN_COLS = OFF_DV + DIFF_WIDTH


def rmsnorm(a, g):
    a32 = a.astype(jnp.float32)
    y = a32 * lax.rsqrt(jnp.mean(a32 * a32, axis=-1, keepdims=True) + EPS)
    return (y * g.astype(jnp.float32)).astype(a.dtype)

def modulate(h, shift, scale):
    return h * (1 + scale) + shift

def dwconv3(a, w, b):
    ap = jnp.pad(a, ((0, 0), (1, 1), (0, 0)))
    return ap[:, :-2] * w[0] + ap[:, 1:-1] * w[1] + ap[:, 2:] * w[2] + b

def axial_rope_tables(rows, n_lat):
    row = jnp.broadcast_to(jnp.arange(rows, dtype=jnp.float32)[:, None], (rows, GRID_W)).reshape(-1)
    col = jnp.broadcast_to(jnp.arange(GRID_W, dtype=jnp.float32)[None, :], (rows, GRID_W)).reshape(-1)
    inv_freq = ROPE_BASE ** (-jnp.arange(ROPE_FREQS, dtype=jnp.float32) / ROPE_FREQS)
    ang = jnp.stack([row[:, None] * inv_freq, col[:, None] * inv_freq], axis=1)
    ang = jnp.stack([ang, ang], axis=2).reshape(n_lat, 4 * ROPE_FREQS)
    return jnp.cos(ang), jnp.sin(ang)

def rope_2d(x, cos, sin):
    xr = x.reshape(*x.shape[:-1], 2, 2, ROPE_FREQS)
    rot = jnp.stack([-xr[..., 1, :], xr[..., 0, :]], axis=-2).reshape(x.shape)
    return x * cos[:, None, None, :] + rot * sin[:, None, None, :]

def to_mlstm_heads(a):
    B, T, _ = a.shape
    return a.reshape(B, T, MLSTM_HEADS, MLSTM_HEAD_DIM).transpose(0, 2, 1, 3).astype(jnp.float32)

def mlstm_project(p, conv_w, conv_b, b_gate):
    B, T, _ = p.shape
    qk = jax.nn.silu(dwconv3(p[..., OFF_MQ:OFF_MV], conv_w, conv_b))
    q = to_mlstm_heads(qk[..., :MLSTM_WIDTH])
    k = to_mlstm_heads(qk[..., MLSTM_WIDTH:]) * (MLSTM_HEAD_DIM ** -0.5)
    v = to_mlstm_heads(p[..., OFF_MV:OFF_MO])
    g = (p[..., OFF_MG:OFF_DQ].reshape(B, T, 4, MLSTM_HEADS) + b_gate).astype(jnp.float32)
    g = jnp.transpose(g, (2, 0, 3, 1))
    return q, k, v, g[0], jax.nn.log_sigmoid(g[1]), g[2], jax.nn.log_sigmoid(g[3])

def mlstm_chunkwise(q, k, v, i_pre, log_f, state):
    B, H, T, Dh = q.shape
    nc = T // MLSTM_CHUNK

    def to_chunks(a):
        return jnp.moveaxis(a.reshape(B, H, nc, MLSTM_CHUNK, *a.shape[3:]), 2, 0)

    xs = (to_chunks(q), to_chunks(k), to_chunks(v), to_chunks(i_pre), to_chunks(log_f))
    causal = jnp.tril(jnp.ones((MLSTM_CHUNK, MLSTM_CHUNK), dtype=bool))

    def step(carry, inp):
        C, n, m = carry
        qc, kc, vc, ic, fc = inp
        b = jnp.cumsum(fc, axis=-1)
        d_log = jnp.where(causal, b[..., :, None] - b[..., None, :] + ic[..., None, :], -jnp.inf)
        m_inter = b + m[..., None]
        m_t = jnp.maximum(m_inter, jnp.max(d_log, axis=-1))
        w_intra = jnp.exp(d_log - m_t[..., None])
        w_inter = jnp.exp(m_inter - m_t)
        s = jnp.einsum('bhld,bhsd->bhls', qc, kc) * w_intra
        num = w_inter[..., None] * jnp.einsum('bhld,bhde->bhle', qc, C) + jnp.einsum('bhls,bhse->bhle', s, vc)
        den = w_inter * jnp.einsum('bhld,bhd->bhl', qc, n) + jnp.sum(s, axis=-1)
        h = num / jnp.maximum(jnp.abs(den), jnp.exp(-m_t))[..., None]
        b_last = b[..., -1]
        log_w = b_last[..., None] - b + ic
        m_new = jnp.maximum(b_last + m, jnp.max(log_w, axis=-1))
        w_s = jnp.exp(log_w - m_new[..., None])
        decay = jnp.exp(b_last + m - m_new)
        C_new = decay[..., None, None] * C + jnp.einsum('bhs,bhsd,bhse->bhde', w_s, kc, vc)
        n_new = decay[..., None] * n + jnp.einsum('bhs,bhsd->bhd', w_s, kc)
        return (C_new, n_new, m_new), h

    state, hs = lax.scan(step, state, xs)
    return jnp.moveaxis(hs, 0, 2).reshape(B, H, T, Dh), state

def mlstm_output(h, p, g_norm):
    B, H, T, Dh = h.shape
    h = rmsnorm(h.transpose(0, 2, 1, 3), g_norm.reshape(H, Dh)).reshape(B, T, H * Dh)
    return h * jax.nn.sigmoid(p[..., OFF_MO:OFF_MG].astype(jnp.float32))

def mlstm_group(p_lat, p_ctx, conv_w, conv_b, b_gate, g_norm, need_ctx):
    ql, kl, vl, ifl, lfl, ibl, lbl = mlstm_project(p_lat, conv_w, conv_b, b_gate)
    qc, kc, vc, ifc, lfc, ibc, lbc = mlstm_project(p_ctx, conv_w, conv_b, b_gate)
    B = p_lat.shape[0]
    zero = (jnp.zeros((B, MLSTM_HEADS, MLSTM_HEAD_DIM, MLSTM_HEAD_DIM), jnp.float32),
            jnp.zeros((B, MLSTM_HEADS, MLSTM_HEAD_DIM), jnp.float32),
            jnp.zeros((B, MLSTM_HEADS), jnp.float32))

    def rev(*arrs):
        return tuple(jnp.flip(a, axis=2) for a in arrs)

    hc_f, st_f = mlstm_chunkwise(qc, kc, vc, ifc, lfc, zero)
    hl_f, _ = mlstm_chunkwise(ql, kl, vl, ifl, lfl, st_f)
    hc_b, st_b = mlstm_chunkwise(*rev(qc, kc, vc, ibc, lbc), zero)
    hl_b, _ = mlstm_chunkwise(*rev(ql, kl, vl, ibl, lbl), st_b)
    out_lat = mlstm_output(hl_f + jnp.flip(hl_b, axis=2), p_lat, g_norm)
    out_ctx = mlstm_output(hc_f + jnp.flip(hc_b, axis=2), p_ctx, g_norm) if need_ctx else None
    return out_lat, out_ctx

def diff_split(p):
    B, T, _ = p.shape
    q = p[..., OFF_DQ:OFF_DK].reshape(B, T, DIFF_HEADS, 2, DIFF_QK_DIM)
    k = p[..., OFF_DK:OFF_DV].reshape(B, T, DIFF_HEADS, 2, DIFF_QK_DIM)
    v = p[..., OFF_DV:IN_COLS].reshape(B, T, DIFF_HEADS, DIFF_V_DIM)
    return q, k, v

def diff_attend(q, k, v, lam):
    B, Tq = q.shape[:2]
    qb = jnp.moveaxis(q.astype(jnp.float32).reshape(B, Tq // Q_BLOCK, Q_BLOCK, *q.shape[2:]), 1, 0)
    k32 = k.astype(jnp.float32)
    v32 = v.astype(jnp.float32)
    scale = DIFF_QK_DIM ** -0.5

    def one_block(qblk):
        s = jnp.einsum('bqhcd,bkhcd->bhcqk', qblk, k32) * scale
        pr = jax.nn.softmax(s, axis=-1)
        pd = pr[:, :, 0] - lam * pr[:, :, 1]
        return jnp.einsum('bhqk,bkhe->bqhe', pd, v32)

    o = lax.map(one_block, qb)
    return jnp.moveaxis(o, 0, 1).reshape(B, Tq, DIFF_HEADS, DIFF_V_DIM)

def diff_output(o, g_norm, lam_init):
    B, T = o.shape[:2]
    return (rmsnorm(o, g_norm) * (1.0 - lam_init)).reshape(B, T, DIFF_WIDTH)

def diff_group(p_lat, p_ctx, cos, sin, lam, lam_init, g_norm, need_ctx):
    ql, kl, vl = diff_split(p_lat)
    qc, kc, vc = diff_split(p_ctx)
    ql = rope_2d(ql, cos, sin)
    kl = rope_2d(kl, cos, sin)
    k_all = jnp.concatenate([kc.astype(jnp.float32), kl.astype(jnp.float32)], axis=1)
    v_all = jnp.concatenate([vc, vl], axis=1)
    out_lat = diff_output(diff_attend(ql, k_all, v_all, lam), g_norm, lam_init)
    out_ctx = diff_output(diff_attend(qc, kc, vc, lam), g_norm, lam_init) if need_ctx else None
    return out_lat, out_ctx

def conv_ffn(h, w_up, conv_w, conv_b, w_down):
    u = dwconv3(h @ w_up, conv_w, conv_b)
    gate, val = jnp.split(u, 2, axis=-1)
    return (jax.nn.silu(gate) * val) @ w_down

def first_inputs(seed: int = 0) -> dict:
    key = jax.random.key(seed)
    ks = jax.random.split(key, 32)
    f32 = jnp.float32

    def nrm(k, shape, s):
        return jax.random.normal(k, shape, f32) * s

    x = nrm(ks[0], (BATCH, SEQ, D_MODEL), 1.0)
    c = nrm(ks[1], (BATCH, D_MODEL), 1.0)
    ctx = nrm(ks[2], (BATCH, CTX_LEN, D_MODEL), 1.0)
    c_ctx = nrm(ks[3], (D_MODEL,), 1.0)
    w_mod = nrm(ks[4], (DEPTH, D_MODEL, N_MOD * D_MODEL), 0.5 * D_MODEL ** -0.5)
    b_mod = nrm(ks[5], (DEPTH, N_MOD * D_MODEL), 0.02)
    g_pre_mix = 1.0 + nrm(ks[6], (DEPTH, D_MODEL), 0.05)
    g_post_mix = 1.0 + nrm(ks[7], (DEPTH, D_MODEL), 0.05)
    w_in = nrm(ks[8], (DEPTH, D_MODEL, IN_COLS), D_MODEL ** -0.5)
    i_bias = nrm(ks[9], (DEPTH, 2, MLSTM_HEADS), 0.1)
    f_bias = 3.0 + 3.0 * jax.random.uniform(ks[10], (DEPTH, 2, MLSTM_HEADS), f32)
    b_gate = jnp.stack([i_bias[:, 0], f_bias[:, 0], i_bias[:, 1], f_bias[:, 1]], axis=1)
    conv_qk_w = nrm(ks[11], (DEPTH, CONV_W, 2 * MLSTM_WIDTH), CONV_W ** -0.5)
    conv_qk_b = nrm(ks[12], (DEPTH, 2 * MLSTM_WIDTH), 0.02)
    g_mlstm = 1.0 + nrm(ks[13], (DEPTH, MLSTM_WIDTH), 0.05)
    lambda_q1 = nrm(ks[14], (DEPTH, DIFF_QK_DIM), 0.1)
    lambda_k1 = nrm(ks[15], (DEPTH, DIFF_QK_DIM), 0.1)
    lambda_q2 = nrm(ks[16], (DEPTH, DIFF_QK_DIM), 0.1)
    lambda_k2 = nrm(ks[17], (DEPTH, DIFF_QK_DIM), 0.1)
    g_diff = 1.0 + nrm(ks[18], (DEPTH, DIFF_V_DIM), 0.05)
    w_out = nrm(ks[19], (DEPTH, MIX_WIDTH, D_MODEL), MIX_WIDTH ** -0.5)
    g_pre_ffn = 1.0 + nrm(ks[20], (DEPTH, D_MODEL), 0.05)
    g_post_ffn = 1.0 + nrm(ks[21], (DEPTH, D_MODEL), 0.05)
    w_up = nrm(ks[22], (DEPTH, D_MODEL, 2 * D_FF), D_MODEL ** -0.5)
    conv_ffn_w = nrm(ks[23], (DEPTH, CONV_W, 2 * D_FF), CONV_W ** -0.5)
    conv_ffn_b = nrm(ks[24], (DEPTH, 2 * D_FF), 0.02)
    w_down = nrm(ks[25], (DEPTH, D_FF, D_MODEL), D_FF ** -0.5)
    return {"x": x, "c": c, "ctx": ctx, "c_ctx": c_ctx, "w_mod": w_mod, "b_mod": b_mod,
            "g_pre_mix": g_pre_mix, "g_post_mix": g_post_mix, "w_in": w_in, "b_gate": b_gate,
            "conv_qk_w": conv_qk_w, "conv_qk_b": conv_qk_b, "g_mlstm": g_mlstm,
            "lambda_q1": lambda_q1, "lambda_k1": lambda_k1, "lambda_q2": lambda_q2, "lambda_k2": lambda_k2,
            "g_diff": g_diff, "w_out": w_out, "g_pre_ffn": g_pre_ffn, "g_post_ffn": g_post_ffn,
            "w_up": w_up, "conv_ffn_w": conv_ffn_w, "conv_ffn_b": conv_ffn_b, "w_down": w_down}

def first_block(x, c, ctx, c_ctx, w_mod, b_mod, g_pre_mix, g_post_mix, w_in, b_gate,
              conv_qk_w, conv_qk_b, g_mlstm, lambda_q1, lambda_k1, lambda_q2, lambda_k2,
              g_diff, w_out, g_pre_ffn, g_post_ffn, w_up, conv_ffn_w, conv_ffn_b, w_down):
    n_lat = x.shape[1]
    ROWS = n_lat // GRID_W
    cos, sin = axial_rope_tables(ROWS, n_lat)
    for l in range(DEPTH):
        need_ctx = l < DEPTH - 1
        mod = jax.nn.silu(c) @ w_mod[l] + b_mod[l]
        sh1, sc1, ga1, sh2, sc2, ga2 = jnp.split(mod[:, None, :], N_MOD, axis=-1)
        cmod = jax.nn.silu(c_ctx) @ w_mod[l] + b_mod[l]
        csh1, csc1, cga1, csh2, csc2, cga2 = jnp.split(cmod, N_MOD, axis=-1)

        p_lat = modulate(rmsnorm(x, g_pre_mix[l]), sh1, sc1) @ w_in[l]
        p_ctx = modulate(rmsnorm(ctx, g_pre_mix[l]), csh1, csc1) @ w_in[l]
        m_lat, m_ctx = mlstm_group(p_lat, p_ctx, conv_qk_w[l], conv_qk_b[l], b_gate[l], g_mlstm[l], need_ctx)
        lam_init = 0.8 - 0.6 * math.exp(-0.3 * l)
        lam = (jnp.exp(jnp.sum(lambda_q1[l].astype(jnp.float32) * lambda_k1[l].astype(jnp.float32)))
               - jnp.exp(jnp.sum(lambda_q2[l].astype(jnp.float32) * lambda_k2[l].astype(jnp.float32)))
               + lam_init)
        d_lat, d_ctx = diff_group(p_lat, p_ctx, cos, sin, lam, lam_init, g_diff[l], need_ctx)
        y_lat = jnp.concatenate([m_lat, d_lat], axis=-1).astype(x.dtype) @ w_out[l]
        x = x + ga1 * rmsnorm(y_lat, g_post_mix[l])

        h_lat = modulate(rmsnorm(x, g_pre_ffn[l]), sh2, sc2)
        x = x + ga2 * rmsnorm(conv_ffn(h_lat, w_up[l], conv_ffn_w[l], conv_ffn_b[l], w_down[l]), g_post_ffn[l])

        if need_ctx:
            y_ctx = jnp.concatenate([m_ctx, d_ctx], axis=-1).astype(ctx.dtype) @ w_out[l]
            ctx = ctx + cga1 * rmsnorm(y_ctx, g_post_mix[l])
            h_ctx = modulate(rmsnorm(ctx, g_pre_ffn[l]), csh2, csc2)
            ctx = ctx + cga2 * rmsnorm(conv_ffn(h_ctx, w_up[l], conv_ffn_w[l], conv_ffn_b[l], w_down[l]), g_post_ffn[l])
    return x


S5_WIDTH = D_MODEL // 4
S5_GROUP = 16
S5_GROUPS = S5_WIDTH // S5_GROUP
S5_STATE = 64
LRU_WIDTH = 3 * D_MODEL // 4
LRU_HEADS = 12
LRU_HEAD_DIM = LRU_WIDTH // LRU_HEADS
CONV_WIDTH = 4
LRU_C = 8.0
IN_COLS_2 = S5_WIDTH + 2 * LRU_WIDTH + 2 * D_MODEL
MOE_GROUPS = 4
EXPERTS_PER_GROUP = 8
N_EXPERTS = MOE_GROUPS * EXPERTS_PER_GROUP
TOP_K = 2
EXPERT_FF = D_MODEL // 8
NORM_EPS = 1e-6


def rms_norm(x, w):
    x32 = x.astype(jnp.float32)
    y = x32 * lax.rsqrt(jnp.mean(x32 * x32, axis=-1, keepdims=True) + NORM_EPS)
    return (y * w.astype(jnp.float32)).astype(x.dtype)

def _linear_combine(left, right):
    a_l, b_l = left
    a_r, b_r = right
    return a_r * a_l, a_r * b_l + b_r

def s5_branch(u, lam_re, lam_im, log_step, b_re, b_im, c_re, c_im, d_skip, w_glu, b_glu):
    bsz, seqlen, _ = u.shape
    f32 = jnp.float32
    u32 = u.astype(f32).reshape(bsz, seqlen, S5_GROUPS, S5_GROUP)
    lam = lax.complex(lam_re.astype(f32), lam_im.astype(f32))
    step = jnp.exp(log_step.astype(f32))[:, None]
    lam_bar = jnp.exp(lam * step)
    b_c = lax.complex(b_re.astype(f32), b_im.astype(f32))
    b_bar = ((lam_bar - 1.0) / lam)[..., None] * b_c
    bu = jnp.einsum('gpc,blgc->blgp', b_bar, u32.astype(jnp.complex64))
    a = jnp.broadcast_to(lam_bar, bu.shape)
    _, states = lax.associative_scan(_linear_combine, (a, bu), axis=1)
    c_c = lax.complex(c_re.astype(f32), c_im.astype(f32))
    y = jnp.real(jnp.einsum('gcp,blgp->blgc', c_c, states))
    y = y + d_skip.astype(f32).reshape(S5_GROUPS, S5_GROUP) * u32
    y = jax.nn.gelu(y.reshape(bsz, seqlen, S5_WIDTH))
    glu = jax.nn.sigmoid(y @ w_glu.astype(f32) + b_glu.astype(f32))
    return y * glu

def block_diag_linear(x, w, b):
    bsz, seqlen, _ = x.shape
    xh = x.reshape(bsz, seqlen, LRU_HEADS, LRU_HEAD_DIM)
    y = jnp.einsum('blhi,hij->blhj', xh, w.astype(x.dtype))
    return y.reshape(bsz, seqlen, LRU_WIDTH) + b.astype(x.dtype)

def rglru_branch(xb, yb, conv_w, conv_b, w_a, b_a, w_x, b_x, lam):
    f32 = jnp.float32
    seqlen = xb.shape[1]
    x32 = xb.astype(f32)
    xp = jnp.pad(x32, ((0, 0), (CONV_WIDTH - 1, 0), (0, 0)))
    xc = conv_b.astype(f32)
    for k in range(CONV_WIDTH):
        xc = xc + xp[:, k:k + seqlen] * conv_w[k].astype(f32)
    r = jax.nn.sigmoid(block_diag_linear(xc, w_a.astype(f32), b_a.astype(f32)))
    i = jax.nn.sigmoid(block_diag_linear(xc, w_x.astype(f32), b_x.astype(f32)))
    log_a = -LRU_C * r * jax.nn.softplus(-lam.astype(f32))
    a = jnp.exp(log_a)
    mult = jnp.sqrt(-jnp.expm1(2.0 * log_a))
    pos = jnp.arange(seqlen)[None, :, None]
    mult = jnp.where(pos == 0, 1.0, mult)
    _, h = lax.associative_scan(_linear_combine, (a, xc * i * mult), axis=1)
    return h * jax.nn.gelu(yb.astype(f32))

def mixer_sublayer(x, norm_w, w_in, b_gate, s5_lam_re, s5_lam_im, s5_log_step, s5_b_re, s5_b_im,
                   s5_c_re, s5_c_im, s5_d, s5_w_glu, s5_b_glu, lru_conv_w, lru_conv_b, lru_w_a,
                   lru_b_a, lru_w_x, lru_b_x, lru_lambda, w_proj_s5, w_proj_lru, w_out):
    h = rms_norm(x, norm_w)
    proj = h @ w_in
    o1 = S5_WIDTH
    o2 = o1 + LRU_WIDTH
    o3 = o2 + LRU_WIDTH
    u_s5 = proj[..., :o1]
    x_lru = proj[..., o1:o2]
    y_lru = proj[..., o2:o3]
    gates = jax.nn.sigmoid((proj[..., o3:] + b_gate).astype(jnp.float32))
    g_s5 = gates[..., :D_MODEL]
    g_lru = gates[..., D_MODEL:]
    out_s5 = s5_branch(u_s5, s5_lam_re, s5_lam_im, s5_log_step, s5_b_re, s5_b_im,
                       s5_c_re, s5_c_im, s5_d, s5_w_glu, s5_b_glu)
    out_lru = rglru_branch(x_lru, y_lru, lru_conv_w, lru_conv_b, lru_w_a, lru_b_a,
                           lru_w_x, lru_b_x, lru_lambda)
    br_s5 = out_s5.astype(x.dtype) @ w_proj_s5
    br_lru = out_lru.astype(x.dtype) @ w_proj_lru
    merged = (g_s5 * br_s5.astype(jnp.float32) + g_lru * br_lru.astype(jnp.float32)).astype(x.dtype)
    return x + merged @ w_out

def moe_sublayer(x, norm_w, w_rg, b_rg, w_re, b_re, w_e_gate, w_e_up, w_e_down):
    bsz, seqlen, d = x.shape
    f32 = jnp.float32
    ht = rms_norm(x, norm_w).reshape(bsz * seqlen, d)
    h32 = ht.astype(f32)
    g_prob = jax.nn.softmax(h32 @ w_rg.astype(f32) + b_rg.astype(f32), axis=-1)
    g_top, g_idx = lax.top_k(g_prob, 1)
    e_logits = (h32 @ w_re.astype(f32) + b_re.astype(f32)).reshape(-1, MOE_GROUPS, EXPERTS_PER_GROUP)
    e_sel = jnp.take_along_axis(e_logits, g_idx[:, :, None], axis=1)[:, 0]
    e_prob = jax.nn.softmax(e_sel, axis=-1)
    e_top, e_idx = lax.top_k(e_prob, TOP_K)
    e_top = e_top / jnp.sum(e_top, axis=-1, keepdims=True)
    weights = g_top * e_top
    expert_id = g_idx * EXPERTS_PER_GROUP + e_idx
    combine = jnp.sum(jax.nn.one_hot(expert_id, N_EXPERTS, dtype=f32) * weights[..., None], axis=1)
    gate = jnp.einsum('td,edf->tef', ht, w_e_gate)
    up = jnp.einsum('td,edf->tef', ht, w_e_up)
    act = jax.nn.silu(gate) * up * combine[:, :, None].astype(ht.dtype)
    out = jnp.einsum('tef,efd->td', act, w_e_down)
    return x + out.reshape(bsz, seqlen, d)

def second_inputs(seed: int = 0) -> dict:
    key = jax.random.key(seed)
    ks = jax.random.split(key, 40)
    f32 = jnp.float32

    def nrm(k, shape, scale):
        return jax.random.normal(k, shape, f32) * scale

    G, P, GS = S5_GROUPS, S5_STATE, S5_GROUP
    x = nrm(ks[0], (BATCH, SEQ, D_MODEL), 1.0)
    norm_mix_w = 1.0 + nrm(ks[1], (DEPTH, D_MODEL), 0.02)
    w_in = nrm(ks[2], (DEPTH, D_MODEL, IN_COLS_2), D_MODEL ** -0.5)
    b_gate = nrm(ks[3], (DEPTH, 2 * D_MODEL), 0.02)
    s5_lam_re = -0.5 + nrm(ks[4], (DEPTH, G, P), 0.01)
    s5_lam_im = math.pi * jnp.arange(P, dtype=f32) + nrm(ks[5], (DEPTH, G, P), 0.01)
    s5_log_step = jax.random.uniform(ks[6], (DEPTH, G), f32, math.log(1e-3), math.log(1e-1))
    s5_b_re = nrm(ks[7], (DEPTH, G, P, GS), (2.0 * GS) ** -0.5)
    s5_b_im = nrm(ks[8], (DEPTH, G, P, GS), (2.0 * GS) ** -0.5)
    s5_c_re = nrm(ks[9], (DEPTH, G, GS, P), (2.0 * P) ** -0.5)
    s5_c_im = nrm(ks[10], (DEPTH, G, GS, P), (2.0 * P) ** -0.5)
    s5_d = nrm(ks[11], (DEPTH, S5_WIDTH), 1.0)
    s5_w_glu = nrm(ks[12], (DEPTH, S5_WIDTH, S5_WIDTH), S5_WIDTH ** -0.5)
    s5_b_glu = nrm(ks[13], (DEPTH, S5_WIDTH), 0.02)
    lru_conv_w = nrm(ks[14], (DEPTH, CONV_WIDTH, LRU_WIDTH), CONV_WIDTH ** -0.5)
    lru_conv_b = nrm(ks[15], (DEPTH, LRU_WIDTH), 0.02)
    lru_w_a = nrm(ks[16], (DEPTH, LRU_HEADS, LRU_HEAD_DIM, LRU_HEAD_DIM), LRU_HEAD_DIM ** -0.5)
    lru_b_a = nrm(ks[17], (DEPTH, LRU_WIDTH), 0.02)
    lru_w_x = nrm(ks[18], (DEPTH, LRU_HEADS, LRU_HEAD_DIM, LRU_HEAD_DIM), LRU_HEAD_DIM ** -0.5)
    lru_b_x = nrm(ks[19], (DEPTH, LRU_WIDTH), 0.02)
    a0 = jax.random.uniform(ks[20], (DEPTH, LRU_WIDTH), f32, 0.9, 0.999)
    s = a0 ** (1.0 / LRU_C)
    lru_lambda = jnp.log(s) - jnp.log1p(-s)
    w_proj_s5 = nrm(ks[21], (DEPTH, S5_WIDTH, D_MODEL), S5_WIDTH ** -0.5)
    w_proj_lru = nrm(ks[22], (DEPTH, LRU_WIDTH, D_MODEL), LRU_WIDTH ** -0.5)
    w_out = nrm(ks[23], (DEPTH, D_MODEL, D_MODEL), D_MODEL ** -0.5)
    norm_ffn_w = 1.0 + nrm(ks[24], (DEPTH, D_MODEL), 0.02)
    w_router_group = nrm(ks[25], (DEPTH, D_MODEL, MOE_GROUPS), D_MODEL ** -0.5)
    b_router_group = nrm(ks[26], (DEPTH, MOE_GROUPS), 0.01)
    w_router_expert = nrm(ks[27], (DEPTH, D_MODEL, N_EXPERTS), D_MODEL ** -0.5)
    b_router_expert = nrm(ks[28], (DEPTH, N_EXPERTS), 0.01)
    w_e_gate = nrm(ks[29], (DEPTH, N_EXPERTS, D_MODEL, EXPERT_FF), D_MODEL ** -0.5)
    w_e_up = nrm(ks[30], (DEPTH, N_EXPERTS, D_MODEL, EXPERT_FF), D_MODEL ** -0.5)
    w_e_down = nrm(ks[31], (DEPTH, N_EXPERTS, EXPERT_FF, D_MODEL), EXPERT_FF ** -0.5)
    norm_final_w = 1.0 + nrm(ks[32], (D_MODEL,), 0.02)
    return {'x': x, 'norm_mix_w': norm_mix_w, 'w_in': w_in, 'b_gate': b_gate,
            's5_lam_re': s5_lam_re, 's5_lam_im': s5_lam_im, 's5_log_step': s5_log_step,
            's5_b_re': s5_b_re, 's5_b_im': s5_b_im, 's5_c_re': s5_c_re, 's5_c_im': s5_c_im,
            's5_d': s5_d, 's5_w_glu': s5_w_glu, 's5_b_glu': s5_b_glu,
            'lru_conv_w': lru_conv_w, 'lru_conv_b': lru_conv_b, 'lru_w_a': lru_w_a, 'lru_b_a': lru_b_a,
            'lru_w_x': lru_w_x, 'lru_b_x': lru_b_x, 'lru_lambda': lru_lambda,
            'w_proj_s5': w_proj_s5, 'w_proj_lru': w_proj_lru, 'w_out': w_out,
            'norm_ffn_w': norm_ffn_w, 'w_router_group': w_router_group, 'b_router_group': b_router_group,
            'w_router_expert': w_router_expert, 'b_router_expert': b_router_expert,
            'w_e_gate': w_e_gate, 'w_e_up': w_e_up, 'w_e_down': w_e_down, 'norm_final_w': norm_final_w}

def second_block(x, norm_mix_w, w_in, b_gate, s5_lam_re, s5_lam_im, s5_log_step, s5_b_re, s5_b_im,
              s5_c_re, s5_c_im, s5_d, s5_w_glu, s5_b_glu, lru_conv_w, lru_conv_b, lru_w_a, lru_b_a,
              lru_w_x, lru_b_x, lru_lambda, w_proj_s5, w_proj_lru, w_out, norm_ffn_w,
              w_router_group, b_router_group, w_router_expert, b_router_expert,
              w_e_gate, w_e_up, w_e_down, norm_final_w):
    for i in range(DEPTH):
        x = mixer_sublayer(x, norm_mix_w[i], w_in[i], b_gate[i], s5_lam_re[i], s5_lam_im[i],
                           s5_log_step[i], s5_b_re[i], s5_b_im[i], s5_c_re[i], s5_c_im[i], s5_d[i],
                           s5_w_glu[i], s5_b_glu[i], lru_conv_w[i], lru_conv_b[i], lru_w_a[i],
                           lru_b_a[i], lru_w_x[i], lru_b_x[i], lru_lambda[i], w_proj_s5[i],
                           w_proj_lru[i], w_out[i])
        x = moe_sublayer(x, norm_ffn_w[i], w_router_group[i], b_router_group[i],
                         w_router_expert[i], b_router_expert[i], w_e_gate[i], w_e_up[i], w_e_down[i])
    return rms_norm(x, norm_final_w)


def setup_inputs(seed=0):
    out = dict(first_inputs(seed))
    for name, value in second_inputs(seed + 1).items():
        if name != "x":
            out[name + "_2"] = value
    return out


def reference(
    x, c, ctx, c_ctx, w_mod, b_mod, g_pre_mix, g_post_mix, w_in, b_gate, conv_qk_w, conv_qk_b,
    g_mlstm, lambda_q1, lambda_k1, lambda_q2, lambda_k2, g_diff, w_out, g_pre_ffn, g_post_ffn,
    w_up, conv_ffn_w, conv_ffn_b, w_down, norm_mix_w_2, w_in_2, b_gate_2, s5_lam_re_2,
    s5_lam_im_2, s5_log_step_2, s5_b_re_2, s5_b_im_2, s5_c_re_2, s5_c_im_2, s5_d_2, s5_w_glu_2,
    s5_b_glu_2, lru_conv_w_2, lru_conv_b_2, lru_w_a_2, lru_b_a_2, lru_w_x_2, lru_b_x_2,
    lru_lambda_2, w_proj_s5_2, w_proj_lru_2, w_out_2, norm_ffn_w_2, w_router_group_2,
    b_router_group_2, w_router_expert_2, b_router_expert_2, w_e_gate_2, w_e_up_2, w_e_down_2,
    norm_final_w_2,
):
    x = first_block(
        x, c, ctx, c_ctx, w_mod, b_mod, g_pre_mix, g_post_mix, w_in, b_gate, conv_qk_w,
        conv_qk_b, g_mlstm, lambda_q1, lambda_k1, lambda_q2, lambda_k2, g_diff, w_out,
        g_pre_ffn, g_post_ffn, w_up, conv_ffn_w, conv_ffn_b, w_down,
    )
    return second_block(
        x, norm_mix_w_2, w_in_2, b_gate_2, s5_lam_re_2, s5_lam_im_2, s5_log_step_2, s5_b_re_2,
        s5_b_im_2, s5_c_re_2, s5_c_im_2, s5_d_2, s5_w_glu_2, s5_b_glu_2, lru_conv_w_2,
        lru_conv_b_2, lru_w_a_2, lru_b_a_2, lru_w_x_2, lru_b_x_2, lru_lambda_2, w_proj_s5_2,
        w_proj_lru_2, w_out_2, norm_ffn_w_2, w_router_group_2, b_router_group_2,
        w_router_expert_2, b_router_expert_2, w_e_gate_2, w_e_up_2, w_e_down_2, norm_final_w_2,
    )


_drawn_inputs = setup_inputs


def setup_inputs(seed=0):
    import zlib

    import numpy as np

    out = dict(_drawn_inputs(seed))
    spreads = {}
    factors = {'conv_qk_b': 19.947,
     'lambda_q1': 200.0,
     'conv_ffn_b': 3.16,
     'norm_mix_w_2': 2.921,
     'b_gate_2': 5.722,
     's5_lam_re_2': 200.0,
     's5_b_re_2': 2.706,
     's5_b_im_2': 2.87,
     's5_c_re_2': 2.853,
     's5_c_im_2': 3.734,
     's5_b_glu_2': 40.933,
     'lru_b_a_2': 26.463,
     'lru_b_x_2': 6.161,
     'b_router_group_2': 39.132,
     'b_router_expert_2': 35.013,
     'norm_final_w_2': 21.508,
     'lambda_q2': 2.678,
     'norm_ffn_w_2': 8.0}
    for name, (base, spread) in spreads.items():
        noise = np.random.default_rng([zlib.crc32(name.encode()), seed]).standard_normal(out[name].shape)
        drawn = base * np.exp(spread * noise) if base else spread * noise
        out[name] = __import__('jax').numpy.asarray(drawn.astype(out[name].dtype))
    for name, factor in factors.items():
        out[name] = (out[name] * factor).astype(out[name].dtype)
    return out
```

```python
import math
from contextlib import ExitStack

import numpy as np

import concourse.bass as bass
from concourse import mybir

F32 = mybir.dt.float32
F32R = mybir.dt.float32r
ALU = mybir.AluOpType
ACT = mybir.ActivationFunctionType
AX = mybir.AxisListType

P = 128
D = 2048
KT = D // P
T = 256
TT = T // P
NB = 512
EPS = 1e-6
HEADS = 8
D_FF = 5632
FT = D_FF // P
S5_TILES = 4
ST_TILES = 16
LRU_TILES = 12
EXPERTS = 32
EXPERT_GROUPS = 4
E_FF = 256
GELU_C = math.sqrt(2.0 / math.pi)
BIG = 1.0e30
RING = 4
SLOT_K = 4

COLS = [("c", 16), ("c_ctx", 16), ("g_pre_mix", 16), ("g_post_mix", 16), ("g_pre_ffn", 16),
        ("g_post_ffn", 16), ("norm_mix", 16), ("norm_ffn", 16), ("norm_final", 16), ("b_mod", 96),
        ("conv_qk_w", 48), ("conv_qk_b", 16), ("g_mlstm", 8), ("g_diff", 1),
        ("conv_ffn_w", 3 * 2 * FT), ("conv_ffn_b", 2 * FT), ("b_gate2", 32),
        ("lam_re", ST_TILES), ("lam_im", ST_TILES), ("log_step", ST_TILES), ("s5_d", 4), ("b_glu", 4),
        ("lru_conv_w", 48), ("lru_conv_b", 12), ("lru_b_a", 12), ("lru_b_x", 12), ("lru_lambda", 12)]
COL_AT = {}
_at = 0
for _name, _n in COLS:
    COL_AT[_name] = (_at, _n)
    _at += _n
N_COLS = _at

C_ID, C_REV, C_MF, C_MB, C_ROT, C_PAIR, C_IOTA, C_COS, C_SIN = 0, 128, 256, 384, 512, 640, 642, 658, 914
N_CONST, N_CONST_ALL = 658, 1170


def shape_constants():
    cst = np.zeros((P, N_CONST_ALL), np.float32)
    cst[:, C_ID:C_ID + P] = np.eye(P)
    cst[:, C_REV:C_REV + P] = np.eye(P)[:, ::-1]
    s, t = np.arange(P)[:, None], np.arange(P)[None, :]
    cst[:, C_MF:C_MF + P] = np.where(s <= t, 0.0, -BIG)
    cst[:, C_MB:C_MB + P] = np.where(s >= t, 0.0, -BIG)
    for m in range(P):
        if (m % 32) < 16:
            cst[m + 16, C_ROT + m] = -1.0
        else:
            cst[m - 16, C_ROT + m] = 1.0
    inv = (np.float32(10000.0) ** (-np.arange(16, dtype=np.float32) / np.float32(16))).astype(np.float32)
    tok = np.arange(T)
    pos = np.stack([tok // 64, tok % 64]).astype(np.float32)
    for m in range(P):
        i = m % 64
        ang = pos[i // 32] * inv[i % 16]
        cst[m, C_COS:C_COS + T] = np.cos(ang)
        cst[m, C_SIN:C_SIN + T] = np.sin(ang)
    cst[0:2, C_PAIR] = 1.0
    cst[2:4, C_PAIR + 1] = 1.0
    cst[:, C_IOTA:C_IOTA + 16] = np.arange(16)
    return cst


MOD_FIRST = 8
MOD_REST = 6 * D // NB - MOD_FIRST


class Gemm:

    def __init__(self, name, blocks, slots, dmas=1, stages=("free",), extra=0):
        self.name, self.blocks, self.slots, self.dmas, self.stages = name, blocks, slots, dmas, stages
        self.extra = extra


CONV = ("a1", "free", "a2", "d2")
GEMMS = [Gemm("mod", MOD_FIRST, 4),
         Gemm("mk", 2, 4, 1, CONV, 2), Gemm("mv", 2, 4, extra=2), Gemm("dk", 2, 4, extra=2), Gemm("dv", 2, 4, extra=2),
         Gemm("mq", 2, 4, 1, CONV), Gemm("dq", 2, 4), Gemm("mo", 2, 4),
         Gemm("wout", 4, 4)]
FFN_PARTS = [(0, 8), (8, 8), (16, 6)]
UP = ("a1", "free", "a2", "d2", "a3", "d3")
for _i, (_f, _n) in enumerate(FFN_PARTS):
    GEMMS += [Gemm(f"up{_i}", _n, 4, 2, UP), Gemm(f"down{_i}", 4, _n // 2)]
GEMMS += [Gemm("in_u", 1, 4), Gemm("in_x", 3, 4, 1, ("a1", "free")),
          Gemm("in_y", 3, 4, 1, ("a1", "d1", "a2", "free")), Gemm("glu", 1, 1)]
for _i in range(4):
    GEMMS += [Gemm(f"gates{_i}", 2, 4), Gemm(f"proj{_i}", 1, 4, 1, ("free", "d2"))]
GEMMS += [Gemm("out2", 4, 4)]
for _i in range(4):
    GEMMS += [Gemm(f"moe_up{_i}", 8, 4, 2, ("a2", "free", "d2", "a3", "d3")), Gemm(f"moe_down{_i}", 4, 4)]
G = {g.name: g for g in GEMMS}
_slot, _split, _block, _ring, _stage, RING_AT = 0, 0, 0, [0] * RING, {}, []
for _g in GEMMS:
    _g.s0, _g.m0, _g.b0, _g.base = _slot, _split, _block, dict(_stage)
    for _s in range(_g.blocks * _g.slots * (1 + _g.extra)):
        _r = len(RING_AT) % RING
        _ring[_r] += 16 * _g.dmas
        RING_AT.append(_ring[_r])
    for _s in _g.stages:
        _stage[_s] = _stage.get(_s, 0) + _g.blocks
    _slot = len(RING_AT)
    _split += _g.blocks * _g.slots
    _block += _g.blocks
for _g, _next in zip(GEMMS, GEMMS[1:] + [None]):
    _g.next = _next
KB = 1024
TWO_PI = 6.2831845
APPLY = {"h1": 0, "mix": 8, "ffn": 12, "mix2": 16, "lru": 20, "merged": 24, "moe": 28}
TMPS = {"ffn": 0, "mix2": 4, "moe": 8}


class Steps:

    def __init__(self, eng, sem):
        self.eng, self.sem, self.n, self.dyn = eng, sem, 0, 0

    def __call__(self, ins):
        ins.then_inc(self.sem, 1)
        self.n += 1
        self.eng.wait_ge(self.sem, self.dyn + self.n)


def program(nc, A):
    ctx = ExitStack()
    base = (nc.sbuf_base + 63) // 64 * 64

    def at(name, shape, off, dt=F32):
        return nc.alloc_sbuf_tensor_at(name, shape, dt, offset=base + off)

    sem_of = {}

    def sem(name):
        if name not in sem_of:
            sem_of[name] = ctx.enter_context(nc.semaphore(name))
        return sem_of[name]

    with ctx:
        RAW = at("w_raw", [P, RING, SLOT_K, NB], 0)
        WHI = at("w_hi", [P, 2, SLOT_K, NB], 32 * KB, F32R)
        WLO = at("w_lo", [P, 2, SLOT_K, NB], 48 * KB, F32R)
        A0, B0 = 64 * KB, 128 * KB
        H1HI = at("h1_hi", [P, 2, KT, T], A0, F32R)
        H1LO = at("h1_lo", [P, 2, KT, T], A0 + 32 * KB, F32R)
        MQ = at("m_q", [P, HEADS, T], A0 + 16 * KB)
        DQ = at("d_q", [P, HEADS, T], A0 + 24 * KB)
        MO = at("m_o", [P, HEADS, T], A0 + 48 * KB)
        QTH = at("q_tanh", [P, 4, T], A0 + 56 * KB)
        MIX = at("mixed", [P, KT, T], A0 + 32 * KB)
        MW = at("m_weights", [P, 2, 4, T], A0)
        MP = at("m_probs", [P, 2, 4, T], A0 + 8 * KB)
        MH = at("m_h", [P, TT, 4, P], A0)
        MSQ = at("m_hsq", [P, TT, 4, P], A0 + 4 * KB)
        NUM = at("m_num", [P, 2, TT, 4, P], A0 + 56 * KB)
        DE = at("d_exp", [P, 2, 2, NB], A0)
        DPT = at("d_probsT", [P, 2, 4, P], A0 + 8 * KB)
        DP = at("d_probs", [P, 2, NB], A0 + 12 * KB)
        DO = at("d_out", [P, TT, HEADS, P], A0 + 16 * KB)
        DSQ = at("d_osq", [P, TT, HEADS, P], A0)
        RT1 = at("rope_1", [P, 2, T], A0 + 56 * KB)
        RT2 = at("rope_2", [P, 2, T], A0 + 58 * KB)
        HHI = at("h_hi", [P, KT, T], A0, F32R)
        HLO = at("h_lo", [P, KT, T], A0 + 16 * KB, F32R)
        AHI = at("act_hi", [P, KT, T], A0 + 32 * KB, F32R)
        ALO = at("act_lo", [P, KT, T], A0 + 48 * KB, F32R)
        XIN = at("x_in", [P, 2, KT, T], B0)
        SQW = at("squares_wide", [P, 4, 4, 2, T], A0)
        TMPW = at("h_tmp_wide", [P, 2, 4, T], B0 + 48 * KB)
        MROW = at("mod_rows", [4, 2, NB], B0 + 56 * KB)
        C4 = at("c_pair", [P, KT, 4], B0 + 60 * KB, F32R)
        C4F = at("c_silu", [P, 4, KT], B0 + 60 * KB + 256)
        RBW = at("rstd_wide", [P, 2, T], B0 + 60 * KB + 512)
        LAMV = at("lambdas", [P, 4, 64], B0 + 62 * KB + 512)
        LAMP = at("lambda_products", [P, 2, 64], B0 + 63 * KB + 512)
        MK = at("m_k", [P, HEADS, 2, T], B0)
        MV = at("m_v", [P, 4, HEADS, 129], B0 + 16 * KB)
        DK = at("d_k", [P, HEADS, 2, T], B0 + 16 * KB + 16512)
        DV = at("d_v", [P, 4, HEADS, P], B0 + 32 * KB + 16512)
        KTH = at("k_tanh", [P, 4, 2, T], B0 + 32 * KB + 16512)
        GALL = at("gates_all", [4 * HEADS, 2 * T], B0 + 16 * KB)
        GROW = at("gates_rows", [HEADS, 4, 2 * T], B0 + 18 * KB)
        GS = at("gates_scan", [HEADS, 3, 2, 2 * T], B0 + 26 * KB)
        WG = at("w_gates", [P, KT, 32], B0 + 38 * KB)
        WGH = at("w_gates_hi", [P, KT, 32], B0 + 40 * KB, F32R)
        WGL = at("w_gates_lo", [P, KT, 32], B0 + 42 * KB, F32R)
        X = at("x_res", [P, KT, T], B0)
        Y = at("y_sub", [P, KT, T], B0 + 16 * KB)
        SQ = at("squares", [P, 2, 4, T], B0 + 48 * KB)
        TMP = at("h_tmp", [P, 2, 4, T], B0 + 56 * KB)
        UC = at("up_conv", [P, 2, 4, T], B0 + 32 * KB)
        UTH = at("up_tanh", [P, 2, 2, T], B0 + 40 * KB)
        UACT = at("up_act", [P, 2, 2, T], B0 + 44 * KB)
        U5 = at("s5_u", [P, S5_TILES, T], B0 + 16 * KB)
        XC = at("lru_x", [P, LRU_TILES, T], B0 + 20 * KB)
        YG = at("lru_y", [P, LRU_TILES, T], B0 + 32 * KB)
        YSQ = at("lru_ysq", [P, 4, T], B0 + 44 * KB)
        YTH = at("lru_yth", [P, 4, T], B0 + 48 * KB)
        S5B = at("s5_b", [P, 2, 4, P], B0 + 52 * KB)
        S5C = at("s5_c", [P, 2, ST_TILES, 32], B0 + 56 * KB)
        S5S = at("s5_small", [P, 20, ST_TILES], B0 + 60 * KB)
        ECS = at("s5_phase", [P, 2, 4, T], A0 + 32 * KB)
        ET = at("s5_e12", [P, 2, 4, T], A0 + 40 * KB)
        EX = at("s5_angle", [P, 2, 2, 16, 16], A0 + 40 * KB)
        EXR = at("s5_round", [P, 2, 2, 16, 16], A0 + 44 * KB)
        ESC = at("s5_sincos", [P, 2, 2, 16, 16], A0 + 48 * KB)
        SM1 = at("s5_m1", [P, 2, T], A0 + 52 * KB)
        SM2 = at("s5_m2", [P, 2, T], A0 + 54 * KB)
        SV = at("s5_v", [P, 2, T], A0 + 56 * KB)
        SZ = at("s5_z", [P, 2, T], A0 + 58 * KB)
        SST = at("s5_states", [P, 2, 2, T], A0 + 60 * KB)
        Y5B = at("s5_yb", [P, S5_TILES, T], B0 + 48 * KB)
        GHI = at("glu_hi", [P, S5_TILES, T], A0 + 32 * KB, F32R)
        GLO = at("glu_lo", [P, S5_TILES, T], A0 + 36 * KB, F32R)
        LH = LRU_TILES // 2
        LW = at("lru_w", [P, 2, LH, P], A0 + 32 * KB)
        LR = at("lru_r", [P, LH, T], A0 + 38 * KB)
        LI = at("lru_i", [P, LH, T], A0 + 44 * KB)
        LA = at("lru_a", [P, LH, T], A0 + 50 * KB)
        LT = at("lru_t", [P, LH, T], A0 + 56 * KB)
        OUT5 = at("out_s5_lru", [P, KT, T], B0 + 44 * KB)
        Y5 = OUT5[:, 0:S5_TILES]
        GT = at("gate_tanh", [P, 2, 4, T], B0 + 16 * KB)
        PM = at("proj_m", [P, 2, 4, T], B0 + 24 * KB)
        MG = at("merged", [P, KT, T], B0 + 44 * KB)
        CB = at("combine_b", [P, EXPERTS, T], B0 + 16 * KB)
        WR = at("w_router", [P, KT, 36], B0 + 16 * KB)
        WRH = at("w_router_hi", [P, KT, 36], B0 + 19 * KB, F32R)
        WRL = at("w_router_lo", [P, KT, 36], B0 + 22 * KB, F32R)
        RLT = at("router_rows", [36, T], B0 + 62 * KB)
        RS = at("router_small", [P, 16, TT, EXPERTS], B0 + 25 * KB)
        COMBT = at("combine_T", [EXPERTS, T], B0 + 60 * KB)
        MTH = at("moe_tanh", [P, 2, T], B0 + 48 * KB)
        MS1 = at("moe_s1", [P, 2, T], B0 + 50 * KB)
        MS2 = at("moe_s2", [P, 2, T], B0 + 52 * KB)
        MACT = at("moe_act", [P, 2, T], B0 + 54 * KB)
        OUTB = at("out_sb", [P, KT, T], A0)
        small_at = B0 + 66048

        def small(name, shape, dt=F32):
            nonlocal small_at
            t = at(name, shape, small_at, dt)
            small_at += (4 * int(np.prod(shape[1:])) + 31) // 32 * 32
            assert small_at + base <= nc.sbuf_usable_end
            return t

        CST = small("consts", [P, N_CONST])
        COL = small("cols", [P, N_COLS])
        MODC = small("mod_cols", [P, 96, 2])
        MACC = small("mod_sums", [P, 2, NB])
        RB = at("rstd_b", [P, 2, T], small_at - 4 * KB)
        ROPE = at("rope_tables", [P, 2, T], small_at - 2 * KB)
        CS = small("c_column", [P, KT])
        ONES = small("ones", [P, P])
        SCALES = small("norm_scales", [P, 6, KT])
        LAM = small("lam_small", [P, 8])
        BG = small("b_gates", [HEADS, 4])
        NEGM = small("neg_max", [HEADS, 2, T])
        ACOL = small("a_cols", [P, 2, 4, HEADS])
        EMT = small("exp_neg_max", [P, 2, TT, HEADS])
        HALF = small("half_biases", [P, 72])
        RBIAS = small("router_bias", [P, 36])
        STAT = small("row_stats", [P, 32])
        PS = ctx.enter_context(nc.psum_tensor("acc", [P, 8 * NB], F32))
        block = ctx.enter_context(nc.Block())

        def col(name, i=0, n=1):
            return COL[:, COL_AT[name][0] + i:COL_AT[name][0] + i + n]

        ring_in = [sem(f"ring_in{r}") for r in range(RING)]
        hi_done = sem("hi_done")
        lo_done = sem("lo_done")
        slot_used = sem("slot_used")
        stage_sem = {s: sem("blk_" + s) for s in ("free", "a1", "d1", "a2", "d2", "a3", "d3")}
        dve_st = Steps(None, sem("dve_step"))

        def mult(i, n):
            return i * n if not isinstance(i, int) or i else 0

        def wait_slot(eng, s, g, i, c, more):
            eng.wait_ge(s, mult(i, 2 * g.slots) + (g.m0 + c + 1 + more))

        def wait_place(eng, g, i, c, more, e=0):
            eng.wait_ge(lo_done, mult(i, 2 * g.slots) + (g.s0 + c * (1 + g.extra) + e + 1 + more))

        def wait_block(eng, g, i, b):
            eng.wait_ge(slot_used, mult(i, 2 * g.slots) + (g.m0 + (b + 1) * g.slots + 2))

        def wait_stage(eng, st, g, i, b):
            eng.wait_ge(stage_sem[st], mult(i, 2) + (g.base.get(st, 0) + b + 1 + (2 if st == "free" else 0)))

        def all_free(eng, g):
            wait_stage(eng, "free", g, 0, g.blocks - 1)

        def to_hi(act, g, i, c):
            at_ = g.s0 + c * (1 + g.extra)
            r, par = at_ % RING, (g.m0 + c) % 2
            act.wait_ge(ring_in[r], mult(i, 16 * g.dmas * (2 * g.slots // RING)) + RING_AT[at_])
            wait_slot(act, slot_used, g, i, c, 0)
            act.activation(WHI[:, par], RAW[:, r], ACT.Copy).then_inc(hi_done, 1)

        def to_lo(dve, g, i, c):
            r, par = (g.s0 + c * (1 + g.extra)) % RING, (g.m0 + c) % 2
            if g.extra and c:
                mod_sum(dve, g, c - 1)
            elif g.name == "mq" and c == 0:
                mod_sum(dve, G["dv"], G["dv"].blocks * G["dv"].slots - 1)
            elif g.extra and g.name != "mk":
                mod_sum(dve, GEMMS[GEMMS.index(g) - 1], GEMMS[GEMMS.index(g) - 1].blocks * g.slots - 1)
            wait_slot(dve, hi_done, g, i, c, 0)
            dve.tensor_tensor(WLO[:, par], RAW[:, r], WHI[:, par].bitcast(F32), ALU.subtract)\
               .then_inc(lo_done, 1)
            if g.extra and c % g.slots == g.slots - 1:
                mod_sums_out(dve, (g.m0 - G["mk"].m0 + c) // g.slots)

        def mod_place(g, c, e):
            n = (g.m0 - G["mk"].m0 + c) * g.extra + e
            return n // 4, n % 4

        def mod_sums_out(dve, w):
            c0, c1 = 4 * max(2 * w - 1, 0), 4 * min(2 * w + 1, MOD_REST)
            dve.wait_ge(sem("mod_sums_read"), w + 1)
            at_ = mod_sums_at(w) + c0 - 4 * (2 * w - 1)
            dve.tensor_tensor(MODC[:, 4 * MOD_FIRST + c0:4 * MOD_FIRST + c1, 0], PS[:, at_:at_ + c1 - c0],
                              col("b_mod", 4 * MOD_FIRST + c0, c1 - c0), ALU.add).then_inc(sem("mod_rest"), 1)

        def mod_sums_at(w):
            return (G["mk"].b0 + min(w + 1, MOD_REST // 2)) % 2 * 4 * NB

        def mod_sum(dve, g, c):
            for e in range(g.extra):
                mb, q = mod_place(g, c, e)
                at_ = g.s0 + c * (1 + g.extra) + 1 + e
                acc = MACC[:, mb % 2]
                dve.wait_ge(ring_in[at_ % RING], RING_AT[at_])
                if q == 0 and mb >= 2:
                    dve.wait_ge(sem("mod_sums_read"), (mb + 1) // 2)
                for k in range(SLOT_K):
                    w, s = RAW[:, at_ % RING, k], CS[:, SLOT_K * q + k:SLOT_K * q + k + 1]
                    if q == 0 and k == 0:
                        ins = dve.tensor_scalar(acc, w, s, None, ALU.mult)
                    else:
                        ins = dve.scalar_tensor_tensor(acc, w, s, acc, ALU.mult, ALU.add)
                    if k < SLOT_K - 1:
                        dve_st(ins)
                ins.then_inc(lo_done, 1)
                dve.wait_ge(lo_done, at_ + 1 + RING)

        def ahead(g):
            return 1 if g.name == "mk" else 2

        def feed(eng, conv, g, stages, steps=None, per=0, beside=None):
            n, s = g.blocks, g.slots

            def work(i, b, prev):
                todo = list(stages)
                for q in range(s):
                    if b > 0 or q >= ahead(g):
                        conv(eng, g, i, b * s + q)
                    if beside and (n <= 4 or b == n - 1):
                        beside(b * s + q)
                    if q >= 1 and prev is not None and todo:
                        todo.pop(0)(g, i, prev)
                while prev is not None and todo:
                    todo.pop(0)(g, i, prev)

            work(0, 0, None)
            if n <= 4:
                for b in range(1, n):
                    work(0, b, b - 1)
            else:
                n0 = steps.n if steps else 0
                with eng.Fori(0, (n - 2) // 2) as i:
                    if steps:
                        steps.dyn = i * (2 * per)
                    work(i, 1, 0)
                    work(i, 2, 1)
                if steps:
                    assert steps.n == n0 + 2 * per, (g.name, steps.n - n0)
                    steps.dyn, steps.n = 0, n0 + per * (n - 2)
                work(0, n - 1, n - 2)
            if g.next:
                for c in range(min(ahead(g.next), g.next.blocks * g.next.slots)):
                    conv(eng, g.next, 0, c)
            for f in stages:
                f(g, 0, n - 1)

        def narrow(b):
            par = b % 2
            return PS[:, par * 1024:par * 1024 + 1024].rearrange("p (j t) -> p j t", j=4)

        def wide(b):
            par = b % 2
            return PS[:, par * 2048:par * 2048 + 2048].rearrange("p (j t) -> p j t", j=4)

        def bank(n, m=NB):
            return PS[:, n * NB:n * NB + m]

        sq_done, ss_done, rec_done, rb_done = sem("sq_done"), sem("ss_done"), sem("rec_done"), sem("rb_done")
        tmp_ready, hhi_ready, hlo_ready = sem("tmp_ready"), sem("hhi_ready"), sem("hlo_ready")
        x_new = sem("x_new")

        @block.sync
        def _(sp):
            def src(g):
                name = g.name
                if name == "mod":
                    return lambda b, q: [(0, NB, A["w_mod"], q, b * NB)]
                w_in = {"mk": 1024, "mv": 2048, "dk": 4096 + 32 + 1024, "dv": 4096 + 32 + 2048,
                        "mq": 0, "dq": 4096 + 32, "mo": 3072}
                if name in w_in:
                    return lambda b, q: [(0, NB, A["w_in"], q, w_in[name] + b * NB)]
                if name == "wout":
                    return lambda b, q: [(0, NB, A["w_out"], q, b * NB)]
                if name[:2] == "up":
                    f0 = FFN_PARTS[int(name[2])][0]
                    return lambda b, q: [(0, 256, A["w_up"], q, (b + f0) * 256),
                                         (256, 256, A["w_up"], q, (b + f0) * 256 + D_FF)]
                if name[:4] == "down":
                    f0 = FFN_PARTS[int(name[4])][0]
                    return lambda b, q: [(0, NB, A["w_down"], q + f0 // 2, b * NB)]
                off = {"in_u": 0, "in_x": NB, "in_y": 4 * NB}
                if name in off:
                    return lambda b, q: [(0, NB, A["w_in_2"], q, off[name] + b * NB)]
                if name == "glu":
                    return lambda b, q: [(0, NB, A["s5_w_glu_2"], 0, 0)]
                if name[:5] == "gates":
                    k = int(name[5])
                    return lambda b, q: [(0, NB, A["w_in_2"], q, (7 + 4 * b + k) * NB)]
                if name[:4] == "proj":
                    k = int(name[4])
                    return lambda b, q: [(0, NB, A["w_proj_s5_2"], 0, k * NB) if q == 0 else
                                         (0, NB, A["w_proj_lru_2"], q - 1, k * NB)]
                if name == "out2":
                    return lambda b, q: [(0, NB, A["w_out_2"], q, b * NB)]
                if name[:6] == "moe_up":
                    e0 = 8 * int(name[6])
                    return lambda b, q: [(0, 256, A["w_e_gate_2"], (b + e0) * 4 + q, 0),
                                         (256, 256, A["w_e_up_2"], (b + e0) * 4 + q, 0)]
                e0 = 8 * int(name[8])
                return lambda b, q: [(0, NB, A["w_e_down_2"], q + e0 // 2, b * NB)]

            def load(g, i, b, q, f):
                c = b * g.slots + q
                r = (g.s0 + c * (1 + g.extra)) % RING
                wait_place(sp, g, i, c, 0)
                for at0, n, w, row, c0 in f(mult(i, 2) + b, q):
                    v = w.rearrange("(q k p) n -> p q k n", p=P, k=SLOT_K)
                    if not isinstance(row, int):
                        sp.dma_start(RAW[:, r, :, at0:at0 + n], v[:, bass.ds(row, 1), :, c0:c0 + n]
                                     .rearrange("p q k n -> p (q k) n")).then_inc(ring_in[r], 16)
                    else:
                        sp.dma_start(RAW[:, r, :, at0:at0 + n],
                                     v[:, row, :, bass.ds(c0, n)]).then_inc(ring_in[r], 16)

            for g in GEMMS:
                f = src(g)
                if g.blocks >= 4 and 2 * g.slots % RING == 0:
                    with sp.Fori(0, g.blocks // 2) as i:
                        for b in range(2):
                            for q in range(g.slots):
                                load(g, i, b, q, f)
                else:
                    for b in range(g.blocks):
                        for q in range(g.slots):
                            load(g, 0, b, q, f)
                            for e in range(g.extra):
                                mb, mq = mod_place(g, b * g.slots + q, e)
                                place = g.s0 + (b * g.slots + q) * (1 + g.extra) + 1 + e
                                wait_place(sp, g, 0, b * g.slots + q, 0, 1 + e)
                                sp.dma_start(RAW[:, place % RING],
                                             A["w_mod"].rearrange("(q k p) n -> p q k n", p=P, k=SLOT_K)
                                             [:, mq, :, (MOD_FIRST + mb) * NB:(MOD_FIRST + mb + 1) * NB])\
                                  .then_inc(ring_in[place % RING], 16)
            sp.wait_ge(sem("out_ready"), 4)
            sp.dma_start(A["out"].rearrange("p (k t) -> p k t", k=KT), OUTB[:]).then_inc(sem("stored"), 16)
            sp.wait_ge(sem("stored"), 16)

        @block.gpsimd
        def _(pool):
            pool.dma_start(COL[:], A["cols"]).then_inc(sem("cols_in"), 16)
            pool.dma_start(XIN[:, 0], A["xT"].rearrange("p (k t) -> p k t", k=KT)).then_inc(sem("x_in"), 16)
            pool.dma_start(XIN[:, 1], A["ctxT"].rearrange("p (k t) -> p k t", k=KT)).then_inc(sem("x_in"), 16)
            pool.dma_start(CST[:], A["consts"][:, 0:N_CONST]).then_inc(sem("const_in"), 16)
            pool.dma_start(LAMV[:], A["lamv"].rearrange("p (k n) -> p k n", k=4)).then_inc(sem("lam_in"), 16)
            pool.dma_start(BG[:], A["b_gateT"]).then_inc(sem("bg_in"), 16)
            pool.dma_start(RBIAS[:], A["b_router"]).then_inc(sem("rbias_in"), 16)
            pool.dma_start(WG[:], A["w_gates"].rearrange("p (k n) -> p k n", k=KT)).then_inc(sem("wg_in"), 16)
            pool.wait_ge(sem("x_in"), 32)
            for ch in range(4):
                x = XIN[:, :, 4 * ch:4 * ch + 4, :]
                pool.tensor_tensor(SQW[:, ch].rearrange("p k s t -> p s k t"), x, x, ALU.mult)\
                    .then_inc(sq_done, 1)
            pool.wait_ge(sem("mod_sums_read"), MOD_REST // 2 + 1)
            pool.dma_start(ROPE[:], A["consts"][:, C_COS:C_SIN + T].rearrange("p (v t) -> p v t", v=2))\
                .then_inc(sem("rope_in"), 16)
            pool.wait_ge(sem("mixd_done"), 1)
            pool.dma_start(X[:], A["xT"].rearrange("p (k t) -> p k t", k=KT)).then_inc(sem("x2_in"), 16)
            pool.wait_ge(hlo_ready, APPLY["mix2"] + 4)
            pool.dma_start(S5B[:], A["s5_b"].rearrange("p (v k n) -> p v k n", v=2, k=4)).then_inc(sem("s5w_in"), 16)
            pool.dma_start(S5C[:], A["s5_c"].rearrange("p (v k n) -> p v k n", v=2, k=ST_TILES))\
                .then_inc(sem("s5w_in"), 16)
            lw = A["lru_w"].rearrange("p (v k n) -> p v k n", v=2, k=LRU_TILES)
            all_free(pool, G["glu"])
            pool.dma_start(LW[:], lw[:, :, 0:LH, :]).then_inc(sem("lw_in"), 16)
            pool.wait_ge(sem("lru_mm"), LRU_TILES // 2)
            pool.dma_start(LW[:], lw[:, :, LH:LRU_TILES, :]).then_inc(sem("lw_in"), 16)
            wait_stage(pool, "free", G["out2"], 0, 3)
            pool.dma_start(WR[:], A["w_router"].rearrange("p (k n) -> p k n", k=KT)).then_inc(sem("wr_in"), 16)

        @block.scalar
        def _(act):
            def stats(n, src, ready):
                for ch in range(4):
                    act.wait_ge(ss_done, 4 * n + ch - 1)
                    ready(ch)
                    act.activation(SQ[:, ch % 2], src[:, 4 * ch:4 * ch + 4, :], ACT.Square).then_inc(sq_done, 1)
                act.wait_ge(rec_done, n + 1)
                act.activation(RB[:, 0], RB[:, 0], ACT.Sqrt).then_inc(rb_done, 1)

            def apply_hi(base_, chunks, buf, out, shift=None):
                for ch in range(chunks):
                    act.wait_ge(tmp_ready, base_ + ch + 1)
                    if shift is None:
                        act.activation(out(ch, None), buf[:, ch % 2], ACT.Copy).then_inc(hhi_ready, 1)
                    else:
                        for k in range(4):
                            last = act.activation(out(ch, k), buf[:, ch % 2, k], ACT.Identity, bias=shift(ch, k))
                        last.then_inc(hhi_ready, 1)

            def nothing(*_):
                pass

            act.wait_ge(sem("cols_in"), 16)
            act.activation(C4F[:, 0:2], col("c", 0, 32).rearrange("p (v k) -> p v k", v=2), ACT.Tanh, scale=0.5)\
               .then_inc(sem("c_tanh"), 1)
            act.wait_ge(sem("c_silu"), 1)
            act.activation(C4[:].rearrange("p k (v h) -> p v k h", v=2)[:, :, :, 0], C4F[:, 2:4], ACT.Copy)\
               .then_inc(sem("c_ready"), 1)
            act.wait_ge(sem("lam_sum"), 1)
            act.activation(LAM[:, 2:4], LAM[:, 0:2], ACT.Exp).then_inc(sem("lam_exp"), 1)
            to_hi(act, G["mod"], 0, 0)
            to_hi(act, G["mod"], 0, 1)

            def first_norm(c):
                if c == 4 * (MOD_FIRST - 1):
                    act.wait_ge(rec_done, 1)
                    act.activation(RBW[:], RBW[:], ACT.Sqrt).then_inc(rb_done, 1)
                    act.wait_ge(sem("wg_in"), 16)
                    act.activation(WGH[:], WG[:], ACT.Copy).then_inc(sem("wg_hi"), 1)
            feed(act, to_hi, G["mod"], [], beside=first_norm)
            act.wait_ge(sem("scales"), 2)
            for ch in range(8):
                for k in range(4 * (ch % 4), 4 * (ch % 4) + 4):
                    last = act.activation(H1HI[:, ch // 4, k, :], XIN[:, ch // 4, k, :], ACT.Identity,
                                          scale=SCALES[:, ch // 4, k:k + 1], bias=MODC[:, k, ch // 4:ch // 4 + 1])
                last.then_inc(hhi_ready, 1)
            act.wait_ge(sem("gate_mm"), 1)
            act.activation(GALL[:], PS[0:4 * HEADS, 6 * NB:7 * NB], ACT.Copy).then_inc(sem("gates_copied"), 1)

            def gate_steps(c):
                if c == 2:
                    act.wait_ge(sem("gate_abs"), 1)
                    gabs = GS[:, 0]
                    act.activation(gabs, gabs, ACT.Exp, scale=-1.0).then_inc(sem("gate_e"), 1)
                    act.wait_ge(sem("gate_e"), 1)
                    act.activation(gabs, gabs, ACT.Ln, bias=1.0).then_inc(sem("gate_ln"), 1)
                if c == 5:
                    act.wait_ge(sem("gate_em"), 1)
                    em = GROW[:, 2]
                    act.activation(em, em, ACT.Exp, scale=-1.0).then_inc(sem("gate_emt"), 1)

            def conv_in(dst, wide_, col0):
                def s1(g, i, b):
                    wait_block(act, g, i, b)
                    ps = wide(g.b0 + b)
                    for j in range(4):
                        t = 4 * b + j
                        out = dst[:, t].rearrange("p s t -> p (s t)") if wide_ else dst[:, t]
                        last = act.activation(out, ps[:, j, 0:512 if wide_ else 256], ACT.Identity,
                                              bias=col("conv_qk_b", col0 + t), scale=col("conv_qk_w", 16 + col0 + t))
                    last.then_inc(stage_sem["a1"], 1)

                def s2(g, i, b):
                    wait_stage(act, "free", g, i, b)
                    th = KTH[:] if wide_ else QTH[:]
                    if b:
                        wait_stage(act, "d2", g, i, b - 1)
                    act.activation(th, dst[:, 4 * b:4 * b + 4], ACT.Tanh, scale=0.5).then_inc(stage_sem["a2"], 1)
                return [s1, s2]

            def copy_out(dst, wide_, func=ACT.Copy, scale=1.0):
                def s1(g, i, b):
                    wait_block(act, g, i, b)
                    ps = wide(g.b0 + b)
                    act.activation(dst(b), ps if wide_ else ps[:, :, 0:256], func, scale=scale)\
                       .then_inc(stage_sem["free"], 1)
                return [s1]

            feed(act, to_hi, G["mk"], conv_in(MK, True, 8), beside=gate_steps)
            feed(act, to_hi, G["mv"], copy_out(lambda b: MV[:, :, 4 * b:4 * b + 4, 0:128], True))
            feed(act, to_hi, G["dk"], copy_out(lambda b: DK[:, 4 * b:4 * b + 4], True))
            feed(act, to_hi, G["dv"], copy_out(lambda b: DV[:, :, 4 * b:4 * b + 4, :], True))
            feed(act, to_hi, G["mq"], conv_in(MQ, False, 0))
            feed(act, to_hi, G["dq"], copy_out(lambda b: DQ[:, 4 * b:4 * b + 4], False))
            feed(act, to_hi, G["mo"], copy_out(lambda b: MO[:, 4 * b:4 * b + 4], False, ACT.Tanh, 0.5))

            def num_copy(h):
                for d in range(2):
                    act.wait_ge(sem("m_pv"), 2 * h + d + 1)
                    ps = bank(6 + d, 258).rearrange("p (u n) -> p u n", u=2)
                    act.activation(NUM[:, d, :, h % 4, :], ps[:, :, 0:128], ACT.Copy)
                    act.activation(STAT[:, 0:16].rearrange("p (d u h) -> p d u h", d=2, u=2)[:, d, :, h % 4],
                                   ps[:, :, 128], ACT.Copy).then_inc(sem("m_num"), 1)

            for h in range(HEADS):
                for d in range(2):
                    act.wait_ge(sem("m_bc"), 2 * h + d + 1)
                    act.wait_ge(sem("m_zero"), h // 4 + 1)
                    if h:
                        act.wait_ge(sem("m_p"), 2 * (h - 1) + d + 1)
                    bc = bank(4 + d)
                    for j in (2, 3):
                        act.activation(MW[:, d, j], bc[:, 0:256], ACT.Exp, bias=ACOL[:, d, j, h:h + 1])
                    for j in range(2):
                        act.activation(MW[:, d, j, 128 * j:128 * j + 128], bc[:, 256 + 128 * j:384 + 128 * j],
                                       ACT.Exp, bias=ACOL[:, d, j, h:h + 1])
                    act.activation(MW[:, d, d, 128 * (1 - d):128 * (1 - d) + 128],
                                   bc[:, 128 * (1 - d):128 * (1 - d) + 128],
                                   ACT.Exp, bias=ACOL[:, d, d, h:h + 1]).then_inc(sem("m_w"), 1)
                if h % 4:
                    num_copy(h - 1)
                if h % 4 == 3:
                    num_copy(h)
                    act.wait_ge(sem("m_var"), h // 4 + 1)
                    act.activation(STAT[:, 0:8], STAT[:, 0:8], ACT.Sqrt).then_inc(sem("m_rstd"), 1)

            def d_exp(u):
                par = u % 2
                act.wait_ge(sem("d_nm"), u + 1)
                if u >= 2:
                    act.wait_ge(sem("d_p"), u - 1)
                for c in range(2):
                    last = act.activation(DE[:, par, c], bank(2 * par + c), ACT.Exp, scale=0.125,
                                          bias=STAT[:, 8 * par + 2 + c:8 * par + 3 + c],
                                          accum_out=STAT[:, 8 * par + 4 + c:8 * par + 5 + c])
                last.then_inc(sem("d_e"), 1)

            def d_copy_t(u):
                act.wait_ge(sem("d_t"), u + 1)
                if u >= 2:
                    act.wait_ge(sem("d_o"), u - 1)
                act.activation(DPT[:, u % 2].rearrange("p j t -> p (j t)"), bank(4 + u % 2), ACT.Copy)\
                   .then_inc(sem("d_tc"), 1)

            def d_copy_o(u):
                act.wait_ge(sem("d_o"), u + 1)
                act.activation(DO[:, u % 2, u // 2, :], bank(6 + u % 2, 128), ACT.Copy).then_inc(sem("d_oc"), 1)

            U = 2 * HEADS
            for u in range(U + 3):
                if 2 <= u < U + 2:
                    d_copy_t(u - 2)
                if u < U:
                    d_exp(u)
                if u >= 3:
                    d_copy_o(u - 3)
            act.wait_ge(sem("d_var"), 1)
            act.activation(STAT[:, 0:16], STAT[:, 0:16], ACT.Sqrt).then_inc(sem("d_rstd"), 1)
            act.wait_ge(sem("mixd_done"), 1)
            for ch in range(4):
                act.activation(HHI[:, 4 * ch:4 * ch + 4], MIX[:, 4 * ch:4 * ch + 4], ACT.Copy).then_inc(hhi_ready, 1)
            copy_y = [lambda g, i, b: (wait_block(act, g, i, b),
                                       act.activation(Y[:, 4 * b:4 * b + 4], narrow(g.b0 + b), ACT.Copy)
                                       .then_inc(stage_sem["free"], 1))]
            feed(act, to_hi, G["wout"], copy_y)
            stats(1, Y, lambda ch: wait_stage(act, "free", G["wout"], 0, ch))
            stats(2, X, lambda ch: act.wait_ge(x_new, ch + 1))
            apply_hi(TMPS["ffn"], 4, TMP, lambda ch, k: HHI[:, 4 * ch + k, :],
                     lambda ch, k: MODC[:, 48 + 4 * ch + k, 0:1])

            def up_stages(part):
                f0 = FFN_PARTS[part][0]

                def s1(g, i, b):
                    wait_block(act, g, i, b)
                    ps, par = narrow(g.b0 + b), b % 2
                    for j in range(4):
                        t = (j // 2) * FT + j % 2 + 2 * (f0 + b)
                        w = COL_AT["conv_ffn_w"][0] + 2 * FT + t + mult(i, 4)
                        bb = COL_AT["conv_ffn_b"][0] + t + mult(i, 4)
                        last = act.activation(UC[:, par, j], ps[:, j], ACT.Identity,
                                              bias=COL[:, bass.ds(bb, 1)], scale=COL[:, bass.ds(w, 1)])
                    last.then_inc(stage_sem["a1"], 1)

                def s2(g, i, b):
                    wait_stage(act, "free", g, i, b)
                    act.activation(UTH[:, b % 2], UC[:, b % 2, 0:2], ACT.Tanh, scale=0.5)\
                       .then_inc(stage_sem["a2"], 1)

                def s3(g, i, b):
                    wait_stage(act, "d2", g, i, b)
                    act.activation(AHI[:, bass.ds(mult(i, 4) + 2 * b, 2)], UACT[:, b % 2], ACT.Copy)\
                       .then_inc(stage_sem["a3"], 1)
                return [s1, s2, s3]

            for part in range(3):
                if part:
                    wait_block(act, G[f"down{part - 1}"], 0, 3)
                feed(act, to_hi, G[f"up{part}"], up_stages(part))
                feed(act, to_hi, G[f"down{part}"], copy_y if part == 0 else [])
            stats(3, Y, lambda ch: wait_stage(act, "free", G["down2"], 0, ch))
            stats(4, X, lambda ch: act.wait_ge(x_new, 4 + ch + 1))
            apply_hi(TMPS["mix2"], 4, TMP, lambda ch, k: HHI[:, 4 * ch:4 * ch + 4, :])

            def u_out(g, i, b):
                wait_block(act, g, i, b)
                act.activation(U5[:], narrow(g.b0 + b), ACT.Copy).then_inc(stage_sem["free"], 1)

            def x_out(g, i, b):
                wait_block(act, g, i, b)
                ps = narrow(g.b0 + b)
                for j in range(4):
                    t = 4 * b + j
                    last = act.activation(XC[:, t], ps[:, j], ACT.Identity, bias=col("lru_conv_b", t),
                                          scale=col("lru_conv_w", 36 + t))
                last.then_inc(stage_sem["a1"], 1)

            def y_out1(g, i, b):
                wait_block(act, g, i, b)
                if b:
                    wait_stage(act, "d1", g, i, b - 1)
                act.activation(YSQ[:], narrow(g.b0 + b), ACT.Square).then_inc(stage_sem["a1"], 1)

            def y_out2(g, i, b):
                wait_stage(act, "d1", g, i, b)
                act.activation(YTH[:], YTH[:], ACT.Tanh, scale=GELU_C).then_inc(stage_sem["a2"], 1)

            feed(act, to_hi, G["in_u"], [u_out])
            feed(act, to_hi, G["in_x"], [x_out])
            feed(act, to_hi, G["in_y"], [y_out1, y_out2])

            def s5(n, m=1):
                return S5S[:, n:n + m]
            act.wait_ge(sem("cols_in"), 16)
            act.activation(s5(0), col("log_step", 0, 16).unsqueeze(1), ACT.Exp).then_inc(sem("s5_step"), 1)
            act.wait_ge(sem("s5_pre"), 1)
            act.activation(s5(1), s5(1), ACT.Exp).then_inc(sem("s5_abs"), 1)
            act.activation(s5(4), s5(3), ACT.Sin)
            act.activation(s5(5), s5(3), ACT.Sin, scale=0.5).then_inc(sem("s5_sin"), 1)
            act.wait_ge(sem("s5_ang"), 1)
            act.activation(ESC[:], EX[:], ACT.Sin, scale=TWO_PI).then_inc(sem("s5_esc"), 1)
            act.wait_ge(sem("s5_y"), 1)
            act.activation(Y5B[:], Y5[:], ACT.Square).then_inc(sem("s5_ysq"), 1)
            act.wait_ge(sem("s5_yt"), 1)
            act.activation(Y5B[:], Y5B[:], ACT.Tanh, scale=GELU_C).then_inc(sem("s5_yth"), 1)
            act.wait_ge(sem("s5_g"), 1)
            act.activation(GHI[:], Y5[:], ACT.Copy).then_inc(sem("s5_ghi"), 1)

            def glu_out(g, i, b):
                wait_block(act, g, i, b)
                act.wait_ge(sem("half_b"), 1)
                for j in range(4):
                    last = act.activation(Y5B[:, j], narrow(g.b0 + b)[:, j], ACT.Tanh, scale=0.5,
                                          bias=HALF[:, 32 + j:33 + j])
                last.then_inc(stage_sem["free"], 1)
            feed(act, to_hi, G["glu"], [glu_out])
            act.activation(HALF[:, 60:72], HALF[:, 60:72], ACT.Exp, scale=-1.0).then_inc(sem("sp_e"), 1)
            act.wait_ge(sem("sp_u"), 1)
            act.activation(S5S[:, 7, 0:12], S5S[:, 6, 0:12], ACT.Ln).then_inc(sem("sp_ln"), 1)
            for half in range(2):
                for h in range(LH):
                    t = half * LH + h
                    act.wait_ge(sem("lru_mm"), t + 1)
                    if half and h == 0:
                        act.wait_ge(sem("lru_out"), 1)
                    ps = bank(t % 2 + 4)
                    act.activation(LR[:, h], ps[:, 0:256], ACT.Tanh, scale=0.5, bias=HALF[:, 36 + t:37 + t])
                    act.activation(LI[:, h], ps[:, 256:512], ACT.Tanh, scale=0.5, bias=HALF[:, 48 + t:49 + t])\
                       .then_inc(sem("lru_ri"), 1)
                act.wait_ge(sem("lru_y"), half + 1)
                act.activation(LA[:], LR[:], ACT.Tanh).then_inc(sem("lru_th"), 1)
                act.activation(LR[:], LR[:], ACT.Exp, scale=-1.0).then_inc(sem("lru_a"), 1)
                act.wait_ge(sem("lru_m"), half + 1)
                act.activation(LA[:], LA[:], ACT.Sqrt, scale=2.0).then_inc(sem("lru_sq"), 1)
            act.wait_ge(sem("lru_out"), 2)
            for ch in range(4):
                act.activation(AHI[:, 4 * ch:4 * ch + 4], OUT5[:, 4 * ch:4 * ch + 4], ACT.Copy)\
                   .then_inc(hhi_ready, 1)

            def gate_out(k):
                def s1(g, i, b):
                    wait_block(act, g, i, b)
                    if k:
                        wait_stage(act, "free", G[f"proj{k - 1}"], 0, 0)
                    for j in range(4):
                        last = act.activation(GT[:, b, j], narrow(g.b0 + b)[:, j], ACT.Tanh, scale=0.5,
                                              bias=HALF[:, 16 * b + 4 * k + j:16 * b + 4 * k + j + 1])
                    last.then_inc(stage_sem["free"], 1)
                return [s1]

            for k in range(4):
                feed(act, to_hi, G[f"gates{k}"], gate_out(k))
                feed(act, to_hi, G[f"proj{k}"], [])
            for ch in range(4):
                wait_stage(act, "d2", G["proj3"], 0, 0)
                wait_block(act, G["gates3"], 0, 1)
                act.activation(HHI[:, 4 * ch:4 * ch + 4], MG[:, 4 * ch:4 * ch + 4], ACT.Copy).then_inc(hhi_ready, 1)
            feed(act, to_hi, G["out2"], [])
            stats(5, X, lambda ch: wait_stage(act, "free", G["out2"], 0, ch))
            apply_hi(TMPS["moe"], 4, TMP, lambda ch, k: HHI[:, 4 * ch:4 * ch + 4, :])
            act.wait_ge(sem("wr_in"), 16)
            act.activation(WRH[:], WR[:], ACT.Copy).then_inc(sem("wr_hi"), 1)
            act.wait_ge(sem("r_mm"), 1)
            act.activation(RLT[:], PS[0:36, 6 * NB:6 * NB + T], ACT.Copy).then_inc(sem("r_rows"), 1)
            act.wait_ge(sem("r_shift"), 1)
            act.activation(RS[:, 2, :, 0:4], RS[:, 2, :, 0:4], ACT.Exp).then_inc(sem("r_exp"), 1)
            act.wait_ge(sem("r_gap"), 1)
            act.activation(RS[:, 9, :, 0:1], RS[:, 9, :, 0:1], ACT.Exp).then_inc(sem("r_gape"), 1)
            act.wait_ge(sem("r_combT"), 1)
            act.activation(COMBT[:], PS[0:EXPERTS, 0:T], ACT.Copy).then_inc(sem("combT"), 1)
            for q in range(8):
                act.wait_ge(sem("cb_mm"), q + 1)
                act.activation(CB[:, 4 * q:4 * q + 4], narrow(q), ACT.Copy).then_inc(sem("cb"), 1)

            def moe_tanh(g, i, b):
                wait_block(act, g, i, b)
                act.activation(MTH[:], narrow(g.b0 + b)[:, 0:2], ACT.Tanh, scale=0.5).then_inc(stage_sem["a2"], 1)

            def moe_hi(g, i, b):
                wait_stage(act, "d2", g, i, b)
                act.activation(AHI[:, bass.ds(mult(i, 4) + 2 * b, 2)], MACT[:], ACT.Copy)\
                   .then_inc(stage_sem["a3"], 1)

            for part in range(4):
                if part:
                    wait_block(act, G[f"moe_down{part - 1}"], 0, 3)
                feed(act, to_hi, G[f"moe_up{part}"], [moe_tanh, nothing, moe_hi])
                feed(act, to_hi, G[f"moe_down{part}"], [])
            stats(6, X, lambda ch: wait_stage(act, "free", G["moe_down3"], 0, ch))

        @block.vector
        def _(dve):
            st, dve_st.eng = dve_st, dve
            dve.sem_inc(lo_done, RING)

            def nothing(*_):
                pass

            def var(n, wide_):
                dve.wait_ge(ss_done, 4 * n + 4)
                m = 2 * T if wide_ else T
                rb = (RBW if wide_ else RB)[:].rearrange("p s t -> p (s t)")[:, 0:m]
                st(dve.tensor_scalar(rb, bank(7, m), 1.0 / D, EPS, ALU.mult, ALU.add))
                dve.reciprocal(rb, rb).then_inc(rec_done, 1)
                dve.wait_ge(rb_done, n + 1)

            def apply(b_hi, b_tmp, chunks, buf, src, scale, rb, out, shift=None):
                def first(ch):
                    if b_hi + ch - 1 > 0:
                        dve.wait_ge(hlo_ready, b_hi + max(ch - 1, 0))
                    for k in range(4):
                        last = dve.scalar_tensor_tensor(buf[:, ch % 2, k], src(ch, k), scale(ch, k), rb(ch),
                                                        ALU.mult, ALU.mult)
                    last.then_inc(tmp_ready, 1)

                def second(ch):
                    dve.wait_ge(hhi_ready, b_hi + ch + 1)
                    if shift is None:
                        o_hi, o_lo = out(ch, None)
                        last = dve.tensor_tensor(o_lo, buf[:, ch % 2], o_hi.bitcast(F32), ALU.subtract)
                    else:
                        for k in range(4):
                            o_hi, o_lo = out(ch, k)
                            last = dve.scalar_tensor_tensor(o_lo, buf[:, ch % 2, k], shift(ch, k), o_hi.bitcast(F32),
                                                            ALU.add, ALU.subtract)
                    last.then_inc(hlo_ready, 1)

                for ch in range(chunks + 1):
                    if ch < chunks:
                        first(ch)
                        if ch == 0:
                            dve.wait_ge(tmp_ready, b_tmp + 1)
                    if ch:
                        dve.wait_ge(tmp_ready, b_tmp + ch)
                        second(ch - 1)

            def split(b_hi, hi, lo, src):
                for ch in range(4):
                    sl = slice(4 * ch, 4 * ch + 4)
                    dve.wait_ge(hhi_ready, b_hi + ch + 1)
                    dve.tensor_tensor(lo[:, sl], src[:, sl], hi[:, sl].bitcast(F32), ALU.subtract)\
                       .then_inc(hlo_ready, 1)

            def residual(n, scale):
                var(n, False)
                for k in range(KT):
                    last = dve.scalar_tensor_tensor(Y[:, k], Y[:, k], scale(k), RB[:, 0], ALU.mult, ALU.mult)
                st(last)
                for ch in range(4):
                    sl = slice(4 * ch, 4 * ch + 4)
                    dve.tensor_tensor(X[:, sl], X[:, sl], Y[:, sl], ALU.add).then_inc(x_new, 1)

            dve.memset(ONES[:], 1.0).then_inc(sem("ones"), 1)
            dve.wait_ge(sem("cols_in"), 16)
            dve.wait_ge(sem("c_tanh"), 1)
            cc = col("c", 0, 32).rearrange("p (v k) -> p v k", v=2)
            st(dve.scalar_tensor_tensor(C4F[:, 0:2], C4F[:, 0:2], 1.0, cc, ALU.add, ALU.mult))
            dve.tensor_scalar(C4F[:, 2:4], C4F[:, 0:2], 0.5, None, ALU.mult).then_inc(sem("c_silu"), 1)
            dve.wait_ge(sem("c_silu"), 1)
            st(dve.tensor_copy(CS[:], C4F[:, 2]))
            dve.wait_ge(sem("c_ready"), 1)
            c4 = C4[:].rearrange("p k (v h) -> p v k h", v=2)
            dve.tensor_tensor(c4[:, :, :, 1], C4F[:, 2:4], c4[:, :, :, 0].bitcast(F32), ALU.subtract)\
               .then_inc(sem("c_ready"), 1)
            dve.wait_ge(sem("lam_in"), 16)
            st(dve.tensor_tensor(LAMP[:], LAMV[:, 0:4:2], LAMV[:, 1:4:2], ALU.mult))
            dve.reduce_sum(LAM[:, 0:2], LAMP[:], axis=AX.X).then_inc(sem("lam_sum"), 1)
            dve.wait_ge(sem("lam_exp"), 1)
            st(dve.tensor_tensor(LAM[:, 4:5], LAM[:, 2:3], LAM[:, 3:4], ALU.subtract))
            dve.tensor_scalar(LAM[:, 5:6], LAM[:, 4:5], 0.2, None, ALU.add).then_inc(sem("lam_ready"), 1)
            for dst, name, n in ((0, "b_gate2", 32), (32, "b_glu", 4), (36, "lru_b_a", 12), (48, "lru_b_x", 12)):
                dve.tensor_scalar(HALF[:, dst:dst + n], col(name, 0, n), 0.5, None, ALU.mult)
            dve.scalar_tensor_tensor(HALF[:, 60:72], col("lru_lambda", 0, 12), -1.0, col("lru_lambda", 0, 12), ALU.mult, ALU.max)\
               .then_inc(sem("half_b"), 1)

            def mod_out(g, i, b):
                wait_block(dve, g, i, b)
                dve.tensor_copy(MROW[:, b % 2], PS[0:4, (b % 2) * NB:(b % 2) * NB + NB]).then_inc(stage_sem["free"], 1)

            to_lo(dve, G["mod"], 0, 0)
            to_lo(dve, G["mod"], 0, 1)

            def first_norm(c):
                if c == 4 * (MOD_FIRST - 1):
                    var(0, True)
                    for s_ in range(2):
                        last = dve.tensor_tensor(XIN[:, s_], XIN[:, s_], RBW[:, s_].unsqueeze(1).broadcast_to([P, KT, T]),
                                                 ALU.mult)
                    last.then_inc(sem("scales"), 1)
                    dve.wait_ge(sem("scales"), 1)
                    dve.wait_ge(sem("wg_hi"), 1)
                    dve.tensor_tensor(WGL[:], WG[:], WGH[:].bitcast(F32), ALU.subtract).then_inc(sem("wg_lo"), 1)
            feed(dve, to_lo, G["mod"], [mod_out], st, 0, beside=first_norm)
            dve.wait_ge(sem("mod_cols"), 1)
            first = 4 * MOD_FIRST
            bm = col("b_mod", 0, first).unsqueeze(2).broadcast_to([P, first, 2])
            st(dve.tensor_tensor(MODC[:, 0:first], bank(6, 2 * first).rearrange("p (k v) -> p k v", v=2), bm, ALU.add))
            for v in range(2):
                last = dve.scalar_tensor_tensor(SCALES[:, v], MODC[:, 16:32, v], 1.0, col("g_pre_mix", 0, 16),
                                                ALU.add, ALU.mult)
            last.then_inc(sem("scales"), 1)
            dve.wait_ge(sem("scales"), 2)
            for ch in range(8):
                if ch >= 2:
                    dve.wait_ge(hlo_ready, ch - 1)
                for j in range(4):
                    k = 4 * (ch % 4) + j
                    last = dve.tensor_scalar(TMPW[:, ch % 2, j], XIN[:, ch // 4, k, :], SCALES[:, ch // 4, k:k + 1],
                                             MODC[:, k, ch // 4:ch // 4 + 1], ALU.mult, ALU.add)
                st(last)
                dve.wait_ge(hhi_ready, ch + 1)
                k4 = slice(4 * (ch % 4), 4 * (ch % 4) + 4)
                dve.tensor_tensor(H1LO[:, ch // 4, k4], TMPW[:, ch % 2], H1HI[:, ch // 4, k4].bitcast(F32), ALU.subtract)\
                   .then_inc(hlo_ready, 1)

            def gate_steps(c):
                if c == 1:
                    dve.wait_ge(sem("grow_mm"), 1)
                    dve.wait_ge(sem("bg_in"), 16)
                    for k in range(4):
                        last = dve.tensor_scalar(GROW[:, k], PS[0:HEADS, (4 + k) * NB:(5 + k) * NB], BG[:, k:k + 1],
                                                 None, ALU.add)
                    last.then_inc(sem("grow"), 1)
                    dve.wait_ge(sem("grow"), 1)
                    forget = GROW[:, 1:4:2]
                    dve.scalar_tensor_tensor(GS[:, 0], forget, -1.0, forget, ALU.mult, ALU.max)\
                       .then_inc(sem("gate_abs"), 1)
                if c == 2:
                    forget = GROW[:, 1:4:2]
                    dve.wait_ge(sem("gate_ln"), 1)
                    st(dve.scalar_tensor_tensor(GS[:, 1], forget, 0.0, GS[:, 0], ALU.min, ALU.subtract))
                    one = ONES[0:HEADS, 0:1].broadcast_to([HEADS, 2 * T])
                    dve.wait_ge(sem("ones"), 1)
                    for d in range(2):
                        last = dve.tensor_tensor_scan(GS[:, 0, d], one, GS[:, 1, d], 0.0, ALU.mult, ALU.add)
                    st(last)
                    for d in range(2):
                        last = dve.tensor_tensor(GS[:, 1, d], GROW[:, 2 * d], GS[:, 0, d], ALU.subtract)
                    st(last)
                if c == 3:
                    for d in range(2):
                        last = dve.tensor_tensor_scan(GS[:, 2, d], GS[:, 1, d], GS[:, 1, d], 0.0, ALU.max, ALU.max)
                    st(last)
                    back = slice(2 * T - 1, T - 1, -1)
                    atok = GROW[:, 0:2]
                    dve.tensor_copy(atok[:, 0, 0:T], GS[:, 1, 0, T:2 * T])
                    dve.tensor_copy(atok[:, 0, T:2 * T], GS[:, 1, 0, 0:T])
                    dve.tensor_copy(atok[:, 1, 0:T], GS[:, 1, 1, back])
                    dve.tensor_copy(atok[:, 1, T:2 * T], GS[:, 1, 1, 0:T][:, ::-1])
                    dve.tensor_scalar(NEGM[:, 0], GS[:, 2, 0, T:2 * T], -1.0, None, ALU.mult)
                    dve.tensor_scalar(NEGM[:, 1], GS[:, 2, 1, back], -1.0, None, ALU.mult)
                    dve.tensor_tensor(GROW[:, 2, 0:T], GS[:, 0, 0, T:2 * T], GS[:, 2, 0, T:2 * T], ALU.add)
                    dve.tensor_tensor(GROW[:, 2, T:2 * T], GS[:, 0, 1, back], GS[:, 2, 1, back], ALU.add)\
                       .then_inc(sem("gate_em"), 1)
                    dve.wait_ge(sem("gate_em"), 1)

            def conv_edges(dst, wide_, col0):
                def s1(g, i, b):
                    wait_stage(dve, "a1", g, i, b)
                    ps = wide(g.b0 + b)
                    for w, to, frm in ((0, slice(1, T), slice(0, T - 1)), (2, slice(0, T - 1), slice(1, T))):
                        for j in range(4):
                            t = 4 * b + j
                            if wide_:
                                p, o = ps[:, j].rearrange("p (s t) -> p s t", s=2)[:, :, frm], dst[:, t, :, to]
                            else:
                                p, o = ps[:, j, frm], dst[:, t, to]
                            last = dve.scalar_tensor_tensor(o, p, col("conv_qk_w", 16 * w + col0 + t), o, ALU.mult, ALU.add)
                        if w == 0:
                            st(last)
                    last.then_inc(stage_sem["free"], 1)

                def s2(g, i, b):
                    wait_stage(dve, "a2", g, i, b)
                    th = KTH[:] if wide_ else QTH[:]
                    o = dst[:, 4 * b:4 * b + 4]
                    if wide_:
                        o, th = o.rearrange("p j s t -> p (j s t)"), th.rearrange("p j s t -> p (j s t)")
                    else:
                        o, th = o.rearrange("p j t -> p (j t)"), th.rearrange("p j t -> p (j t)")
                    dve.scalar_tensor_tensor(o, th, 1.0, o, ALU.add, ALU.mult).then_inc(stage_sem["d2"], 1)
                return [s1, s2]

            feed(dve, to_lo, G["mk"], conv_edges(MK, True, 8), beside=gate_steps)

            def gate_cols(c):
                if c == 3:
                    dve.wait_ge(sem("a_cols"), 1)
                    dve.tensor_copy(ACOL[:].rearrange("p d j h -> p (d j h)"), bank(6, 64))
                    dve.tensor_copy(EMT[:].rearrange("p d u h -> p (d u h)"), PS[:, 6 * NB + 64:6 * NB + 96])\
                       .then_inc(sem("a_copied"), 1)
                    dve.wait_ge(sem("a_copied"), 1)
                    dve.memset(MV[:, :, :, 128:129], 1.0).then_inc(sem("mv_ones"), 1)
            feed(dve, to_lo, G["mv"], [], beside=gate_cols)
            for name in ("dk", "dv"):
                feed(dve, to_lo, G[name], [])
            mod_sums_out(dve, MOD_REST // 2)
            dve.wait_ge(sem("mod_rest"), MOD_REST // 2 + 1)
            dve.scalar_tensor_tensor(SCALES[:, 3], MODC[:, 64:80, 0], 1.0, col("g_pre_ffn", 0, 16), ALU.add, ALU.mult)
            for n, chunk, gname in ((2, 2, "g_post_mix"), (4, 5, "g_post_ffn")):
                last = dve.tensor_tensor(SCALES[:, n], MODC[:, 16 * chunk:16 * chunk + 16, 0], col(gname, 0, 16), ALU.mult)
            st(last)
            feed(dve, to_lo, G["mq"], conv_edges(MQ, False, 0))
            for name in ("dq", "mo"):
                feed(dve, to_lo, G[name], [])

            wait_stage(dve, "free", G["mo"], 0, 1)
            mo_flat = MO[:].rearrange("p h t -> p (h t)")
            st(dve.tensor_scalar(mo_flat, mo_flat, 1.0, None, ALU.add))
            ST16 = STAT[:, 0:16]
            for half in range(2):
                if half == 0:
                    wait_block(dve, G["mo"], 0, 1)
                if half:
                    dve.wait_ge(sem("m_t"), 1)
                dve.memset(MW[:, 0, 1, 0:128], 0.0)
                dve.memset(MW[:, 1, 0, 128:256], 0.0).then_inc(sem("m_zero"), 1)
                dve.wait_ge(sem("m_zero"), half + 1)
                for hh in range(4):
                    h = 4 * half + hh
                    for d in range(2):
                        dve.wait_ge(sem("m_w"), 2 * h + d + 1)
                        dve.wait_ge(sem("m_s"), h + 1)
                        if h:
                            dve.wait_ge(sem("m_pv"), 2 * (h - 1) + d + 1)
                        sp_ = PS[:, (h % 2) * 1024:(h % 2) * 1024 + 1024]
                        dve.scalar_tensor_tensor(MP[:, d].rearrange("p j t -> p (j t)"), sp_, 0.25 * 128 ** -0.5,
                                                 MW[:, d].rearrange("p j t -> p (j t)"), ALU.mult, ALU.mult)\
                           .then_inc(sem("m_p"), 1)
                dve.wait_ge(sem("m_num"), 8 * (half + 1))
                dve.wait_ge(sem("m_p"), 8 * (half + 1))
                st(dve.scalar_tensor_tensor(STAT[:, 16:32], ST16, -1.0, ST16, ALU.mult, ALU.max))
                den = STAT[:, 16:32].rearrange("p (d u h) -> p d u h", d=2, u=2)
                st(dve.tensor_tensor(den, den, EMT[:, :, :, 4 * half:4 * half + 4], ALU.max))
                st(dve.reciprocal(STAT[:, 16:32], STAT[:, 16:32]))
                for d in range(2):
                    last = dve.tensor_tensor((MH, MSQ)[d][:], NUM[:, d],
                                             den[:, d].unsqueeze(3).broadcast_to([P, TT, 4, P]), ALU.mult)
                st(last)
                st(dve.tensor_tensor(MH[:], MH[:], MSQ[:], ALU.add))
                st(dve.tensor_tensor(MSQ[:], MH[:], MH[:], ALU.mult))
                st(dve.reduce_sum(STAT[:, 0:8].rearrange("p (u h) -> p u h", u=2), MSQ[:], axis=AX.X))
                st(dve.tensor_scalar(STAT[:, 0:8], STAT[:, 0:8], 4.0 / P, 4.0 * EPS, ALU.mult, ALU.add))
                dve.reciprocal(STAT[:, 0:8], STAT[:, 0:8]).then_inc(sem("m_var"), 1)
                dve.wait_ge(sem("m_rstd"), half + 1)
                rs = STAT[:, 0:8].rearrange("p (u h) -> p u h", u=2).unsqueeze(3).broadcast_to([P, TT, 4, P])
                dve.tensor_tensor(MH[:], MH[:], rs, ALU.mult).then_inc(sem("m_h"), 1)
                dve.wait_ge(sem("m_t"), half + 1)
                for hh in range(4):
                    h = 4 * half + hh
                    last = dve.scalar_tensor_tensor(MIX[:, h], PS[:, 4 * NB + T * hh:4 * NB + T * hh + T],
                                                    col("g_mlstm", h), MO[:, h], ALU.mult, ALU.mult)
                last.then_inc(sem("mixm_done"), 1)
            dve.wait_ge(sem("mixm_done"), 2)

            cos2 = ROPE[:, 0].unsqueeze(1).broadcast_to([P, 2, T])
            sin2 = ROPE[:, 1].unsqueeze(1).broadcast_to([P, 2, T])
            dve.wait_ge(sem("rope_in"), 16)
            for r in range(8):
                v = DQ[:, 2 * r:2 * r + 2, :] if r < 4 else DK[:, 2 * (r - 4):2 * (r - 4) + 2, 0, :]
                st(dve.tensor_tensor(RT1[:], v, cos2, ALU.mult))
                dve.wait_ge(sem("rot"), r + 1)
                st(dve.tensor_tensor(RT2[:], bank(r % 2).rearrange("p (h t) -> p h t", h=2), sin2, ALU.mult))
                dve.tensor_tensor(v, RT1[:], RT2[:], ALU.add).then_inc(sem("roped"), 1)
                dve.wait_ge(sem("roped"), r + 1)

            def d_max(u):
                par = u % 2
                dve.wait_ge(sem("d_s"), u + 1)
                s8 = STAT[:, 8 * par:8 * par + 8]
                st(dve.reduce_max(s8[:, 0:2], PS[:, par * 1024:par * 1024 + 1024].rearrange("p (c k) -> p c k", c=2),
                                  axis=AX.X))
                dve.tensor_scalar(s8[:, 2:4], s8[:, 0:2], -0.125, None, ALU.mult).then_inc(sem("d_nm"), 1)

            def d_prob(u):
                par = u % 2
                s8 = STAT[:, 8 * par:8 * par + 8]
                dve.wait_ge(sem("d_e"), u + 1)
                st(dve.reciprocal(s8[:, 6:8], s8[:, 4:6]))
                st(dve.tensor_scalar(s8[:, 7:8], s8[:, 7:8], LAM[:, 5:6], None, ALU.mult))
                st(dve.tensor_scalar(DE[:, par, 1], DE[:, par, 1], s8[:, 7:8], None, ALU.mult))
                if u >= 2:
                    dve.wait_ge(sem("d_t"), u - 1)
                dve.scalar_tensor_tensor(DP[:, par], DE[:, par, 0], s8[:, 6:7], DE[:, par, 1],
                                         ALU.mult, ALU.subtract).then_inc(sem("d_p"), 1)

            U = 2 * HEADS
            dve.wait_ge(sem("m_t"), 2)
            for u in range(U + 2):
                if u >= 2:
                    d_prob(u - 2)
                    dve.wait_ge(sem("d_p"), u - 1)
                if u < U:
                    d_max(u)
            dve.wait_ge(sem("d_oc"), U)
            dve.wait_ge(sem("d_p"), U)
            st(dve.tensor_tensor(DSQ[:], DO[:], DO[:], ALU.mult))
            st(dve.reduce_sum(ST16.rearrange("p (u h) -> p u h", u=2), DSQ[:], axis=AX.X))
            st(dve.tensor_scalar(ST16, ST16, 1.0 / (P * 0.64), EPS / 0.64, ALU.mult, ALU.add))
            dve.reciprocal(ST16, ST16).then_inc(sem("d_var"), 1)
            dve.wait_ge(sem("d_rstd"), 1)
            rs = ST16.rearrange("p (u h) -> p u h", u=2).unsqueeze(3).broadcast_to([P, TT, HEADS, P])
            dve.tensor_tensor(DO[:], DO[:], rs, ALU.mult).then_inc(sem("d_on"), 1)
            dve.wait_ge(sem("d_ot"), 1)
            dve.tensor_scalar(MIX[:, 8:16].rearrange("p h t -> p (h t)"), PS[:, 0:2048], col("g_diff"), None, ALU.mult)\
               .then_inc(sem("mixd_done"), 1)
            split(APPLY["mix"], HHI, HLO, MIX)
            feed(dve, to_lo, G["wout"], [])
            dve.wait_ge(sem("x2_in"), 16)
            residual(1, lambda k: SCALES[:, 2, k:k + 1])
            dve.wait_ge(x_new, 4)
            var(2, False)
            wait_block(dve, G["wout"], 0, 3)
            apply(APPLY["ffn"], TMPS["ffn"], 4, TMP, lambda ch, k: X[:, 4 * ch + k],
                  lambda ch, k: SCALES[:, 3, 4 * ch + k:4 * ch + k + 1], lambda ch: RB[:, 0],
                  lambda ch, k: (HHI[:, 4 * ch + k], HLO[:, 4 * ch + k]), lambda ch, k: MODC[:, 48 + 4 * ch + k, 0:1])

            def up_stages(part):
                f0 = FFN_PARTS[part][0]

                def s1(g, i, b):
                    wait_stage(dve, "a1", g, i, b)
                    ps, par = narrow(g.b0 + b), b % 2
                    for w, to, frm in ((0, slice(1, T), slice(0, T - 1)), (2, slice(0, T - 1), slice(1, T))):
                        for j in range(4):
                            t = (j // 2) * FT + j % 2 + 2 * (f0 + b)
                            at_ = COL_AT["conv_ffn_w"][0] + 2 * FT * w + t + mult(i, 4)
                            last = dve.scalar_tensor_tensor(UC[:, par, j, to], ps[:, j, frm], COL[:, bass.ds(at_, 1)],
                                                            UC[:, par, j, to], ALU.mult, ALU.add)
                        if w == 0:
                            st(last)
                    last.then_inc(stage_sem["free"], 1)

                def s2(g, i, b):
                    wait_stage(dve, "a2", g, i, b)
                    par = b % 2
                    st(dve.scalar_tensor_tensor(UTH[:, par], UTH[:, par], 1.0, UC[:, par, 0:2], ALU.add, ALU.mult))
                    dve.scalar_tensor_tensor(UACT[:, par], UTH[:, par], 0.5, UC[:, par, 2:4], ALU.mult, ALU.mult)\
                       .then_inc(stage_sem["d2"], 1)

                def s3(g, i, b):
                    wait_stage(dve, "a3", g, i, b)
                    k = bass.ds(mult(i, 4) + 2 * b, 2)
                    dve.tensor_tensor(ALO[:, k], UACT[:, b % 2], AHI[:, k].bitcast(F32), ALU.subtract)\
                       .then_inc(stage_sem["d3"], 1)
                return [s1, s2, s3]

            def add_y(g, i, b):
                wait_block(dve, g, i, b)
                y = Y[:, 4 * b:4 * b + 4]
                dve.tensor_tensor(y, narrow(g.b0 + b), y, ALU.add).then_inc(stage_sem["free"], 1)

            for part in range(3):
                feed(dve, to_lo, G[f"up{part}"], up_stages(part), st, 2)
                if part == 1:
                    wait_stage(dve, "free", G["down0"], 0, 3)
                if part == 2:
                    wait_stage(dve, "free", G["down1"], 0, 3)
                feed(dve, to_lo, G[f"down{part}"], [add_y] if part else [])
            wait_stage(dve, "free", G["down2"], 0, 3)
            residual(3, lambda k: SCALES[:, 4, k:k + 1])
            dve.wait_ge(x_new, 8)
            var(4, False)
            wait_block(dve, G["down2"], 0, 3)
            apply(APPLY["mix2"], TMPS["mix2"], 4, TMP, lambda ch, k: X[:, 4 * ch + k],
                  lambda ch, k: col("norm_mix", 4 * ch + k), lambda ch: RB[:, 0],
                  lambda ch, k: (HHI[:, 4 * ch:4 * ch + 4], HLO[:, 4 * ch:4 * ch + 4]))

            def x_taps(g, i, b):
                wait_stage(dve, "a1", g, i, b)
                ps = narrow(g.b0 + b)
                for w in range(3):
                    back_ = 3 - w
                    for j in range(4):
                        t = 4 * b + j
                        o = XC[:, t, back_:T]
                        last = dve.scalar_tensor_tensor(o, ps[:, j, 0:T - back_], col("lru_conv_w", 12 * w + t), o,
                                                        ALU.mult, ALU.add)
                    if w < 2:
                        st(last)
                last.then_inc(stage_sem["free"], 1)

            def y_cube(g, i, b):
                wait_stage(dve, "a1", g, i, b)
                if b:
                    wait_stage(dve, "free", g, i, b - 1)
                st(dve.tensor_scalar(YSQ[:], YSQ[:], 0.044715, 1.0, ALU.mult, ALU.add))
                dve.tensor_tensor(YTH[:], narrow(g.b0 + b), YSQ[:], ALU.mult).then_inc(stage_sem["d1"], 1)

            def y_gelu(g, i, b):
                wait_stage(dve, "a2", g, i, b)
                dve.scalar_tensor_tensor(YG[:, 4 * b:4 * b + 4], YTH[:], 1.0, narrow(g.b0 + b), ALU.add, ALU.mult)\
                   .then_inc(stage_sem["free"], 1)

            feed(dve, to_lo, G["in_u"], [])
            feed(dve, to_lo, G["in_x"], [x_taps])
            feed(dve, to_lo, G["in_y"], [y_cube, y_gelu])

            def s5(n, m=1):
                return S5S[:, n:n + m]
            re, im = col("lam_re", 0, 16).unsqueeze(1), col("lam_im", 0, 16).unsqueeze(1)
            MAGIC = 1.5 * 2 ** 23
            dve.wait_ge(sem("s5_step"), 1)
            st(dve.tensor_tensor(s5(2), im, s5(0), ALU.mult))
            dve.tensor_tensor(s5(1), re, s5(0), ALU.mult)
            st(dve.tensor_scalar(s5(11), s5(2), 1.0 / (2 * math.pi), MAGIC, ALU.mult, ALU.add))
            st(dve.tensor_scalar(s5(11), s5(11), MAGIC, None, ALU.subtract))
            st(dve.scalar_tensor_tensor(s5(3), s5(11), -6.28125, s5(2), ALU.mult, ALU.add))
            c2 = float(np.float32(2 * math.pi - 6.28125))
            st(dve.scalar_tensor_tensor(s5(3), s5(11), -c2, s5(3), ALU.mult, ALU.add))
            pi_ = float(np.nextafter(np.float32(math.pi), np.float32(0)))
            dve.tensor_scalar(s5(3), s5(3), pi_, -pi_, ALU.min, ALU.max).then_inc(sem("s5_pre"), 1)
            dve.wait_ge(sem("s5_pre"), 1)
            st(dve.tensor_scalar(s5(14), s5(3), 1.0 / (2 * math.pi), None, ALU.mult))
            st(dve.tensor_scalar(s5(15), s5(14), 16.0, None, ALU.mult))
            st(dve.tensor_scalar(s5(11), s5(15), MAGIC, None, ALU.add))
            st(dve.tensor_scalar(s5(11), s5(11), MAGIC, None, ALU.subtract))
            st(dve.tensor_tensor(s5(15), s5(15), s5(11), ALU.subtract))
            iota = CST[:, C_IOTA:C_IOTA + 16].unsqueeze(1).broadcast_to([P, 16, 16])
            for w in range(2):
                last = dve.tensor_tensor(EX[:, 0, w], s5(14 + w).rearrange("p a s -> p (a s)").unsqueeze(2)
                                         .broadcast_to([P, 16, 16]), iota, ALU.mult)
            st(last)

            def flat(x):
                return x.rearrange("p a s n -> p (a s n)")
            st(dve.tensor_scalar(flat(EX[:, 1]), flat(EX[:, 0]), 0.25, None, ALU.add))
            ex, exr = EX[:].rearrange("p f a s n -> p (f a s n)"), EXR[:].rearrange("p f a s n -> p (f a s n)")
            st(dve.tensor_scalar(exr, ex, MAGIC, None, ALU.add))
            st(dve.tensor_scalar(exr, exr, MAGIC, None, ALU.subtract))
            dve.tensor_tensor(ex, ex, exr, ALU.subtract).then_inc(sem("s5_ang"), 1)
            dve.wait_ge(sem("s5_abs"), 1)
            dve.wait_ge(sem("s5_sin"), 1)
            st(dve.tensor_tensor(s5(12), s5(5), s5(5), ALU.mult))
            st(dve.tensor_scalar(s5(12), s5(12), -2.0, 1.0, ALU.mult, ALU.add))
            dve.tensor_tensor(s5(7), s5(1), s5(4), ALU.mult)
            st(dve.tensor_tensor(s5(6), s5(1), s5(12), ALU.mult))
            st(dve.tensor_scalar(s5(6), s5(6), -1.0, None, ALU.add))
            dve.tensor_tensor(s5(11), re, re, ALU.mult)
            st(dve.tensor_tensor(s5(12), im, im, ALU.mult))
            st(dve.tensor_tensor(s5(8), s5(11), s5(12), ALU.add))
            st(dve.reciprocal(s5(8), s5(8)))
            dve.tensor_tensor(s5(11), s5(6), re, ALU.mult)
            st(dve.tensor_tensor(s5(12), s5(7), im, ALU.mult))
            st(dve.tensor_tensor(s5(9), s5(11), s5(12), ALU.add))
            dve.tensor_tensor(s5(11), s5(7), re, ALU.mult)
            st(dve.tensor_tensor(s5(12), s5(6), im, ALU.mult))
            st(dve.tensor_tensor(s5(10), s5(11), s5(12), ALU.subtract))
            for n in (9, 10):
                last = dve.tensor_tensor(s5(n), s5(n), s5(8), ALU.mult)
            st(last)
            dve.wait_ge(sem("s5w_in"), 32)
            cf = [S5S[:, n].unsqueeze(2).broadcast_to([P, ST_TILES, 32]) for n in (9, 10)]

            def m5(x):
                return x.rearrange("p a t -> p (a t)").rearrange("p (k n) -> p k n", k=ST_TILES)
            wait_block(dve, G["down2"], 0, 3)
            for o, v, f in ((SM1, 0, 0), (SM2, 1, 1), (SV, 0, 1), (SZ, 1, 0)):
                last = dve.tensor_tensor(m5(o), S5C[:, v], cf[f], ALU.mult)
            st(last)
            dve.tensor_tensor(S5C[:, 0], m5(SM1), m5(SM2), ALU.subtract)
            st(dve.tensor_tensor(S5C[:, 1], m5(SV), m5(SZ), ALU.add))
            dve.tensor_scalar(S5C[:, 1], S5C[:, 1], -1.0, None, ALU.mult).then_inc(sem("s5_c"), 1)
            dve.wait_ge(sem("s5_c"), 1)
            dve.wait_ge(sem("s5_esc"), 1)
            for kt in range(S5_TILES):
                def fine(f):
                    return ESC[:, f, 0, 4 * kt:4 * kt + 4].unsqueeze(2).broadcast_to([P, 4, 16, 16])

                def coarse(f):
                    return ESC[:, f, 1, 4 * kt:4 * kt + 4].unsqueeze(3).broadcast_to([P, 4, 16, 16])

                def t5(x):
                    return x.rearrange("p s (a n) -> p s a n", a=16)
                for f, (g1, h1), (g2, h2), op in ((0, (1, 1), (0, 0), ALU.subtract), (1, (0, 1), (1, 0), ALU.add)):
                    dve.tensor_tensor(t5(ET[:, 0]), coarse(g1), fine(h1), ALU.mult)
                    st(dve.tensor_tensor(t5(ET[:, 1]), coarse(g2), fine(h2), ALU.mult))
                    st(dve.tensor_tensor(ECS[:, f], ET[:, 0], ET[:, 1], op))
                for a in range(4):
                    s_ = 4 * kt + a
                    cs = ECS[:, 0, a].unsqueeze(1).broadcast_to([P, 2, T])
                    sn = ECS[:, 1, a].unsqueeze(1).broadcast_to([P, 2, T])
                    dve.wait_ge(sem("s5_bu"), s_ + 1)
                    bu = bank(4 + s_ % 2).rearrange("p (f t) -> p f t", f=2)
                    dve.tensor_tensor(SM1[:], bu, cs, ALU.mult)
                    dve.tensor_tensor(SM2[:], bu, sn, ALU.mult).then_inc(sem("s5_bu_read"), 1)
                    dve.wait_ge(sem("s5_bu_read"), s_ + 1)
                    dve.tensor_tensor(SV[:, 0], SM1[:, 0], SM2[:, 1], ALU.add)
                    st(dve.tensor_tensor(SV[:, 1], SM1[:, 1], SM2[:, 0], ALU.subtract))
                    r = S5S[:, 1, s_:s_ + 1].broadcast_to([P, T])
                    dve.tensor_tensor_scan(SZ[:, 0], r, SV[:, 0], 0.0, ALU.mult, ALU.add)
                    st(dve.tensor_tensor_scan(SZ[:, 1], r, SV[:, 1], 0.0, ALU.mult, ALU.add))
                    dve.tensor_tensor(SM1[:], SZ[:], cs, ALU.mult)
                    st(dve.tensor_tensor(SM2[:], SZ[:], sn, ALU.mult))
                    if s_ >= 2:
                        dve.wait_ge(sem("s5_cy"), s_ - 1)
                    dve.tensor_tensor(SST[:, s_ % 2, 0], SM1[:, 0], SM2[:, 1], ALU.subtract)
                    dve.tensor_tensor(SST[:, s_ % 2, 1], SM1[:, 1], SM2[:, 0], ALU.add).then_inc(sem("s5_s"), 1)
                    dve.wait_ge(sem("s5_s"), s_ + 1)
                dve.wait_ge(sem("s5_cy"), 4 * kt + 4)
                dve.scalar_tensor_tensor(Y5[:, kt], U5[:, kt], col("s5_d", kt), PS[:, (6 + kt % 2) * NB:(6 + kt % 2) * NB + T],
                                         ALU.mult, ALU.add).then_inc(sem("s5_yk"), 1)
            dve.wait_ge(sem("s5_yk"), 4)
            dve.tensor_copy(STAT[:, 0:1], Y5[:, 3, 0:1]).then_inc(sem("s5_y"), 1)
            dve.wait_ge(sem("s5_ysq"), 1)
            st(dve.tensor_scalar(Y5B[:], Y5B[:], 0.044715, 1.0, ALU.mult, ALU.add))
            dve.tensor_tensor(Y5B[:], Y5B[:], Y5[:], ALU.mult).then_inc(sem("s5_yt"), 1)
            dve.wait_ge(sem("s5_yth"), 1)
            st(dve.scalar_tensor_tensor(Y5[:], Y5B[:], 1.0, Y5[:], ALU.add, ALU.mult))
            dve.tensor_scalar(Y5[:], Y5[:], 0.5, None, ALU.mult).then_inc(sem("s5_g"), 1)
            dve.wait_ge(sem("s5_ghi"), 1)
            dve.wait_ge(sem("s5_g"), 1)
            dve.tensor_tensor(GLO[:], Y5[:], GHI[:].bitcast(F32), ALU.subtract).then_inc(sem("s5_glo"), 1)
            feed(dve, to_lo, G["glu"], [])
            wait_stage(dve, "free", G["glu"], 0, 0)
            st(dve.scalar_tensor_tensor(Y5[:], Y5B[:], 1.0, Y5[:], ALU.add, ALU.mult))
            st(dve.tensor_scalar(Y5[:], Y5[:], 0.5, None, ALU.mult))

            dve.wait_ge(sem("sp_e"), 1)
            z = HALF[:, 60:72]
            u_ = S5S[:, 6, 0:12]
            dve.tensor_scalar(u_, z, 1.0, None, ALU.add).then_inc(sem("sp_u"), 1)
            dve.wait_ge(sem("sp_u"), 1)
            st(dve.tensor_scalar(S5S[:, 8, 0:12], u_, -1.0, None, ALU.add))
            st(dve.tensor_scalar(S5S[:, 9, 0:12], S5S[:, 8, 0:12], 0.0, None, ALU.is_equal))
            st(dve.tensor_tensor(S5S[:, 8, 0:12], S5S[:, 8, 0:12], S5S[:, 9, 0:12], ALU.add))
            st(dve.reciprocal(S5S[:, 8, 0:12], S5S[:, 8, 0:12]))
            dve.wait_ge(sem("sp_ln"), 1)
            st(dve.tensor_tensor(S5S[:, 7, 0:12], S5S[:, 7, 0:12], S5S[:, 8, 0:12], ALU.mult))
            st(dve.tensor_tensor(S5S[:, 7, 0:12], S5S[:, 7, 0:12], S5S[:, 9, 0:12], ALU.add))
            st(dve.tensor_tensor(S5S[:, 7, 0:12], S5S[:, 7, 0:12], z, ALU.mult))
            st(dve.tensor_scalar(S5S[:, 8, 0:12], col("lru_lambda", 0, 12), -1.0, 0.0, ALU.mult, ALU.max))
            st(dve.tensor_tensor(S5S[:, 7, 0:12], S5S[:, 7, 0:12], S5S[:, 8, 0:12], ALU.add))
            st(dve.tensor_scalar(z, S5S[:, 7, 0:12], 4.0, None, ALU.mult))
            for half in range(2):
                for h in range(LH):
                    t = half * LH + h
                    dve.wait_ge(sem("lru_ri"), t + 1)
                    last = dve.tensor_scalar(LR[:, h], LR[:, h], 1.0, HALF[:, 60 + t:61 + t], ALU.add, ALU.mult)
                last.then_inc(sem("lru_y"), 1)
                dve.wait_ge(sem("lru_th"), half + 1)
                st(dve.tensor_scalar(LT[:], LA[:], 1.0, None, ALU.add))
                st(dve.reciprocal(LT[:], LT[:]))
                dve.tensor_tensor(LA[:], LA[:], LT[:], ALU.mult).then_inc(sem("lru_m"), 1)
                xs = XC[:, half * LH:(half + 1) * LH]
                st(dve.scalar_tensor_tensor(LI[:], LI[:], 1.0, xs, ALU.add, ALU.mult))
                dve.wait_ge(sem("lru_sq"), half + 1)
                st(dve.memset(LA[:, :, 0:1], 1.0))
                st(dve.tensor_tensor(LI[:], LI[:], LA[:], ALU.mult))
                dve.wait_ge(sem("lru_a"), half + 1)
                for h in range(LH):
                    last = dve.tensor_tensor_scan(LT[:, h], LR[:, h], LI[:, h], 0.0, ALU.mult, ALU.add)
                st(last)
                dve.scalar_tensor_tensor(OUT5[:, 4 + half * LH:4 + (half + 1) * LH], LT[:], 0.25,
                                         YG[:, half * LH:(half + 1) * LH], ALU.mult, ALU.mult)\
                   .then_inc(sem("lru_out"), 1)
            dve.wait_ge(sem("lru_out"), 2)
            split(APPLY["lru"], AHI, ALO, OUT5)

            def proj_out(k):
                def s1(g, i, b):
                    wait_block(dve, g, i, b)
                    wait_stage(dve, "free", G[f"gates{k}"], 0, 1)
                    ps = wide(g.b0 + b)
                    for v in range(2):
                        last = dve.scalar_tensor_tensor(PM[:, v], GT[:, v], 1.0, ps[:, :, T * v:T * v + T],
                                                        ALU.add, ALU.mult)
                    last.then_inc(stage_sem["free"], 1)

                def s2(g, i, b):
                    wait_stage(dve, "free", g, i, b)
                    st(dve.tensor_tensor(PM[:, 0], PM[:, 0], PM[:, 1], ALU.add))
                    dve.tensor_scalar(MG[:, 4 * k:4 * k + 4], PM[:, 0], 0.5, None, ALU.mult)\
                       .then_inc(stage_sem["d2"], 1)
                return [s1, s2]

            for k in range(4):
                feed(dve, to_lo, G[f"gates{k}"], [])
                feed(dve, to_lo, G[f"proj{k}"], proj_out(k))
            wait_stage(dve, "d2", G["proj3"], 0, 0)
            split(APPLY["merged"], HHI, HLO, MG)

            def add_x(g, i, b):
                wait_block(dve, g, i, b)
                x = X[:, 4 * b:4 * b + 4]
                dve.tensor_tensor(x, narrow(g.b0 + b), x, ALU.add).then_inc(stage_sem["free"], 1)

            feed(dve, to_lo, G["out2"], [add_x])
            wait_stage(dve, "free", G["out2"], 0, 3)
            var(5, False)
            apply(APPLY["moe"], TMPS["moe"], 4, TMP, lambda ch, k: X[:, 4 * ch + k],
                  lambda ch, k: col("norm_ffn", 4 * ch + k), lambda ch: RB[:, 0],
                  lambda ch, k: (HHI[:, 4 * ch:4 * ch + 4], HLO[:, 4 * ch:4 * ch + 4]))
            dve.wait_ge(sem("wr_hi"), 1)
            dve.tensor_tensor(WRL[:], WR[:], WRH[:].bitcast(F32), ALU.subtract).then_inc(sem("wr_lo"), 1)
            dve.wait_ge(sem("r_cols"), 1)
            dve.wait_ge(sem("rbias_in"), 16)
            lg = RS[:, 0:2].rearrange("p a u e -> p (a u e)")[:, 0:72].rearrange("p (u e) -> p u e", u=2)
            st(dve.tensor_tensor(lg, bank(7, 72).rearrange("p (u e) -> p u e", u=2),
                                 RBIAS[:].unsqueeze(1).broadcast_to([P, TT, 36]), ALU.add))

            def r(n, m):
                return RS[:, n, :, 0:m]

            def first_of(best, values, n, slot, dst):
                it = CST[:, C_IOTA:C_IOTA + n].unsqueeze(1).broadcast_to([P, TT, n])
                st(dve.tensor_tensor(r(slot, n), values, best.broadcast_to([P, TT, n]), ALU.is_equal))
                st(dve.tensor_scalar(r(slot, n), r(slot, n), -1000.0, 1000.0, ALU.mult, ALU.add))
                st(dve.tensor_tensor(r(slot, n), r(slot, n), it, ALU.add))
                st(dve.tensor_reduce(r(slot + 1, 1), r(slot, n), AX.X, ALU.min))
                st(dve.tensor_tensor(dst, it, r(slot + 1, 1).broadcast_to([P, TT, n]), ALU.is_equal))

            gl = lg[:, :, 0:4]
            st(dve.reduce_max(r(4, 1), gl, axis=AX.X))
            dve.tensor_tensor(r(2, 4), gl, r(4, 1).broadcast_to([P, TT, 4]), ALU.subtract).then_inc(sem("r_shift"), 1)
            first_of(r(4, 1), gl, 4, 5, r(3, 4))
            dve.wait_ge(sem("r_exp"), 1)
            st(dve.reduce_sum(r(4, 1), r(2, 4), axis=AX.X))
            st(dve.reciprocal(r(4, 1), r(4, 1)))
            el = lg[:, :, 4:36].rearrange("p u (g e) -> p u g e", g=4)
            for u in range(TT):
                last = dve.tensor_tensor(RS[:, 7, u].rearrange("p (g e) -> p g e", g=4), el[:, u],
                                         r(3, 4)[:, u].unsqueeze(2).broadcast_to([P, 4, 8]), ALU.mult)
            st(last)
            for u in range(TT):
                last = dve.reduce_sum(RS[:, 8, u, 0:8], RS[:, 7, u].rearrange("p (g e) -> p e g", g=4), axis=AX.X)
            st(last)
            st(dve.reduce_max(r(9, 1), r(8, 8), axis=AX.X))
            st(dve.tensor_copy(r(10, 1), r(9, 1)))
            first_of(r(10, 1), r(8, 8), 8, 5, r(11, 8))
            st(dve.scalar_tensor_tensor(r(8, 8), r(11, 8), -BIG, r(8, 8), ALU.mult, ALU.add))
            st(dve.reduce_max(r(12, 1), r(8, 8), axis=AX.X))
            first_of(r(12, 1), r(8, 8), 8, 5, r(13, 8))
            dve.tensor_tensor(r(9, 1), r(12, 1), r(10, 1), ALU.subtract).then_inc(sem("r_gap"), 1)
            dve.wait_ge(sem("r_gape"), 1)
            st(dve.tensor_scalar(r(10, 1), r(9, 1), 1.0, None, ALU.add))
            st(dve.reciprocal(r(10, 1), r(10, 1)))
            st(dve.tensor_tensor(r(10, 1), r(10, 1), r(4, 1), ALU.mult))
            st(dve.tensor_tensor(r(9, 1), r(9, 1), r(10, 1), ALU.mult))
            dve.tensor_tensor(r(11, 8), r(11, 8), r(10, 1).broadcast_to([P, TT, 8]), ALU.mult)
            st(dve.tensor_tensor(r(13, 8), r(13, 8), r(9, 1).broadcast_to([P, TT, 8]), ALU.mult))
            st(dve.tensor_tensor(r(11, 8), r(11, 8), r(13, 8), ALU.add))
            for u in range(TT):
                last = dve.tensor_tensor(RS[:, 14, u].rearrange("p (g e) -> p g e", g=4),
                                         r(3, 4)[:, u].unsqueeze(2).broadcast_to([P, 4, 8]),
                                         r(11, 8)[:, u].unsqueeze(1).broadcast_to([P, 4, 8]), ALU.mult)
            last.then_inc(sem("r_comb"), 1)

            def moe_mid(part):
                def s2(g, i, b):
                    wait_stage(dve, "a2", g, i, b)
                    if part == 0:
                        dve.wait_ge(sem("cb"), 8)
                    ps = narrow(g.b0 + b)
                    st(dve.scalar_tensor_tensor(MS1[:], MTH[:], 1.0, ps[:, 0:2], ALU.add, ALU.mult))
                    dve.scalar_tensor_tensor(MS2[:], MS1[:], 0.5, ps[:, 2:4], ALU.mult, ALU.mult)\
                       .then_inc(stage_sem["free"], 1)
                    wait_stage(dve, "free", g, i, b)
                    cb = CB[:, bass.ds(mult(i, 2) + b + 8 * part, 1)].rearrange("p e t -> p (e t)")\
                        .unsqueeze(1).broadcast_to([P, 2, T])
                    dve.tensor_tensor(MACT[:], MS2[:], cb, ALU.mult).then_inc(stage_sem["d2"], 1)
                return s2

            def moe_lo(g, i, b):
                wait_stage(dve, "a3", g, i, b)
                wait_stage(dve, "d2", g, i, b)
                k = bass.ds(mult(i, 4) + 2 * b, 2)
                dve.tensor_tensor(ALO[:, k], MACT[:], AHI[:, k].bitcast(F32), ALU.subtract)\
                   .then_inc(stage_sem["d3"], 1)

            for part in range(4):
                feed(dve, to_lo, G[f"moe_up{part}"], [moe_mid(part), nothing, moe_lo], st, 1)
                if part:
                    wait_stage(dve, "free", G[f"moe_down{part - 1}"], 0, 3)
                feed(dve, to_lo, G[f"moe_down{part}"], [add_x])
            var(6, False)
            wait_block(dve, G["moe_down3"], 0, 3)
            for ch in range(4):
                for k in range(4 * ch, 4 * ch + 4):
                    last = dve.scalar_tensor_tensor(OUTB[:, k], X[:, k], col("norm_final", k), RB[:, 0],
                                                    ALU.mult, ALU.mult)
                last.then_inc(sem("out_ready"), 1)

        @block.tensor
        def _(pe):
            pe.sem_inc(slot_used, 2)
            pe.sem_inc(stage_sem["free"], 2)
            ident, rev = CST[:, C_ID:C_ID + P], CST[:, C_REV:C_REV + P]

            def slot(g, i, b, q, products):
                c = b * g.slots + q
                par = (g.m0 + c) % 2
                wait_place(pe, g, i, c, RING)
                last = products(par, q)
                last.then_inc(slot_used, 1)

            def mod_sums(w, free):
                pe.wait_ge(stage_sem["free"], free)
                for mb in range(max(2 * w - 1, 0), min(2 * w + 1, MOD_REST)):
                    pe.wait_ge(lo_done, G["mk"].s0 + (4 * mb + 3) // 2 * 3 + (4 * mb + 3) % 2 + 2 + RING)
                    for j in range(4):
                        at_ = mod_sums_at(w) + 4 * (mb - 2 * w + 1) + j
                        last = pe.matmul(PS[:, at_:at_ + 1], MACC[:, mb % 2, P * j:P * j + P], ONES[:, 0:1],
                                         start=True, stop=True)
                last.then_inc(sem("mod_sums_read"), 1)

            def blocks(g, products, beside=None):
                def one(i, b):
                    pe.wait_ge(stage_sem["free"], mult(i, 2) + (g.base.get("free", 0) + b + 1))
                    w = (g.m0 - G["mk"].m0) // 4 + b
                    if w and (g.extra or g.name == "mq" and b == 0):
                        pe.wait_ge(sem("mod_rest"), w if g.extra else w + 1)
                    for q in range(g.slots):
                        slot(g, i, b, q, products(g, i, b))
                        if beside:
                            beside(b * g.slots + q)
                        if g.extra and q == 1:
                            mod_sums(w, g.base["free"] + b + 2)
                if g.blocks >= 4 and 2 * g.slots % RING == 0:
                    with pe.Fori(0, g.blocks // 2) as i:
                        one(i, 0)
                        one(i, 1)
                else:
                    for b in range(g.blocks):
                        one(0, b)

            def weights_still(hi, lo, wide_):
                def products(g, i, b):
                    ps = wide(g.b0 + b) if wide_ else narrow(g.b0 + b)

                    def run(par, q):
                        for k in range(SLOT_K):
                            kt = SLOT_K * q + k
                            end = q == g.slots - 1 and k == SLOT_K - 1
                            for j in range(4):
                                out = ps[:, j]
                                first = q == 0 and k == 0 and (wide_ or j % 2 == 0)
                                w = slice(P * j, P * j + P)
                                pe.matmul(out, WHI[:, par, k, w], hi(kt), start=first, stop=False)
                                pe.matmul(out, WHI[:, par, k, w], lo(kt), start=False, stop=False)
                                last = pe.matmul(out, WLO[:, par, k, w], hi(kt), start=False,
                                                 stop=end and (wide_ or j % 2 == 1))
                        return last
                    return run
                return products

            def tokens_still(g, i, b):
                ps = wide(g.b0 + b)

                def run(par, q):
                    for k in range(SLOT_K):
                        kt = SLOT_K * q + k
                        end = q == g.slots - 1 and k == SLOT_K - 1
                        for j in range(4):
                            x = [h[:, j // 2, kt, P * (j % 2):P * (j % 2) + P] for h in (H1HI, H1LO)]
                            pe.matmul(ps[:, j], x[0], WHI[:, par, k], start=q == 0 and k == 0, stop=False)
                            pe.matmul(ps[:, j], x[1], WHI[:, par, k], start=False, stop=False)
                            last = pe.matmul(ps[:, j], x[0], WLO[:, par, k], start=False, stop=end)
                    return last
                return run

            def stats(n, wide_):
                for ch in range(4):
                    pe.wait_ge(sq_done, 4 * n + ch + 1)
                    for k in range(4):
                        rhs = SQW[:, ch, k] if wide_ else SQ[:, ch % 2, k]
                        out = bank(7).rearrange("p (s t) -> p s t", s=2) if wide_ else bank(7, T)
                        last = pe.matmul(out, ONES[:], rhs, start=ch == 0 and k == 0, stop=ch == 3 and k == 3)
                    last.then_inc(ss_done, 1)

            def mod(g, i, b):
                par_b = b % 2

                def run(par, q):
                    for k in range(SLOT_K):
                        kt = SLOT_K * q + k
                        out = PS[0:4, par_b * NB:par_b * NB + NB]
                        pe.matmul(out, C4[:, kt], WHI[:, par, k], start=q == 0 and k == 0, stop=False)
                        last = pe.matmul(out, C4[:, kt], WLO[:, par, k], start=False,
                                         stop=q == g.slots - 1 and k == SLOT_K - 1)
                    return last
                return run

            def mod_cols(g, i, b):
                wait_stage(pe, "free", g, i, b)
                for j in range(4):
                    at_ = 6 * NB + 8 * b + 2 * j + mult(i, 16)
                    last = pe.matmul(PS[:, bass.ds(at_, 2)], MROW[:, b % 2, P * j:P * j + P],
                                     CST[0:4, C_PAIR:C_PAIR + 2], start=True, stop=True)
                return last

            pe.wait_ge(sem("c_ready"), 2)
            pe.wait_ge(sem("const_in"), 16)
            pe.wait_ge(sem("ones"), 1)
            g = G["mod"]

            def mod_block(i, b):
                pe.wait_ge(stage_sem["free"], mult(i, 2) + (b + 1))
                for q in range(g.slots):
                    slot(g, i, b, q, mod(g, i, b))
            mod_block(0, 0)
            with pe.Fori(0, (g.blocks - 2) // 2) as i:
                mod_block(i, 1)
                mod_cols(g, i, 0)
                mod_block(i, 2)
                mod_cols(g, i, 1)
            stats(0, True)
            mod_block(0, g.blocks - 1)
            mod_cols(g, 0, g.blocks - 2)
            mod_cols(g, 0, g.blocks - 1).then_inc(sem("mod_cols"), 1)
            pe.wait_ge(hlo_ready, 8)
            pe.wait_ge(sem("wg_lo"), 1)
            for k in range(KT):
                out = PS[0:4 * HEADS, 6 * NB:7 * NB].rearrange("p (s t) -> p s t", s=2)
                pe.matmul(out, WGH[:, k], H1HI[:, :, k], start=k == 0, stop=False)
                pe.matmul(out, WGH[:, k], H1LO[:, :, k], start=False, stop=False)
                last = pe.matmul(out, WGL[:, k], H1HI[:, :, k], start=False, stop=k == KT - 1)
            last.then_inc(sem("gate_mm"), 1)
            all_free(pe, G["mod"])

            def gate_rows(c):
                if c == 0:
                    pe.wait_ge(sem("gates_copied"), 1)
                    for kind in range(4):
                        pick = ident[0:4 * HEADS, HEADS * kind:HEADS * kind + HEADS]
                        parts = ([(0, GALL[:, T:2 * T]), (T, GALL[:, 0:T])] if kind < 2 else [(0, GALL[:, ::-1])])
                        for at_, rhs in parts:
                            c0 = (4 + kind) * NB + at_
                            last = pe.matmul(PS[0:HEADS, c0:c0 + rhs.shape[1]], pick, rhs, start=True, stop=True)
                    last.then_inc(sem("grow_mm"), 1)
                if c == 1:
                    pe.wait_ge(sem("grow"), 1)
            blocks(G["mk"], weights_still(lambda k: H1HI[:, :, k], lambda k: H1LO[:, :, k], True), gate_rows)

            def gate_cols(c):
                if c == 1:
                    all_free(pe, G["mk"])
                    pe.wait_ge(sem("gate_emt"), 1)
                    for d in range(2):
                        for j in range(4):
                            at_ = 6 * NB + HEADS * (4 * d + j)
                            pe.matmul(PS[:, at_:at_ + HEADS], GROW[:, d, P * j:P * j + P], ident[0:HEADS, 0:HEADS],
                                      start=True, stop=True)
                        for u in range(TT):
                            at_ = 6 * NB + 64 + HEADS * (2 * d + u)
                            last = pe.matmul(PS[:, at_:at_ + HEADS], GROW[:, 2, T * d + P * u:T * d + P * u + P],
                                             ident[0:HEADS, 0:HEADS], start=True, stop=True)
                    last.then_inc(sem("a_cols"), 1)
                if c == 3:
                    pe.wait_ge(sem("a_copied"), 1)
            blocks(G["mv"], tokens_still, gate_cols)
            blocks(G["dk"], weights_still(lambda k: H1HI[:, :, k], lambda k: H1LO[:, :, k], True))
            blocks(G["dv"], tokens_still)

            def lat(x):
                return lambda k: x[:, 0, k]

            def half_wide(g, i, b):
                ps = wide(g.b0 + b)

                def run(par, q):
                    for k in range(SLOT_K):
                        kt = SLOT_K * q + k
                        end = q == g.slots - 1 and k == SLOT_K - 1
                        for j in range(4):
                            out, w = ps[:, j, 0:T], slice(P * j, P * j + P)
                            pe.matmul(out, WHI[:, par, k, w], H1HI[:, 0, kt], start=q == 0 and k == 0, stop=False)
                            pe.matmul(out, WHI[:, par, k, w], H1LO[:, 0, kt], start=False, stop=False)
                            last = pe.matmul(out, WLO[:, par, k, w], H1HI[:, 0, kt], start=False, stop=end)
                    return last
                return run
            mod_sums(MOD_REST // 2, G["mq"].base["free"] + 1)
            for name in ("mq", "dq", "mo"):
                blocks(G[name], half_wide)

            all_free(pe, G["mo"])
            wait_stage(pe, "d2", G["mq"], 0, 1)

            def m_scores(h):
                if h >= 2:
                    pe.wait_ge(sem("m_p"), 2 * (h - 1))
                for j in range(4):
                    at_ = (h % 2) * 1024 + T * j
                    last = pe.matmul(PS[:, at_:at_ + T], MK[:, h, j // 2, P * (j % 2):P * (j % 2) + P], MQ[:, h],
                                     start=True, stop=True)
                last.then_inc(sem("m_s"), 1)
                for d in range(2):
                    if h:
                        pe.wait_ge(sem("m_w"), 2 * (h - 1) + d + 1)
                    if h == 4:
                        pe.wait_ge(sem("mixm_done"), 1)
                    pe.matmul(bank(4 + d).rearrange("p (r t) -> p r t", r=2),
                              ident[0:HEADS, h:h + 1].broadcast_to([HEADS, P]),
                              NEGM[:, d].unsqueeze(1).broadcast_to([HEADS, 2, T]), start=True, stop=False)
                    mask = CST[:, C_MF + P * d:C_MF + P * d + P].unsqueeze(1).broadcast_to([P, 2, P])
                    pe.matmul(PS[:, (4 + d) * NB + T:(5 + d) * NB].rearrange("p (r t) -> p r t", r=2),
                              ident, mask, start=False, stop=True).then_inc(sem("m_bc"), 1)

            def m_values(h):
                for d in range(2):
                    pe.wait_ge(sem("m_p"), 2 * h + d + 1)
                    if h:
                        pe.wait_ge(sem("m_num"), 2 * (h - 1) + d + 1)
                    for u in range(TT):
                        keys = [2, 3] + [j for j in range(2) if (j <= u if d == 0 else j >= u)]
                        for j in keys:
                            at_ = (6 + d) * NB + 129 * u
                            last = pe.matmul(PS[:, at_:at_ + 129], MP[:, d, j, P * u:P * u + P], MV[:, j, h],
                                             start=j == keys[0], stop=j == keys[-1])
                    last.then_inc(sem("m_pv"), 1)

            def m_transposes(half):
                pe.wait_ge(sem("m_h"), half + 1)
                for hh in range(4):
                    for u in range(TT):
                        at_ = 4 * NB + T * hh + P * u
                        last = pe.transpose(PS[:, at_:at_ + P], MH[:, u, hh], ident)
                last.then_inc(sem("m_t"), 1)

            m_scores(0)
            for h in range(HEADS):
                if h % 4 != 3:
                    m_scores(h + 1)
                m_values(h)
                if h % 4 == 3:
                    m_transposes(h // 4)
                    if h == 3:
                        m_scores(h + 1)
            pe.wait_ge(sem("mixm_done"), 2)
            for r in range(8):
                v = DQ[:, 2 * r:2 * r + 2, :] if r < 4 else DK[:, 2 * (r - 4):2 * (r - 4) + 2, 0, :]
                if r >= 2:
                    pe.wait_ge(sem("roped"), r - 1)
                pe.matmul(bank(r % 2).rearrange("p (h t) -> p h t", h=2), CST[:, C_ROT:C_ROT + P], v,
                          start=True, stop=True).then_inc(sem("rot"), 1)
            pe.wait_ge(sem("roped"), 8)
            U = 2 * HEADS

            def d_scores(u):
                if u >= 2:
                    pe.wait_ge(sem("d_e"), u - 1)
                for c in range(2):
                    half_ = slice(64 * c, 64 * c + 64)
                    last = pe.matmul(bank(2 * (u % 2) + c).rearrange("p (s t) -> p s t", s=2),
                                     DQ[half_, u // 2, P * (u % 2):P * (u % 2) + P], DK[half_, u // 2],
                                     start=True, stop=True)
                last.then_inc(sem("d_s"), 1)

            def d_transposes(u):
                pe.wait_ge(sem("d_p"), u + 1)
                if u >= 2:
                    pe.wait_ge(sem("d_tc"), u - 1)
                for j in range(4):
                    at_ = (4 + u % 2) * NB + P * j
                    last = pe.transpose(PS[:, at_:at_ + P], DP[:, u % 2, P * j:P * j + P], ident)
                last.then_inc(sem("d_t"), 1)

            def d_values(u):
                pe.wait_ge(sem("d_tc"), u + 1)
                if u >= 2:
                    pe.wait_ge(sem("d_oc"), u - 1)
                for j in range(4):
                    last = pe.matmul(bank(6 + u % 2, P), DPT[:, u % 2, j], DV[:, j, u // 2], start=j == 0, stop=j == 3)
                last.then_inc(sem("d_o"), 1)

            for u in range(U + 3):
                if u < U:
                    d_scores(u)
                if 2 <= u < U + 2:
                    d_transposes(u - 2)
                if u >= 3:
                    d_values(u - 3)
            pe.wait_ge(sem("d_on"), 1)
            for h in range(HEADS):
                for u in range(TT):
                    at_ = T * h + P * u
                    last = pe.transpose(PS[:, at_:at_ + P], DO[:, u, h], ident)
            last.then_inc(sem("d_ot"), 1)

            here = weights_still(lambda k: HHI[:, k], lambda k: HLO[:, k], False)
            inner = weights_still(lambda k: AHI[:, k], lambda k: ALO[:, k], False)
            pe.wait_ge(hlo_ready, APPLY["mix"] + 4)
            blocks(G["wout"], here)
            stats(1, False)
            stats(2, False)
            pe.wait_ge(hlo_ready, APPLY["ffn"] + 4)
            for part in range(3):
                blocks(G[f"up{part}"], here)
                wait_stage(pe, "d3", G[f"up{part}"], 0, G[f"up{part}"].blocks - 1)
                blocks(G[f"down{part}"], inner)
            stats(3, False)
            stats(4, False)
            pe.wait_ge(hlo_ready, APPLY["mix2"] + 4)
            for name in ("in_u", "in_x", "in_y"):
                blocks(G[name], here)
            wait_stage(pe, "free", G["in_y"], 0, 2)
            pe.wait_ge(sem("s5w_in"), 32)

            def s5_in(s):
                a, kt = s % 4, s // 4
                if s >= 2:
                    pe.wait_ge(sem("s5_bu_read"), s - 1)
                rows = slice(32 * a, 32 * a + 32)
                for f in range(2):
                    at_ = (4 + s % 2) * NB + T * f
                    last = pe.matmul(PS[:, at_:at_ + T], S5B[rows, f, kt], U5[rows, kt], start=True, stop=True)
                last.then_inc(sem("s5_bu"), 1)

            s5_in(0)
            for s in range(ST_TILES):
                if s + 1 < ST_TILES:
                    s5_in(s + 1)
                a, kt = s % 4, s // 4
                pe.wait_ge(sem("s5_s"), s + 1)
                pe.wait_ge(sem("s5_c"), 1)
                if kt >= 2 and a == 0:
                    pe.wait_ge(sem("s5_yk"), kt - 1)
                for f in range(2):
                    last = pe.matmul(PS[32 * a:32 * a + 32, (6 + kt % 2) * NB:(6 + kt % 2) * NB + T],
                                     S5C[:, f, s], SST[:, s % 2, f], start=f == 0, stop=f == 1)
                last.then_inc(sem("s5_cy"), 1)
            pe.wait_ge(sem("s5_glo"), 1)
            blocks(G["glu"], weights_still(lambda k: GHI[:, k], lambda k: GLO[:, k], False))
            for t in range(LRU_TILES):
                pe.wait_ge(sem("lw_in"), 16 * (t // LH + 1))
                if t >= 2:
                    pe.wait_ge(sem("lru_ri"), t - 1)
                for v in range(2):
                    at_ = (4 + t % 2) * NB + T * v
                    last = pe.matmul(PS[:, at_:at_ + T], LW[:, v, t % LH], XC[:, t], start=True, stop=True)
                last.then_inc(sem("lru_mm"), 1)
            pe.wait_ge(hlo_ready, APPLY["lru"] + 4)

            def proj(g, i, b):
                ps = wide(g.b0 + b)

                def run(par, q):
                    for k in range(SLOT_K):
                        kt = SLOT_K * q + k
                        end = q == g.slots - 1 and k == SLOT_K - 1
                        for j in range(4):
                            out, w = ps[:, j, 0:T] if q == 0 else ps[:, j, T:2 * T], slice(P * j, P * j + P)
                            pe.matmul(out, WHI[:, par, k, w], AHI[:, kt], start=q == 0 and k == 0, stop=False)
                            pe.matmul(out, WHI[:, par, k, w], ALO[:, kt], start=False, stop=False)
                            last = pe.matmul(out, WLO[:, par, k, w], AHI[:, kt], start=False, stop=end)
                    return last
                return run

            for k in range(4):
                blocks(G[f"gates{k}"], here)
                wait_stage(pe, "free", G[f"gates{k}"], 0, 1)
                blocks(G[f"proj{k}"], proj)
                wait_stage(pe, "free", G[f"proj{k}"], 0, 0)
            pe.wait_ge(hlo_ready, APPLY["merged"] + 4)
            blocks(G["out2"], here)
            stats(5, False)
            pe.wait_ge(hlo_ready, APPLY["moe"] + 4)
            pe.wait_ge(sem("wr_lo"), 1)
            for k in range(KT):
                out = PS[0:36, 6 * NB:6 * NB + T]
                pe.matmul(out, WRH[:, k], HHI[:, k], start=k == 0, stop=False)
                pe.matmul(out, WRH[:, k], HLO[:, k], start=False, stop=False)
                last = pe.matmul(out, WRL[:, k], HHI[:, k], start=False, stop=k == KT - 1)
            last.then_inc(sem("r_mm"), 1)
            pe.wait_ge(sem("r_rows"), 1)
            for u in range(TT):
                last = pe.matmul(bank(7)[:, 36 * u:36 * u + 36], RLT[:, P * u:P * u + P], ident[0:36, 0:36],
                                 start=True, stop=True)
            last.then_inc(sem("r_cols"), 1)
            pe.wait_ge(sem("r_comb"), 1)
            wait_stage(pe, "free", G["out2"], 0, 3)
            for u in range(TT):
                last = pe.matmul(PS[0:EXPERTS, P * u:P * u + P], RS[:, 14, u], ident, start=True, stop=True)
            last.then_inc(sem("r_combT"), 1)
            pe.wait_ge(sem("combT"), 1)
            for q in range(8):
                if q >= 2:
                    pe.wait_ge(sem("cb"), q - 1)
                for j in range(4):
                    e = 4 * q + j
                    last = pe.matmul(narrow(q)[:, j], ident[0:EXPERTS, e:e + 1].broadcast_to([EXPERTS, P]), COMBT[:],
                                     start=True, stop=True)
                last.then_inc(sem("cb_mm"), 1)
            pe.wait_ge(sem("cb"), 8)
            for part in range(4):
                blocks(G[f"moe_up{part}"], here)
                wait_stage(pe, "d3", G[f"moe_up{part}"], 0, 7)
                blocks(G[f"moe_down{part}"], inner)
            stats(6, False)


def columns(v):
    return np.ascontiguousarray(np.asarray(v).reshape(-1, P).T)


def kernel(**inputs):
    import numpy as _np
    import concourse.bacc as _bacc
    from concourse import mybir as _mybir
    from concourse.bass_utils import run_bass_kernel_spmd as _run

    a = {k: _np.asarray(v) for k, v in inputs.items()}
    cols = {"c": columns(a["c"]), "c_ctx": columns(a["c_ctx"]), "b_mod": columns(a["b_mod"]),
            "norm_mix": columns(a["norm_mix_w_2"]), "norm_ffn": columns(a["norm_ffn_w_2"]),
            "norm_final": columns(a["norm_final_w_2"]), "g_mlstm": columns(a["g_mlstm"]),
            "g_diff": columns(a["g_diff"]), "b_gate2": columns(a["b_gate_2"]),
            "lam_re": columns(a["s5_lam_re_2"]), "lam_im": columns(a["s5_lam_im_2"]),
            "log_step": columns(_np.repeat(a["s5_log_step_2"], 64)),
            "s5_d": columns(a["s5_d_2"]), "b_glu": columns(a["s5_b_glu_2"]),
            "lru_b_a": columns(a["lru_b_a_2"]), "lru_b_x": columns(a["lru_b_x_2"]),
            "lru_lambda": columns(a["lru_lambda_2"]),
            "lru_conv_w": columns(a["lru_conv_w_2"]), "lru_conv_b": columns(a["lru_conv_b_2"])}
    for n in ("g_pre_mix", "g_post_mix", "g_pre_ffn", "g_post_ffn", "conv_qk_w", "conv_qk_b", "conv_ffn_w", "conv_ffn_b"):
        cols[n] = columns(a[n])

    def token_cols(x):
        return _np.ascontiguousarray(x.reshape(T, KT, P).transpose(2, 1, 0).reshape(P, KT * T))

    def rows(w):
        n = w.shape[1]
        return _np.ascontiguousarray(w.reshape(-1, P, n).transpose(1, 0, 2).reshape(P, -1))

    s5_b = _np.zeros((P, 2, 4, P), _np.float32)
    s5_c = _np.zeros((P, 2, ST_TILES, 32), _np.float32)
    for f, (b, c) in enumerate(((a["s5_b_re_2"][0], a["s5_c_re_2"][0]), (a["s5_b_im_2"][0], a["s5_c_im_2"][0]))):
        for g in range(32):
            tile, half = g // 2, g % 2
            at = 32 * (tile % 4) + 16 * half
            s5_b[at:at + 16, f, tile // 4, 64 * half:64 * half + 64] = b[g].T
            s5_c[64 * half:64 * half + 64, f, tile, 16 * half:16 * half + 16] = c[g].T
    lru_w = _np.stack([a["lru_w_a_2"][0], a["lru_w_x_2"][0]]).transpose(2, 0, 1, 3).reshape(P, -1)
    arrays = {
        "cols": _np.concatenate([cols[n] for n, _ in COLS], axis=1),
        "consts": shape_constants(),
        "xT": token_cols(a["x"][0]), "ctxT": token_cols(a["ctx"][0]),
        "lamv": _np.tile(_np.concatenate([a[n].ravel() for n in ("lambda_q1", "lambda_k1", "lambda_q2", "lambda_k2")]), (P, 1)),
        "b_gateT": a["b_gate"][0].T,
        "b_router": _np.tile(_np.concatenate([a["b_router_group_2"][0], a["b_router_expert_2"][0]]), (P, 1)),
        "w_gates": rows(a["w_in"][0][:, 4096:4128]),
        "w_router": rows(_np.concatenate([a["w_router_group_2"][0], a["w_router_expert_2"][0]], axis=1)),
        "s5_b": s5_b.reshape(P, -1), "s5_c": s5_c.reshape(P, -1), "lru_w": lru_w,
        "w_mod": a["w_mod"][0], "w_in": a["w_in"][0], "w_out": a["w_out"][0], "w_up": a["w_up"][0],
        "w_down": a["w_down"][0], "w_in_2": a["w_in_2"][0], "s5_w_glu_2": a["s5_w_glu_2"][0],
        "w_proj_s5_2": a["w_proj_s5_2"][0], "w_proj_lru_2": a["w_proj_lru_2"][0], "w_out_2": a["w_out_2"][0],
        "w_e_gate_2": a["w_e_gate_2"][0].reshape(EXPERTS * D, E_FF),
        "w_e_up_2": a["w_e_up_2"][0].reshape(EXPERTS * D, E_FF),
        "w_e_down_2": a["w_e_down_2"][0].reshape(EXPERTS * E_FF, D),
    }
    arrays = {n: _np.ascontiguousarray(v) for n, v in arrays.items()}
    nc = _bacc.Bacc("TRN2", target_bir_lowering=False, num_devices=1)
    aps = {n: nc.dram_tensor("in_" + n, v.shape, _mybir.dt.from_np(v.dtype), kind="ExternalInput").ap()
           for n, v in arrays.items()}
    aps["out"] = nc.dram_tensor("out_T", (P, KT * T), _mybir.dt.float32, kind="ExternalOutput").ap()
    program(nc, aps)
    r = _run(nc, [{"in_" + n: v for n, v in arrays.items()}], core_ids=[0])
    out = r.results[0]["out_T"]
    return _np.ascontiguousarray(out.reshape(P, KT, T).transpose(2, 1, 0).reshape(1, T, D))
```

```python
import math
from contextlib import ExitStack

import numpy as np

import concourse.bass as bass
from concourse import mybir

F32 = mybir.dt.float32
F32R = mybir.dt.float32r
ALU = mybir.AluOpType
ACT = mybir.ActivationFunctionType
AX = mybir.AxisListType

P = 128
D = 2048
KT = D // P
T = 256
TT = T // P
NB = 512
EPS = 1e-6
HEADS = 8
D_FF = 5632
FT = D_FF // P
S5_TILES = 4
ST_TILES = 16
LRU_TILES = 12
EXPERTS = 32
EXPERT_GROUPS = 4
E_FF = 256
GELU_C = math.sqrt(2.0 / math.pi)
BIG = 1.0e30
RING = 4
SLOT_K = 4

COLS = [("c", 16), ("c_ctx", 16), ("g_pre_mix", 16), ("g_post_mix", 16), ("g_pre_ffn", 16),
        ("g_post_ffn", 16), ("norm_mix", 16), ("norm_ffn", 16), ("norm_final", 16), ("b_mod", 96),
        ("conv_qk_w", 48), ("conv_qk_b", 16), ("g_mlstm", 8), ("g_diff", 1),
        ("conv_ffn_w", 3 * 2 * FT), ("conv_ffn_b", 2 * FT), ("b_gate2", 32),
        ("lam_re", ST_TILES), ("lam_im", ST_TILES), ("log_step", ST_TILES), ("s5_d", 4), ("b_glu", 4),
        ("lru_conv_w", 48), ("lru_conv_b", 12), ("lru_b_a", 12), ("lru_b_x", 12), ("lru_lambda", 12)]
COL_AT = {}
_at = 0
for _name, _n in COLS:
    COL_AT[_name] = (_at, _n)
    _at += _n
N_COLS = _at

C_ID, C_REV, C_MF, C_MB, C_ROT, C_PAIR, C_IOTA, C_COS, C_SIN = 0, 128, 256, 384, 512, 640, 642, 658, 914
N_CONST, N_CONST_ALL = 658, 1170


def shape_constants():
    cst = np.zeros((P, N_CONST_ALL), np.float32)
    cst[:, C_ID:C_ID + P] = np.eye(P)
    cst[:, C_REV:C_REV + P] = np.eye(P)[:, ::-1]
    s, t = np.arange(P)[:, None], np.arange(P)[None, :]
    cst[:, C_MF:C_MF + P] = np.where(s <= t, 0.0, -BIG)
    cst[:, C_MB:C_MB + P] = np.where(s >= t, 0.0, -BIG)
    for m in range(P):
        if (m % 32) < 16:
            cst[m + 16, C_ROT + m] = -1.0
        else:
            cst[m - 16, C_ROT + m] = 1.0
    inv = (np.float32(10000.0) ** (-np.arange(16, dtype=np.float32) / np.float32(16))).astype(np.float32)
    tok = np.arange(T)
    pos = np.stack([tok // 64, tok % 64]).astype(np.float32)
    for m in range(P):
        i = m % 64
        ang = pos[i // 32] * inv[i % 16]
        cst[m, C_COS:C_COS + T] = np.cos(ang)
        cst[m, C_SIN:C_SIN + T] = np.sin(ang)
    cst[0:2, C_PAIR] = 1.0
    cst[2:4, C_PAIR + 1] = 1.0
    cst[:, C_IOTA:C_IOTA + 16] = np.arange(16)
    return cst


MOD_FIRST = 8
MOD_REST = 6 * D // NB - MOD_FIRST


class Gemm:

    def __init__(self, name, blocks, slots, dmas=1, stages=("free",), extra=0):
        self.name, self.blocks, self.slots, self.dmas, self.stages = name, blocks, slots, dmas, stages
        self.extra = extra


CONV = ("a1", "free", "a2", "d2")
GEMMS = [Gemm("mod", MOD_FIRST, 4),
         Gemm("mk", 2, 4, 1, CONV, 2), Gemm("mv", 2, 4, extra=2), Gemm("dk", 2, 4, extra=2), Gemm("dv", 2, 4, extra=2),
         Gemm("mq", 2, 4, 1, CONV), Gemm("dq", 2, 4), Gemm("mo", 2, 4),
         Gemm("wout", 4, 4)]
FFN_PARTS = [(0, 8), (8, 8), (16, 6)]
UP = ("a1", "free", "a2", "d2", "a3", "d3")
for _i, (_f, _n) in enumerate(FFN_PARTS):
    GEMMS += [Gemm(f"up{_i}", _n, 4, 2, UP), Gemm(f"down{_i}", 4, _n // 2)]
GEMMS += [Gemm("in_u", 1, 4), Gemm("in_x", 3, 4, 1, ("a1", "free")),
          Gemm("in_y", 3, 4, 1, ("a1", "d1", "a2", "free")),
          Gemm("gates0", 2, 4), Gemm("glu", 1, 1)]
for _i in (1, 2, 3):
    GEMMS += [Gemm(f"gates{_i}", 2, 4), Gemm(f"proj{_i - 1}", 1, 4, 1, ("free", "d2"))]
GEMMS += [Gemm("proj3", 1, 4, 1, ("free", "d2"))]
GEMMS += [Gemm("out2", 4, 4)]
MOE = ("a2", "free", "d2", "a3", "d3")
FIRST_EXPERTS = 2
GEMMS += [Gemm("moe_first", FIRST_EXPERTS, 4, 2, ("a2", "free")), Gemm("moe_up0", 8 - FIRST_EXPERTS, 4, 2, MOE),
          Gemm("moe_down0", 4, 4)]
for _i in (1, 2, 3):
    GEMMS += [Gemm(f"moe_up{_i}", 8, 4, 2, MOE), Gemm(f"moe_down{_i}", 4, 4)]
G = {g.name: g for g in GEMMS}
_slot, _split, _block, _ring, _stage, RING_AT = 0, 0, 0, [0] * RING, {}, []
for _g in GEMMS:
    _g.s0, _g.m0, _g.b0, _g.base = _slot, _split, _block, dict(_stage)
    for _s in range(_g.blocks * _g.slots * (1 + _g.extra)):
        _r = len(RING_AT) % RING
        _ring[_r] += 16 * _g.dmas
        RING_AT.append(_ring[_r])
    for _s in _g.stages:
        _stage[_s] = _stage.get(_s, 0) + _g.blocks
    _slot = len(RING_AT)
    _split += _g.blocks * _g.slots
    _block += _g.blocks
for _g, _next in zip(GEMMS, GEMMS[1:] + [None]):
    _g.next = _next
KB = 1024
TWO_PI = 6.2831845
APPLY = {"h1": 0, "mix": 8, "ffn": 12, "mix2": 16, "lru": 20, "merged": 24, "moe": 28}
TMPS = {"ffn": 0, "mix2": 4, "moe": 8}


class Steps:

    def __init__(self, eng, sem):
        self.eng, self.sem, self.n, self.dyn = eng, sem, 0, 0

    def __call__(self, ins):
        ins.then_inc(self.sem, 1)
        self.n += 1
        self.eng.wait_ge(self.sem, self.dyn + self.n)


def program(nc, A):
    ctx = ExitStack()
    base = (nc.sbuf_base + 63) // 64 * 64

    def at(name, shape, off, dt=F32):
        return nc.alloc_sbuf_tensor_at(name, shape, dt, offset=base + off)

    sem_of = {}

    def sem(name):
        if name not in sem_of:
            sem_of[name] = ctx.enter_context(nc.semaphore(name))
        return sem_of[name]

    with ctx:
        RAW = at("w_raw", [P, RING, SLOT_K, NB], 0)
        WHI = at("w_hi", [P, 2, SLOT_K, NB], 32 * KB, F32R)
        WLO = at("w_lo", [P, 2, SLOT_K, NB], 48 * KB, F32R)
        A0, B0 = 64 * KB, 128 * KB
        H1HI = at("h1_hi", [P, 2, KT, T], A0, F32R)
        H1LO = at("h1_lo", [P, 2, KT, T], A0 + 32 * KB, F32R)
        MQ = at("m_q", [P, HEADS, T], A0 + 16 * KB)
        DQ = at("d_q", [P, HEADS, T], A0 + 24 * KB)
        MO = at("m_o", [P, HEADS, T], A0 + 48 * KB)
        QTH = at("q_tanh", [P, 4, T], A0 + 56 * KB)
        MIX = at("mixed", [P, KT, T], A0 + 32 * KB)
        MW = at("m_weights", [P, 2, 4, T], A0)
        MP = at("m_probs", [P, 2, 4, T], A0 + 8 * KB)
        MH = at("m_h", [P, TT, 4, P], A0 + 40 * KB)
        MSQ = at("m_hsq", [P, TT, 4, P], A0 + 44 * KB)
        NUM = at("m_num", [P, 2, TT, 4, P], A0 + 56 * KB)
        DE = at("d_exp", [P, 2, 2, NB], A0)
        DPT = at("d_probsT", [P, 2, 4, P], A0 + 8 * KB)
        DP = at("d_probs", [P, 2, NB], A0 + 12 * KB)
        DO = at("d_out", [P, TT, HEADS, P], A0 + 16 * KB)
        DSQ = at("d_osq", [P, TT, HEADS, P], A0)
        RT1 = at("rope_1", [P, 2, T], A0 + 56 * KB)
        RT2 = at("rope_2", [P, 2, T], A0 + 58 * KB)
        HHI = at("h_hi", [P, KT, T], A0, F32R)
        HLO = at("h_lo", [P, KT, T], A0 + 16 * KB, F32R)
        AHI = at("act_hi", [P, KT, T], A0 + 32 * KB, F32R)
        ALO = at("act_lo", [P, KT, T], A0 + 48 * KB, F32R)
        XIN = at("x_in", [P, 2, KT, T], B0)
        SQW = at("squares_wide", [P, KT, 2, T], A0)
        TMPW = at("h_tmp_wide", [P, 2, 4, T], B0 + 48 * KB)
        MROW = at("mod_rows", [4, 2, NB], B0 + 56 * KB)
        C4 = at("c_pair", [P, KT, 4], B0 + 60 * KB, F32R)
        C4F = at("c_silu", [P, 4, KT], B0 + 60 * KB + 256)
        RBW = at("rstd_wide", [P, 2, T], B0 + 60 * KB + 512)
        LAMV = at("lambdas", [P, 4, 64], B0 + 62 * KB + 512)
        LAMP = at("lambda_products", [P, 2, 64], B0 + 63 * KB + 512)
        MK = at("m_k", [P, HEADS, 2, T], B0)
        MV = at("m_v", [P, 4, HEADS, 129], B0 + 16 * KB)
        DK = at("d_k", [P, HEADS, 2, T], B0 + 16 * KB + 16512)
        DV = at("d_v", [P, 4, HEADS, P], B0 + 32 * KB + 16512)
        KTH = at("k_tanh", [P, 4, 2, T], B0 + 32 * KB + 16512)
        GALL = at("gates_all", [4 * HEADS, 2 * T], B0 + 16 * KB)
        GROW = at("gates_rows", [HEADS, 4, 2 * T], B0 + 18 * KB)
        GS = at("gates_scan", [HEADS, 3, 2, 2 * T], B0 + 26 * KB)
        WG = at("w_gates", [P, KT, 32], B0 + 38 * KB)
        WGH = at("w_gates_hi", [P, KT, 32], B0 + 40 * KB, F32R)
        WGL = at("w_gates_lo", [P, KT, 32], B0 + 42 * KB, F32R)
        X = at("x_res", [P, KT, T], B0)
        Y = at("y_sub", [P, KT, T], B0 + 16 * KB)
        SQ = at("squares", [P, 2, 4, T], B0 + 48 * KB)
        TMP = at("h_tmp", [P, 2, 4, T], B0 + 56 * KB)
        UC = at("up_conv", [P, 2, 4, T], B0 + 32 * KB)
        UTH = at("up_tanh", [P, 2, 2, T], B0 + 40 * KB)
        UACT = at("up_act", [P, 2, 2, T], B0 + 44 * KB)
        U5 = at("s5_u", [P, S5_TILES, T], B0 + 16 * KB)
        XC = at("lru_x", [P, LRU_TILES, T], B0 + 20 * KB)
        YSQ = at("lru_ysq", [P, 4, T], B0 + 48 * KB)
        S5B = at("s5_b", [P, 2, 4, P], B0 + 52 * KB)
        S5C = at("s5_c", [P, 2, ST_TILES, 32], B0 + 56 * KB)
        S5S = at("s5_small", [P, 20, ST_TILES], B0 + 60 * KB)
        SM3 = at("s5_m3", [P, 2, T], B0 + 61 * KB + 512)
        ET = at("s5_et", [P, 4, T], B0 + 44 * KB)
        ECS = at("s5_phase", [P, 2, 2, 4, T], A0 + 32 * KB)
        EX = at("s5_angle", [P, 2, 2, 16, 16], A0 + 40 * KB)
        EXR = at("s5_round", [P, 2, 2, 16, 16], A0 + 44 * KB)
        ESC = at("s5_sincos", [P, 2, 2, 16, 16], A0 + 48 * KB)
        SM1 = at("s5_m1", [P, 2, T], A0 + 52 * KB)
        SM2 = at("s5_m2", [P, 2, T], A0 + 54 * KB)
        SZ = at("s5_z", [P, 2, 2, T], A0 + 56 * KB)
        SST = at("s5_states", [P, 2, 2, T], A0 + 60 * KB)
        OUT5 = at("out_lru_s5", [P, KT, T], B0 + 32 * KB)
        YG = OUT5[:, 0:LRU_TILES]
        Y5 = OUT5[:, LRU_TILES:KT]
        Y5B = at("s5_yb", [P, S5_TILES, T], B0 + 52 * KB)
        GHI = at("glu_hi", [P, S5_TILES, T], A0 + 56 * KB, F32R)
        GLO = at("glu_lo", [P, S5_TILES, T], A0 + 60 * KB, F32R)
        LH = 4
        LW = at("lru_w", [P, 2, 2, LH, P], A0 + 32 * KB)
        LR = at("lru_r", [P, LH, T], A0 + 40 * KB)
        LI = at("lru_i", [P, LH, T], A0 + 44 * KB)
        LA = at("lru_a", [P, LH, T], A0 + 48 * KB)
        LT = at("lru_t", [P, LH, T], A0 + 52 * KB)
        GT = [[at("gate_e0", [P, 4, T], B0 + 48 * KB), at("gate_e1", [P, 4, T], B0 + 56 * KB)],
              [at("gate_o0", [P, 4, T], B0 + 16 * KB), at("gate_o1", [P, 4, T], B0 + 20 * KB)]]
        PM = at("proj_m", [P, 2, 4, T], B0 + 24 * KB)
        MG = at("merged", [P, KT, T], B0 + 32 * KB)
        CB = at("combine_b", [P, EXPERTS, T], B0 + 16 * KB)
        WR = at("w_router", [P, KT, 36], B0 + 16 * KB)
        WRH = at("w_router_hi", [P, KT, 36], B0 + 19 * KB, F32R)
        WRL = at("w_router_lo", [P, KT, 36], B0 + 22 * KB, F32R)
        RLT = at("router_rows", [36, T], B0 + 62 * KB)
        RS = at("router_small", [P, 16, TT, EXPERTS], B0 + 25 * KB)
        COMBT = at("combine_T", [EXPERTS, T], B0 + 60 * KB)
        MTH = at("moe_tanh", [P, 2, T], B0 + 48 * KB)
        MS1 = at("moe_s1", [P, 2, T], B0 + 50 * KB)
        MS2 = at("moe_s2", [P, 2, T], B0 + 52 * KB)
        MF = at("moe_first", [P, FIRST_EXPERTS, 2, T], B0 + 56 * KB)
        MACT = at("moe_act", [P, 2, T], B0 + 54 * KB)
        OUTB = at("out_sb", [P, KT, T], A0)
        small_at = B0 + 66048

        def small(name, shape, dt=F32):
            nonlocal small_at
            t = at(name, shape, small_at, dt)
            small_at += (4 * int(np.prod(shape[1:])) + 31) // 32 * 32
            assert small_at + base <= nc.sbuf_usable_end
            return t

        CST = small("consts", [P, N_CONST])
        COL = small("cols", [P, N_COLS])
        MODC = small("mod_cols", [P, 96, 2])
        MACC = small("mod_sums", [P, 2, NB])
        RB = at("rstd_b", [P, 2, T], small_at - 4 * KB)
        ROPE = at("rope_tables", [P, 2, T], small_at - 2 * KB)
        CS = small("c_column", [P, KT])
        ONES = small("ones", [P, P])
        SCALES = small("norm_scales", [P, 6, KT])
        LAM = small("lam_small", [P, 8])
        BG = small("b_gates", [HEADS, 4])
        NEGM = small("neg_max", [HEADS, 2, T])
        ACOL = small("a_cols", [P, 2, 4, HEADS])
        EMT = small("exp_neg_max", [P, 2, TT, HEADS])
        HALF = small("half_biases", [P, 72])
        RBIAS = small("router_bias", [P, 36])
        STAT = small("row_stats", [P, 48])
        PS = ctx.enter_context(nc.psum_tensor("acc", [P, 8 * NB], F32))
        block = ctx.enter_context(nc.Block())

        def col(name, i=0, n=1):
            return COL[:, COL_AT[name][0] + i:COL_AT[name][0] + i + n]

        ring_in = [sem(f"ring_in{r}") for r in range(RING)]
        hi_done = sem("hi_done")
        lo_done = sem("lo_done")
        slot_used = sem("slot_used")
        stage_sem = {s: sem("blk_" + s) for s in ("free", "a1", "d1", "a2", "d2", "a3", "d3")}
        dve_st = Steps(None, sem("dve_step"))

        def mult(i, n):
            return i * n if not isinstance(i, int) or i else 0

        def wait_slot(eng, s, g, i, c, more):
            eng.wait_ge(s, mult(i, 2 * g.slots) + (g.m0 + c + 1 + more))

        def wait_place(eng, g, i, c, more, e=0):
            eng.wait_ge(lo_done, mult(i, 2 * g.slots) + (g.s0 + c * (1 + g.extra) + e + 1 + more))

        def wait_block(eng, g, i, b):
            eng.wait_ge(slot_used, mult(i, 2 * g.slots) + (g.m0 + (b + 1) * g.slots + 2))

        def wait_stage(eng, st, g, i, b):
            eng.wait_ge(stage_sem[st], mult(i, 2) + (g.base.get(st, 0) + b + 1 + (2 if st == "free" else 0)))

        def all_free(eng, g):
            wait_stage(eng, "free", g, 0, g.blocks - 1)

        def to_hi(act, g, i, c):
            at_ = g.s0 + c * (1 + g.extra)
            r, par = at_ % RING, (g.m0 + c) % 2
            act.wait_ge(ring_in[r], mult(i, 16 * g.dmas * (2 * g.slots // RING)) + RING_AT[at_])
            wait_slot(act, slot_used, g, i, c, 0)
            act.activation(WHI[:, par], RAW[:, r], ACT.Copy).then_inc(hi_done, 1)

        def to_lo(dve, g, i, c):
            r, par = (g.s0 + c * (1 + g.extra)) % RING, (g.m0 + c) % 2
            if g.extra and c:
                mod_sum(dve, g, c - 1)
            elif g.name == "mq" and c == 0:
                mod_sum(dve, G["dv"], G["dv"].blocks * G["dv"].slots - 1)
            elif g.extra and g.name != "mk":
                mod_sum(dve, GEMMS[GEMMS.index(g) - 1], GEMMS[GEMMS.index(g) - 1].blocks * g.slots - 1)
            wait_slot(dve, hi_done, g, i, c, 0)
            dve.tensor_tensor(WLO[:, par], RAW[:, r], WHI[:, par].bitcast(F32), ALU.subtract)\
               .then_inc(lo_done, 1)
            if g.extra and c % g.slots == g.slots - 1:
                mod_sums_out(dve, (g.m0 - G["mk"].m0 + c) // g.slots)

        def mod_place(g, c, e):
            n = (g.m0 - G["mk"].m0 + c) * g.extra + e
            return n // 4, n % 4

        def mod_sums_out(dve, w):
            c0, c1 = 4 * max(2 * w - 1, 0), 4 * min(2 * w + 1, MOD_REST)
            dve.wait_ge(sem("mod_sums_read"), w + 1)
            at_ = mod_sums_at(w) + c0 - 4 * (2 * w - 1)
            dve.tensor_tensor(MODC[:, 4 * MOD_FIRST + c0:4 * MOD_FIRST + c1, 0], PS[:, at_:at_ + c1 - c0],
                              col("b_mod", 4 * MOD_FIRST + c0, c1 - c0), ALU.add).then_inc(sem("mod_rest"), 1)

        def mod_sums_at(w):
            return (G["mk"].b0 + min(w + 1, MOD_REST // 2)) % 2 * 4 * NB

        def mod_sum(dve, g, c):
            for e in range(g.extra):
                mb, q = mod_place(g, c, e)
                at_ = g.s0 + c * (1 + g.extra) + 1 + e
                acc = MACC[:, mb % 2]
                dve.wait_ge(ring_in[at_ % RING], RING_AT[at_])
                if q == 0 and mb >= 2:
                    dve.wait_ge(sem("mod_sums_read"), (mb + 1) // 2)
                for k in range(SLOT_K):
                    w, s = RAW[:, at_ % RING, k], CS[:, SLOT_K * q + k:SLOT_K * q + k + 1]
                    if q == 0 and k == 0:
                        ins = dve.tensor_scalar(acc, w, s, None, ALU.mult)
                    else:
                        ins = dve.scalar_tensor_tensor(acc, w, s, acc, ALU.mult, ALU.add)
                    if k < SLOT_K - 1:
                        dve_st(ins)
                ins.then_inc(lo_done, 1)
                dve.wait_ge(lo_done, at_ + 1 + RING)

        def ahead(g):
            return min(2, g.blocks * g.slots)

        def feed(eng, conv, g, stages, steps=None, per=0, beside=None, pre=2, last=None):
            n, s = g.blocks, g.slots

            def work(i, b, prev):
                todo = list(stages)
                for q in range(s):
                    if b > 0 or q >= ahead(g):
                        conv(eng, g, i, b * s + q)
                    if beside and (n <= 4 or b == n - 1):
                        beside(b * s + q)
                    if q >= 1 and prev is not None and todo:
                        todo.pop(0)(g, i, prev)
                while prev is not None and todo:
                    todo.pop(0)(g, i, prev)

            work(0, 0, None)
            if n <= 4:
                for b in range(1, n):
                    work(0, b, b - 1)
            else:
                n0 = steps.n if steps else 0
                with eng.Fori(0, (n - 2) // 2) as i:
                    if steps:
                        steps.dyn = i * (2 * per)
                    work(i, 1, 0)
                    work(i, 2, 1)
                if steps:
                    assert steps.n == n0 + 2 * per, (g.name, steps.n - n0)
                    steps.dyn, steps.n = 0, n0 + per * (n - 2)
                work(0, n - 1, n - 2)
            if g.next:
                for c in range(min(ahead(g.next), pre)):
                    conv(eng, g.next, 0, c)
            for f in stages[:last]:
                f(g, 0, n - 1)

        def last_stages(c, g, stages):
            if c == 2:
                for f in stages[1:]:
                    f(g, 0, g.blocks - 1)

        def narrow(b, half=0):
            par = b % 2 + half
            return PS[:, par * 1024:par * 1024 + 1024].rearrange("p (j t) -> p j t", j=4)

        def wide(b):
            par = b % 2
            return PS[:, par * 2048:par * 2048 + 2048].rearrange("p (j t) -> p j t", j=4)

        def proj_bank(k):
            at_ = 0 if k == 3 else 4 * NB
            return PS[:, at_:at_ + 4 * NB].rearrange("p (j t) -> p j t", j=4)

        def m_transposed(half):
            return (4 if half else 2) * NB

        def bank(n, m=NB):
            return PS[:, n * NB:n * NB + m]

        sq_done, ss_done, rec_done, rb_done = sem("sq_done"), sem("ss_done"), sem("rec_done"), sem("rb_done")
        tmp_ready, hhi_ready, hlo_ready = sem("tmp_ready"), sem("hhi_ready"), sem("hlo_ready")
        x_new = sem("x_new")

        @block.sync
        def _(sp):
            def src(g):
                name = g.name
                if name == "mod":
                    return lambda b, q: [(0, NB, A["w_mod"], q, b * NB)]
                w_in = {"mk": 1024, "mv": 2048, "dk": 4096 + 32 + 1024, "dv": 4096 + 32 + 2048,
                        "mq": 0, "dq": 4096 + 32, "mo": 3072}
                if name in w_in:
                    return lambda b, q: [(0, NB, A["w_in"], q, w_in[name] + b * NB)]
                if name == "wout":
                    return lambda b, q: [(0, NB, A["w_out"], q, b * NB)]
                if name[:2] == "up":
                    f0 = FFN_PARTS[int(name[2])][0]
                    return lambda b, q: [(0, 256, A["w_up"], q, (b + f0) * 256),
                                         (256, 256, A["w_up"], q, (b + f0) * 256 + D_FF)]
                if name[:4] == "down":
                    f0 = FFN_PARTS[int(name[4])][0]
                    return lambda b, q: [(0, NB, A["w_down"], q + f0 // 2, b * NB)]
                off = {"in_u": 0, "in_x": NB, "in_y": 4 * NB}
                if name in off:
                    return lambda b, q: [(0, NB, A["w_in_2"], q, off[name] + b * NB)]
                if name == "glu":
                    return lambda b, q: [(0, NB, A["s5_w_glu_2"], 0, 0)]
                if name[:5] == "gates":
                    k = int(name[5])
                    return lambda b, q: [(0, NB, A["w_in_2"], q, (7 + 4 * b + k) * NB)]
                if name[:4] == "proj":
                    k = int(name[4])
                    return lambda b, q: [(0, NB, A["w_proj_s5_2"], 0, k * NB) if q == 0 else
                                         (0, NB, A["w_proj_lru_2"], q - 1, k * NB)]
                if name == "out2":
                    return lambda b, q: [(0, NB, A["w_out_2"], q, b * NB)]
                if name[:6] == "moe_up" or name == "moe_first":
                    e0 = 0 if name == "moe_first" else 8 * int(name[6]) or FIRST_EXPERTS
                    return lambda b, q: [(0, 256, A["w_e_gate_2"], (b + e0) * 4 + q, 0),
                                         (256, 256, A["w_e_up_2"], (b + e0) * 4 + q, 0)]
                e0 = 8 * int(name[8])
                return lambda b, q: [(0, NB, A["w_e_down_2"], q + e0 // 2, b * NB)]

            def load(g, i, b, q, f):
                c = b * g.slots + q
                r = (g.s0 + c * (1 + g.extra)) % RING
                wait_place(sp, g, i, c, 0)
                for at0, n, w, row, c0 in f(mult(i, 2) + b, q):
                    v = w.rearrange("(q k p) n -> p q k n", p=P, k=SLOT_K)
                    if not isinstance(row, int):
                        sp.dma_start(RAW[:, r, :, at0:at0 + n], v[:, bass.ds(row, 1), :, c0:c0 + n]
                                     .rearrange("p q k n -> p (q k) n")).then_inc(ring_in[r], 16)
                    else:
                        sp.dma_start(RAW[:, r, :, at0:at0 + n],
                                     v[:, row, :, bass.ds(c0, n)]).then_inc(ring_in[r], 16)

            for g in GEMMS:
                f = src(g)
                if g.blocks >= 4 and 2 * g.slots % RING == 0:
                    with sp.Fori(0, g.blocks // 2) as i:
                        for b in range(2):
                            for q in range(g.slots):
                                load(g, i, b, q, f)
                else:
                    for b in range(g.blocks):
                        for q in range(g.slots):
                            load(g, 0, b, q, f)
                            for e in range(g.extra):
                                mb, mq = mod_place(g, b * g.slots + q, e)
                                place = g.s0 + (b * g.slots + q) * (1 + g.extra) + 1 + e
                                wait_place(sp, g, 0, b * g.slots + q, 0, 1 + e)
                                sp.dma_start(RAW[:, place % RING],
                                             A["w_mod"].rearrange("(q k p) n -> p q k n", p=P, k=SLOT_K)
                                             [:, mq, :, (MOD_FIRST + mb) * NB:(MOD_FIRST + mb + 1) * NB])\
                                  .then_inc(ring_in[place % RING], 16)
            for ch in range(4):
                sp.wait_ge(sem("out_ready"), ch + 1)
                sp.dma_start(A["out"].rearrange("p (k t) -> p k t", k=KT)[:, 4 * ch:4 * ch + 4],
                             OUTB[:, 4 * ch:4 * ch + 4]).then_inc(sem("stored"), 16)
            sp.wait_ge(sem("stored"), 64)

        @block.gpsimd
        def _(pool):
            pool.dma_start(COL[:], A["cols"]).then_inc(sem("cols_in"), 16)
            pool.dma_start(CST[:], A["consts"][:, 0:N_CONST]).then_inc(sem("const_in"), 16)
            pool.dma_start(LAMV[:], A["lamv"].rearrange("p (k n) -> p k n", k=4)).then_inc(sem("lam_in"), 16)
            pool.dma_start(BG[:], A["b_gateT"]).then_inc(sem("bg_in"), 16)
            pool.dma_start(RBIAS[:], A["b_router"]).then_inc(sem("rbias_in"), 16)
            pool.dma_start(WG[:], A["w_gates"].rearrange("p (k n) -> p k n", k=KT)).then_inc(sem("wg_in"), 16)
            pool.dma_start(XIN[:, 0], A["xT"].rearrange("p (k t) -> p k t", k=KT)).then_inc(sem("x_in"), 16)
            pool.dma_start(XIN[:, 1], A["ctxT"].rearrange("p (k t) -> p k t", k=KT)).then_inc(sem("x_in"), 16)
            pool.wait_ge(sem("x_in"), 32)
            for ch in range(4):
                x = XIN[:, :, 4 * ch:4 * ch + 4, :]
                pool.tensor_tensor(SQW[:, 4 * ch:4 * ch + 4].rearrange("p k s t -> p s k t"), x, x, ALU.mult)\
                    .then_inc(sq_done, 1)
            pool.wait_ge(rb_done, 1)
            pool.wait_ge(sq_done, 4)
            pool.tensor_tensor(XIN[:, 1], XIN[:, 1], RBW[:, 1].unsqueeze(1).broadcast_to([P, KT, T]), ALU.mult)\
                .then_inc(sem("ctx_normed"), 1)
            pool.wait_ge(sem("mod_sums_read"), MOD_REST // 2 + 1)
            pool.dma_start(ROPE[:], A["consts"][:, C_COS:C_SIN + T].rearrange("p (v t) -> p v t", v=2))\
                .then_inc(sem("rope_in"), 16)
            pool.wait_ge(sem("mixd_done"), 1)
            pool.dma_start(X[:], A["xT"].rearrange("p (k t) -> p k t", k=KT)).then_inc(sem("x2_in"), 16)
            pool.wait_ge(hlo_ready, APPLY["mix2"] + 4)
            pool.dma_start(S5B[:], A["s5_b"].rearrange("p (v k n) -> p v k n", v=2, k=4)).then_inc(sem("s5w_in"), 16)
            pool.dma_start(S5C[:], A["s5_c"].rearrange("p (v k n) -> p v k n", v=2, k=ST_TILES))\
                .then_inc(sem("s5w_in"), 16)
            lw = A["lru_w"].rearrange("p (v k n) -> p v k n", v=2, k=LRU_TILES)

            def sines(kt):
                if kt == 0:
                    pool.wait_ge(sem("s5_esc"), 1)
                for a2 in range(2):
                    e = ECS[:, kt % 2, 1, 2 * a2:2 * a2 + 2]
                    k2 = slice(4 * kt + 2 * a2, 4 * kt + 2 * a2 + 2)
                    fine = [ESC[:, f, 0, k2].unsqueeze(2).broadcast_to([P, 2, 16, 16]) for f in range(2)]
                    coarse = [ESC[:, f, 1, k2].unsqueeze(3).broadcast_to([P, 2, 16, 16]) for f in range(2)]
                    pool.tensor_tensor(e.rearrange("p s (a n) -> p s a n", a=16), coarse[0], fine[1], ALU.mult)
                    pool.tensor_tensor(SM3[:].rearrange("p s (a n) -> p s a n", a=16), coarse[1], fine[0], ALU.mult)\
                        .then_inc(sem("s5_turn"), 1)
                    turns[0] += 1
                    pool.wait_ge(sem("s5_turn"), turns[0])
                    pool.tensor_tensor(e, e, SM3[:], ALU.add).then_inc(sem("s5_sines"), 1)
                    pool.wait_ge(sem("s5_sines"), 2 * kt + a2 + 1)

            turns = [0]
            sines(0)
            for s in range(ST_TILES):
                kt, a, z, o = s // 4, s % 4, SZ[:, s % 2], SST[:, s % 2]
                cs = ECS[:, kt % 2, 0, a].unsqueeze(1).broadcast_to([P, 2, T])
                sn = ECS[:, kt % 2, 1, a].unsqueeze(1).broadcast_to([P, 2, T])
                pool.wait_ge(sem("s5_z"), s + 1)
                if s >= 2:
                    pool.wait_ge(sem("s5_cy"), s - 1)
                    pool.wait_ge(sem("s5_s"), s)
                pool.tensor_tensor(o, z, cs, ALU.mult)
                pool.tensor_tensor(SM3[:], z, sn, ALU.mult).then_inc(sem("s5_turn"), 1)
                turns[0] += 1
                pool.wait_ge(sem("s5_turn"), turns[0])
                pool.tensor_tensor(o[:, 0], o[:, 0], SM3[:, 1], ALU.subtract)
                pool.tensor_tensor(o[:, 1], o[:, 1], SM3[:, 0], ALU.add).then_inc(sem("s5_s"), 1)
                pool.wait_ge(sem("s5_s"), s + 1)
                if a == 1 and kt < 3:
                    sines(kt + 1)
                if s == 11:
                    for t in range(2):
                        pool.dma_start(LW[:, t], lw[:, :, LH * t:LH * t + LH, :]).then_inc(sem("lw_in"), 16)
            pool.wait_ge(sem("lru_mm"), LH)
            pool.dma_start(LW[:, 0], lw[:, :, 2 * LH:3 * LH, :]).then_inc(sem("lw_in"), 16)
            pool.wait_ge(hlo_ready, APPLY["merged"] + 4)
            pool.dma_start(WR[:], A["w_router"].rearrange("p (k n) -> p k n", k=KT)).then_inc(sem("wr_in"), 16)

        @block.scalar
        def _(act):
            def stats(n, src, ready):
                for ch in range(4):
                    act.wait_ge(ss_done, 4 * n + ch - 1)
                    ready(ch)
                    act.activation(SQ[:, ch % 2], src[:, 4 * ch:4 * ch + 4, :], ACT.Square).then_inc(sq_done, 1)
                act.wait_ge(rec_done, n + 1)
                act.activation(RB[:, 0], RB[:, 0], ACT.Sqrt).then_inc(rb_done, 1)

            def apply_hi(base_, chunks, buf, out, shift=None):
                for ch in range(chunks):
                    act.wait_ge(tmp_ready, base_ + ch + 1)
                    if shift is None:
                        act.activation(out(ch, None), buf[:, ch % 2], ACT.Copy).then_inc(hhi_ready, 1)
                    else:
                        for k in range(4):
                            last = act.activation(out(ch, k), buf[:, ch % 2, k], ACT.Identity, bias=shift(ch, k))
                        last.then_inc(hhi_ready, 1)

            def nothing(*_):
                pass

            act.wait_ge(sem("cols_in"), 16)
            act.activation(C4F[:, 0:2], col("c", 0, 32).rearrange("p (v k) -> p v k", v=2), ACT.Tanh, scale=0.5)\
               .then_inc(sem("c_tanh"), 1)
            act.wait_ge(sem("c_silu"), 1)
            act.activation(C4[:].rearrange("p k (v h) -> p v k h", v=2)[:, :, :, 0], C4F[:, 2:4], ACT.Copy)\
               .then_inc(sem("c_ready"), 1)
            act.wait_ge(sem("lam_sum"), 1)
            act.activation(LAM[:, 2:4], LAM[:, 0:2], ACT.Exp).then_inc(sem("lam_exp"), 1)
            to_hi(act, G["mod"], 0, 0)
            to_hi(act, G["mod"], 0, 1)

            def first_norm(c):
                if c == 4 * MOD_FIRST - 3:
                    act.wait_ge(rec_done, 1)
                    act.activation(RBW[:], RBW[:], ACT.Sqrt).then_inc(rb_done, 1)
                    act.wait_ge(sem("wg_in"), 16)
                    act.activation(WGH[:], WG[:], ACT.Copy).then_inc(sem("wg_hi"), 1)
            feed(act, to_hi, G["mod"], [], beside=first_norm)
            act.wait_ge(sem("scales"), 2)
            for ch in range(8):
                s = ch % 2
                if ch == 1:
                    act.wait_ge(sem("ctx_normed"), 1)
                for k in range(4 * (ch // 2), 4 * (ch // 2) + 4):
                    last = act.activation(H1HI[:, s, k, :], XIN[:, s, k, :], ACT.Identity,
                                          scale=SCALES[:, s, k:k + 1], bias=MODC[:, k, s:s + 1])
                last.then_inc(hhi_ready, 1)
            def gate_steps(c):
                if c == 4:
                    act.wait_ge(sem("gate_mm"), 1)
                    act.activation(GALL[:], PS[0:4 * HEADS, 6 * NB:7 * NB], ACT.Copy).then_inc(sem("gates_copied"), 1)
                    act.wait_ge(sem("gate_abs"), 1)
                    gabs = GS[:, 0]
                    act.activation(gabs, gabs, ACT.Exp, scale=-1.0).then_inc(sem("gate_e"), 1)
                    act.wait_ge(sem("gate_e"), 1)
                    act.activation(gabs, gabs, ACT.Ln, bias=1.0).then_inc(sem("gate_ln"), 1)
                if c == 7:
                    act.wait_ge(sem("gate_em"), 1)
                    em = GROW[:, 2]
                    act.activation(em, em, ACT.Exp, scale=-1.0).then_inc(sem("gate_emt"), 1)

            def conv_in(dst, wide_, col0):
                def s1(g, i, b):
                    wait_block(act, g, i, b)
                    ps = (wide if wide_ else narrow)(g.b0 + b)
                    for j in range(4):
                        t = 4 * b + j
                        out = dst[:, t].rearrange("p s t -> p (s t)") if wide_ else dst[:, t]
                        last = act.activation(out, ps[:, j], ACT.Identity,
                                              bias=col("conv_qk_b", col0 + t), scale=col("conv_qk_w", 16 + col0 + t))
                    last.then_inc(stage_sem["a1"], 1)

                def s2(g, i, b):
                    wait_stage(act, "free", g, i, b)
                    th = KTH[:] if wide_ else QTH[:]
                    if b:
                        wait_stage(act, "d2", g, i, b - 1)
                    act.activation(th, dst[:, 4 * b:4 * b + 4], ACT.Tanh, scale=0.5).then_inc(stage_sem["a2"], 1)
                return [s1, s2]

            def copy_out(dst, wide_, func=ACT.Copy, scale=1.0):
                def s1(g, i, b):
                    wait_block(act, g, i, b)
                    ps = (wide if wide_ else narrow)(g.b0 + b)
                    act.activation(dst(b), ps, func, scale=scale)\
                       .then_inc(stage_sem["free"], 1)
                return [s1]

            feed(act, to_hi, G["mk"], conv_in(MK, True, 8), beside=gate_steps)
            feed(act, to_hi, G["mv"], copy_out(lambda b: MV[:, :, 4 * b:4 * b + 4, 0:128], True))
            feed(act, to_hi, G["dk"], copy_out(lambda b: DK[:, 4 * b:4 * b + 4], True))
            feed(act, to_hi, G["dv"], copy_out(lambda b: DV[:, :, 4 * b:4 * b + 4, :], True))
            feed(act, to_hi, G["mq"], conv_in(MQ, False, 0))
            feed(act, to_hi, G["dq"], copy_out(lambda b: DQ[:, 4 * b:4 * b + 4], False))
            feed(act, to_hi, G["mo"], copy_out(lambda b: MO[:, 4 * b:4 * b + 4], False, ACT.Tanh, 0.5))

            def num_copy(h):
                for d in range(2):
                    act.wait_ge(sem("m_pv"), 2 * h + d + 1)
                    ps = bank(6 + d, 258).rearrange("p (u n) -> p u n", u=2)
                    act.activation(NUM[:, d, :, h % 4, :], ps[:, :, 0:128], ACT.Copy)
                    act.activation(STAT[:, 0:16].rearrange("p (d u h) -> p d u h", d=2, u=2)[:, d, :, h % 4],
                                   ps[:, :, 128], ACT.Copy).then_inc(sem("m_num"), 1)

            def m_root(half):
                act.wait_ge(sem("m_var"), half + 1)
                act.activation(STAT[:, 16:24], STAT[:, 16:24], ACT.Sqrt).then_inc(sem("m_rstd"), 1)

            for h in range(HEADS):
                for d in range(2):
                    act.wait_ge(sem("m_bc"), 2 * h + d + 1)
                    act.wait_ge(sem("m_zero"), 1)
                    if h:
                        act.wait_ge(sem("m_p"), 2 * (h - 1) + d + 1)
                    bc = bank(4 + d)
                    for j in (2, 3):
                        act.activation(MW[:, d, j], bc[:, 0:256], ACT.Exp, bias=ACOL[:, d, j, h:h + 1])
                    for j in range(2):
                        act.activation(MW[:, d, j, 128 * j:128 * j + 128], bc[:, 256 + 128 * j:384 + 128 * j],
                                       ACT.Exp, bias=ACOL[:, d, j, h:h + 1])
                    act.activation(MW[:, d, d, 128 * (1 - d):128 * (1 - d) + 128],
                                   bc[:, 128 * (1 - d):128 * (1 - d) + 128],
                                   ACT.Exp, bias=ACOL[:, d, d, h:h + 1]).then_inc(sem("m_w"), 1)
                if h == 5:
                    m_root(0)
                if h:
                    num_copy(h - 1)
            num_copy(HEADS - 1)

            def d_exp(u):
                par = u % 2
                act.wait_ge(sem("d_nm"), u + 1)
                if u >= 2:
                    act.wait_ge(sem("d_p"), u - 1)
                for c in range(2):
                    last = act.activation(DE[:, par, c], bank(2 * par + c), ACT.Exp, scale=0.125,
                                          bias=STAT[:, 32 + 8 * par + 2 + c:32 + 8 * par + 3 + c],
                                          accum_out=STAT[:, 32 + 8 * par + 4 + c:32 + 8 * par + 5 + c])
                last.then_inc(sem("d_e"), 1)

            def d_copy_t(u):
                act.wait_ge(sem("d_t"), u + 1)
                if u >= 2:
                    act.wait_ge(sem("d_o"), u - 1)
                act.activation(DPT[:, u % 2].rearrange("p j t -> p (j t)"), bank(4 + u % 2), ACT.Copy)\
                   .then_inc(sem("d_tc"), 1)

            def d_copy_o(u):
                act.wait_ge(sem("d_o"), u + 1)
                act.activation(DO[:, u % 2, u // 2, :], bank(6 + u % 2, 128), ACT.Copy).then_inc(sem("d_oc"), 1)

            U = 2 * HEADS
            for u in range(U + 3):
                if 2 <= u < U + 2:
                    d_copy_t(u - 2)
                if u < U:
                    d_exp(u)
                if u == 0:
                    m_root(1)
                if u >= 3:
                    d_copy_o(u - 3)
            act.wait_ge(sem("d_var"), 1)
            act.activation(STAT[:, 0:16], STAT[:, 0:16], ACT.Sqrt).then_inc(sem("d_rstd"), 1)
            act.wait_ge(sem("mixd_done"), 1)
            for ch in range(4):
                act.activation(HHI[:, 4 * ch:4 * ch + 4], MIX[:, 4 * ch:4 * ch + 4], ACT.Copy).then_inc(hhi_ready, 1)
            copy_y = [lambda g, i, b: (wait_block(act, g, i, b),
                                       act.activation(Y[:, 4 * b:4 * b + 4], narrow(g.b0 + b), ACT.Copy)
                                       .then_inc(stage_sem["free"], 1))]
            feed(act, to_hi, G["wout"], copy_y)
            stats(1, Y, lambda ch: wait_stage(act, "free", G["wout"], 0, ch))
            stats(2, X, lambda ch: act.wait_ge(x_new, ch + 1))
            apply_hi(TMPS["ffn"], 4, TMP, lambda ch, k: HHI[:, 4 * ch + k, :],
                     lambda ch, k: MODC[:, 48 + 4 * ch + k, 0:1])

            def up_stages(part):
                f0 = FFN_PARTS[part][0]

                def s1(g, i, b):
                    wait_block(act, g, i, b)
                    ps, par = narrow(g.b0 + b), b % 2
                    for j in range(4):
                        t = (j // 2) * FT + j % 2 + 2 * (f0 + b)
                        w = COL_AT["conv_ffn_w"][0] + 2 * FT + t + mult(i, 4)
                        bb = COL_AT["conv_ffn_b"][0] + t + mult(i, 4)
                        last = act.activation(UC[:, par, j], ps[:, j], ACT.Identity,
                                              bias=COL[:, bass.ds(bb, 1)], scale=COL[:, bass.ds(w, 1)])
                    last.then_inc(stage_sem["a1"], 1)

                def s2(g, i, b):
                    wait_stage(act, "free", g, i, b)
                    act.activation(UTH[:, b % 2], UC[:, b % 2, 0:2], ACT.Tanh, scale=0.5)\
                       .then_inc(stage_sem["a2"], 1)

                def s3(g, i, b):
                    wait_stage(act, "d2", g, i, b)
                    act.activation(AHI[:, bass.ds(mult(i, 4) + 2 * b, 2)], UACT[:, b % 2], ACT.Copy)\
                       .then_inc(stage_sem["a3"], 1)
                return [s1, s2, s3]

            for part in range(3):
                if part:
                    wait_block(act, G[f"down{part - 1}"], 0, 3)
                stages = up_stages(part)
                feed(act, to_hi, G[f"up{part}"], stages, last=1)
                feed(act, to_hi, G[f"down{part}"], copy_y if part == 0 else [],
                     beside=lambda c: last_stages(c, G[f"up{part}"], stages))
            stats(3, Y, lambda ch: wait_stage(act, "free", G["down2"], 0, ch))
            stats(4, X, lambda ch: act.wait_ge(x_new, 4 + ch + 1))
            apply_hi(TMPS["mix2"], 4, TMP, lambda ch, k: HHI[:, 4 * ch:4 * ch + 4, :])

            def u_out(g, i, b):
                wait_block(act, g, i, b)
                act.activation(U5[:], narrow(g.b0 + b), ACT.Copy).then_inc(stage_sem["free"], 1)

            def x_out(g, i, b):
                wait_block(act, g, i, b)
                ps = narrow(g.b0 + b)
                for j in range(4):
                    t = 4 * b + j
                    last = act.activation(XC[:, t], ps[:, j], ACT.Identity, bias=col("lru_conv_b", t),
                                          scale=col("lru_conv_w", 36 + t))
                last.then_inc(stage_sem["a1"], 1)

            def y_out1(g, i, b):
                wait_block(act, g, i, b)
                if b:
                    wait_stage(act, "free", g, i, b - 1)
                act.activation(YSQ[:], narrow(g.b0 + b), ACT.Square).then_inc(sem("y_squared"), 1)
                act.wait_ge(sem("y_squared"), b + 1)
                act.activation(YSQ[:], YSQ[:], ACT.Identity, scale=0.044715, bias=1.0).then_inc(stage_sem["a1"], 1)

            def y_out2(g, i, b):
                wait_stage(act, "d1", g, i, b)
                act.activation(YSQ[:], YSQ[:], ACT.Tanh, scale=GELU_C).then_inc(stage_sem["a2"], 1)

            def s5(n, m=1):
                return S5S[:, n:n + m]

            def s5_steps(c):
                if c == 0:
                    act.wait_ge(hlo_ready, APPLY["mix2"] + 4)
                    act.activation(s5(0), col("log_step", 0, 16).unsqueeze(1), ACT.Exp).then_inc(sem("s5_step"), 1)
                    act.activation(HALF[:, 60:72], HALF[:, 60:72], ACT.Exp, scale=-1.0).then_inc(sem("sp_e"), 1)
                if c == 1:
                    act.wait_ge(sem("sp_u"), 1)
                    act.activation(S5S[:, 17, 0:12], S5S[:, 16, 0:12], ACT.Ln).then_inc(sem("sp_ln"), 1)
                if c == 3:
                    act.wait_ge(sem("s5_pre"), 1)
                    act.activation(s5(1), s5(1), ACT.Exp).then_inc(sem("s5_abs"), 1)
                    act.activation(s5(4), s5(3), ACT.Sin)
                    act.activation(s5(5), s5(3), ACT.Sin, scale=0.5).then_inc(sem("s5_sin"), 1)
                    act.wait_ge(sem("s5_ang"), 1)
                    act.activation(ESC[:], EX[:], ACT.Sin, scale=TWO_PI).then_inc(sem("s5_esc"), 1)

            feed(act, to_hi, G["in_u"], [u_out], beside=s5_steps)
            feed(act, to_hi, G["in_x"], [x_out])
            feed(act, to_hi, G["in_y"], [y_out1, y_out2])

            def lru_in(n):
                if n:
                    act.wait_ge(sem("lru_out"), n)
                else:
                    act.wait_ge(sem("s5_s"), ST_TILES)
                    act.wait_ge(sem("s5_yk"), S5_TILES)
                for h in range(LH):
                    t = n * LH + h
                    act.wait_ge(sem("lru_mm"), t + 1)
                    ps = bank(4 + h)
                    act.activation(LR[:, h], ps[:, 0:256], ACT.Tanh, scale=0.5, bias=HALF[:, 36 + t:37 + t])
                    last = act.activation(LI[:, h], ps[:, 256:512], ACT.Tanh, scale=0.5, bias=HALF[:, 48 + t:49 + t])
                last.then_inc(sem("lru_ri"), 1)

            def lru_exp(n):
                act.wait_ge(sem("lru_y"), n + 1)
                act.activation(LA[:], LR[:], ACT.Tanh)
                act.activation(LT[:], LR[:], ACT.Exp, scale=-2.0).then_inc(sem("lru_th"), 1)
                act.wait_ge(sem("lru_th"), n + 1)
                act.activation(LR[:], LR[:], ACT.Exp, scale=-1.0).then_inc(sem("lru_a"), 1)

            def lru_root(n):
                act.wait_ge(sem("lru_m"), n + 1)
                act.activation(LA[:], LA[:], ACT.Sqrt).then_inc(sem("lru_sq"), 1)

            def beside_gates(c):
                if c == 0:
                    act.wait_ge(sem("s5_yk"), S5_TILES)
                    act.activation(Y5B[:], U5[:], ACT.Square).then_inc(sem("s5_ysq"), 1)
                if c == 1:
                    act.wait_ge(sem("s5_yt"), 1)
                    act.activation(Y5B[:], Y5B[:], ACT.Tanh, scale=GELU_C).then_inc(sem("s5_yth"), 1)
                if c == 3:
                    act.wait_ge(sem("s5_g"), 1)
                    act.wait_ge(sem("s5_s"), ST_TILES)
                    act.activation(GHI[:], Y5, ACT.Copy).then_inc(sem("s5_ghi"), 1)
                if c % 3 == 0:
                    lru_in(c // 3)
                elif c % 3 == 1:
                    lru_exp(c // 3)
                elif c % 3 == 2:
                    lru_root(c // 3)

            def glu_out(g, i, b):
                wait_block(act, g, i, b)
                act.wait_ge(sem("half_b"), 1)
                for j in range(4):
                    last = act.activation(Y5B[:, j], narrow(g.b0 + b)[:, j], ACT.Tanh, scale=0.5,
                                          bias=HALF[:, 32 + j:33 + j])
                last.then_inc(stage_sem["free"], 1)

            def gate_out(k):
                def s1(g, i, b):
                    wait_block(act, g, i, b)
                    if k >= 2:
                        wait_stage(act, "free", G[f"proj{k - 2}"], 0, 0)
                    if k == 1:
                        act.wait_ge(sem("lru_out"), 3)
                    for j in range(4):
                        last = act.activation(GT[k % 2][b][:, j], narrow(g.b0 + b)[:, j], ACT.Tanh, scale=0.5,
                                              bias=HALF[:, 16 * b + 4 * k + j:16 * b + 4 * k + j + 1])
                    last.then_inc(stage_sem["free"], 1)
                return [s1]

            def split_mixer(c):
                if c < 4:
                    act.wait_ge(sem("s5_out"), 1)
                    k4 = slice(4 * ((c + 1) % 4), 4 * ((c + 1) % 4) + 4)
                    act.activation(AHI[:, k4], OUT5[:, 4 * c:4 * c + 4], ACT.Copy).then_inc(hhi_ready, 1)

            feed(act, to_hi, G["gates0"], gate_out(0), beside=beside_gates)
            lru_root(2)
            feed(act, to_hi, G["glu"], [glu_out])
            feed(act, to_hi, G["gates1"], gate_out(1), beside=split_mixer)
            def split_merged(ch):
                wait_stage(act, "d2", G[f"proj{ch}"], 0, 0)
                wait_block(act, G["gates3"], 0, 1)
                act.activation(HHI[:, 4 * ch:4 * ch + 4], MG[:, 4 * ch:4 * ch + 4], ACT.Copy).then_inc(hhi_ready, 1)

            for k in range(4):
                feed(act, to_hi, G[f"proj{k}"], [], beside=lambda c: split_merged(c - 1) if k == 3 and c >= 1 else None)
                if k < 2:
                    feed(act, to_hi, G[f"gates{k + 2}"], gate_out(k + 2))
            split_merged(3)

            def router_hi(c):
                if c == 2:
                    act.wait_ge(sem("wr_in"), 16)
                    act.activation(WRH[:], WR[:], ACT.Copy).then_inc(sem("wr_hi"), 1)
            feed(act, to_hi, G["out2"], [], beside=router_hi)
            stats(5, X, lambda ch: wait_stage(act, "free", G["out2"], 0, ch))
            apply_hi(TMPS["moe"], 4, TMP, lambda ch, k: HHI[:, 4 * ch:4 * ch + 4, :])
            def router(c):
                if c == 4:
                    act.wait_ge(sem("r_mm"), 1)
                    act.activation(RLT[:], PS[0:36, 6 * NB:6 * NB + T], ACT.Copy).then_inc(sem("r_rows"), 1)
                if c == 5:
                    act.wait_ge(sem("r_shift"), 1)
                    act.activation(RS[:, 2, :, 0:4], RS[:, 2, :, 0:4], ACT.Exp).then_inc(sem("r_exp"), 1)
                if c == 6:
                    act.wait_ge(sem("r_gap"), 1)
                    act.activation(RS[:, 9, :, 0:1], RS[:, 9, :, 0:1], ACT.Exp).then_inc(sem("r_gape"), 1)
                if c == 7:
                    act.wait_ge(sem("r_combT"), 1)
                    act.activation(COMBT[:], PS[0:EXPERTS, 7 * NB:7 * NB + T], ACT.Copy).then_inc(sem("combT"), 1)

            def moe_tanh(g, i, b):
                wait_block(act, g, i, b)
                wait_stage(act, "free", g, i, b - 1)
                act.activation(MTH[:], narrow(g.b0 + b)[:, 0:2], ACT.Tanh, scale=0.5).then_inc(stage_sem["a2"], 1)

            def moe_hi(off):
                def s3(g, i, b):
                    wait_stage(act, "d2", g, i, b)
                    act.activation(AHI[:, bass.ds(mult(i, 4) + 2 * b + off, 2)], MACT[:], ACT.Copy)\
                       .then_inc(stage_sem["a3"], 1)
                return s3

            feed(act, to_hi, G["moe_first"], [moe_tanh], beside=router)
            for q in range(8):
                act.wait_ge(sem("cb_mm"), q + 1)
                act.activation(CB[:, 4 * q:4 * q + 4], narrow(q, 2), ACT.Copy).then_inc(sem("cb"), 1)
            for b in range(FIRST_EXPERTS):
                act.wait_ge(sem("first_act"), b + 1)
                act.activation(AHI[:, 2 * b:2 * b + 2], MF[:, b], ACT.Copy).then_inc(sem("first_hi"), 1)

            for part in range(4):
                if part:
                    wait_block(act, G[f"moe_down{part - 1}"], 0, 3)
                feed(act, to_hi, G[f"moe_up{part}"], [moe_tanh, nothing, moe_hi(0 if part else 2 * FIRST_EXPERTS)])
                feed(act, to_hi, G[f"moe_down{part}"], [])
            stats(6, X, lambda ch: wait_stage(act, "free", G["moe_down3"], 0, ch))

        @block.vector
        def _(dve):
            st, dve_st.eng = dve_st, dve
            dve.sem_inc(lo_done, RING)

            def nothing(*_):
                pass

            def var(n, wide_):
                dve.wait_ge(ss_done, 4 * n + 4)
                m = 2 * T if wide_ else T
                rb = (RBW if wide_ else RB)[:].rearrange("p s t -> p (s t)")[:, 0:m]
                st(dve.tensor_scalar(rb, bank(7, m), 1.0 / D, EPS, ALU.mult, ALU.add))
                dve.reciprocal(rb, rb).then_inc(rec_done, 1)
                dve.wait_ge(rb_done, n + 1)

            def apply(b_hi, b_tmp, chunks, buf, src, scale, rb, out, shift=None):
                def first(ch):
                    if b_hi + ch - 1 > 0:
                        dve.wait_ge(hlo_ready, b_hi + max(ch - 1, 0))
                    for k in range(4):
                        last = dve.scalar_tensor_tensor(buf[:, ch % 2, k], src(ch, k), scale(ch, k), rb(ch),
                                                        ALU.mult, ALU.mult)
                    last.then_inc(tmp_ready, 1)

                def second(ch):
                    dve.wait_ge(hhi_ready, b_hi + ch + 1)
                    if shift is None:
                        o_hi, o_lo = out(ch, None)
                        last = dve.tensor_tensor(o_lo, buf[:, ch % 2], o_hi.bitcast(F32), ALU.subtract)
                    else:
                        for k in range(4):
                            o_hi, o_lo = out(ch, k)
                            last = dve.scalar_tensor_tensor(o_lo, buf[:, ch % 2, k], shift(ch, k), o_hi.bitcast(F32),
                                                            ALU.add, ALU.subtract)
                    last.then_inc(hlo_ready, 1)

                for ch in range(chunks + 1):
                    if ch < chunks:
                        first(ch)
                        if ch == 0:
                            dve.wait_ge(tmp_ready, b_tmp + 1)
                    if ch:
                        dve.wait_ge(tmp_ready, b_tmp + ch)
                        second(ch - 1)

            def split(b_hi, hi, lo, src):
                for ch in range(4):
                    sl = slice(4 * ch, 4 * ch + 4)
                    dve.wait_ge(hhi_ready, b_hi + ch + 1)
                    dve.tensor_tensor(lo[:, sl], src[:, sl], hi[:, sl].bitcast(F32), ALU.subtract)\
                       .then_inc(hlo_ready, 1)

            def residual(n, scale):
                var(n, False)
                for ch in range(4):
                    for k in range(4 * ch, 4 * ch + 4):
                        last = dve.scalar_tensor_tensor(Y[:, k], Y[:, k], scale(k), RB[:, 0], ALU.mult, ALU.mult)
                    st(last)
                    sl = slice(4 * ch, 4 * ch + 4)
                    dve.tensor_tensor(X[:, sl], X[:, sl], Y[:, sl], ALU.add).then_inc(x_new, 1)

            dve.memset(ONES[:], 1.0).then_inc(sem("ones"), 1)
            dve.wait_ge(sem("cols_in"), 16)
            dve.wait_ge(sem("c_tanh"), 1)
            cc = col("c", 0, 32).rearrange("p (v k) -> p v k", v=2)
            st(dve.scalar_tensor_tensor(C4F[:, 0:2], C4F[:, 0:2], 1.0, cc, ALU.add, ALU.mult))
            dve.tensor_scalar(C4F[:, 2:4], C4F[:, 0:2], 0.5, None, ALU.mult).then_inc(sem("c_silu"), 1)
            dve.wait_ge(sem("c_silu"), 1)
            st(dve.tensor_copy(CS[:], C4F[:, 2]))
            dve.wait_ge(sem("c_ready"), 1)
            c4 = C4[:].rearrange("p k (v h) -> p v k h", v=2)
            dve.tensor_tensor(c4[:, :, :, 1], C4F[:, 2:4], c4[:, :, :, 0].bitcast(F32), ALU.subtract)\
               .then_inc(sem("c_ready"), 1)
            dve.wait_ge(sem("lam_in"), 16)
            st(dve.tensor_tensor(LAMP[:], LAMV[:, 0:4:2], LAMV[:, 1:4:2], ALU.mult))
            dve.reduce_sum(LAM[:, 0:2], LAMP[:], axis=AX.X).then_inc(sem("lam_sum"), 1)
            dve.wait_ge(sem("lam_exp"), 1)
            st(dve.tensor_tensor(LAM[:, 4:5], LAM[:, 2:3], LAM[:, 3:4], ALU.subtract))
            dve.tensor_scalar(LAM[:, 5:6], LAM[:, 4:5], 0.2, None, ALU.add).then_inc(sem("lam_ready"), 1)
            for dst, name, n in ((0, "b_gate2", 32), (32, "b_glu", 4), (36, "lru_b_a", 12), (48, "lru_b_x", 12)):
                dve.tensor_scalar(HALF[:, dst:dst + n], col(name, 0, n), 0.5, None, ALU.mult)
            dve.scalar_tensor_tensor(HALF[:, 60:72], col("lru_lambda", 0, 12), -1.0, col("lru_lambda", 0, 12), ALU.mult, ALU.max)\
               .then_inc(sem("half_b"), 1)

            def mod_out(g, i, b):
                wait_block(dve, g, i, b)
                dve.tensor_copy(MROW[:, b % 2], PS[0:4, (b % 2) * NB:(b % 2) * NB + NB]).then_inc(stage_sem["free"], 1)

            to_lo(dve, G["mod"], 0, 0)
            to_lo(dve, G["mod"], 0, 1)

            def first_norm(c):
                if c == 4 * MOD_FIRST - 3:
                    var(0, True)
                if c == 4 * MOD_FIRST - 1:
                    dve.wait_ge(sq_done, 4)
                    dve.tensor_tensor(XIN[:, 0], XIN[:, 0], RBW[:, 0].unsqueeze(1).broadcast_to([P, KT, T]), ALU.mult)\
                       .then_inc(sem("scales"), 1)
                    dve.wait_ge(sem("scales"), 1)
                    dve.wait_ge(sem("wg_hi"), 1)
                    dve.tensor_tensor(WGL[:], WG[:], WGH[:].bitcast(F32), ALU.subtract).then_inc(sem("wg_lo"), 1)
            feed(dve, to_lo, G["mod"], [mod_out], st, 0, beside=first_norm, pre=1)
            dve.wait_ge(sem("mod_cols"), 1)
            first = 4 * MOD_FIRST
            bm = col("b_mod", 0, first).unsqueeze(2).broadcast_to([P, first, 2])
            st(dve.tensor_tensor(MODC[:, 0:first], bank(6, 2 * first).rearrange("p (k v) -> p k v", v=2), bm, ALU.add))
            for v in range(2):
                last = dve.scalar_tensor_tensor(SCALES[:, v], MODC[:, 16:32, v], 1.0, col("g_pre_mix", 0, 16),
                                                ALU.add, ALU.mult)
            last.then_inc(sem("scales"), 1)
            dve.wait_ge(sem("scales"), 2)
            for ch in range(8):
                if ch >= 2:
                    dve.wait_ge(hlo_ready, ch - 1)
                s, q = ch % 2, ch // 2
                if ch == 1:
                    dve.wait_ge(sem("ctx_normed"), 1)
                if ch == 3:
                    to_lo(dve, G["mk"], 0, 1)
                for j in range(4):
                    k = 4 * q + j
                    last = dve.tensor_scalar(TMPW[:, ch % 2, j], XIN[:, s, k, :], SCALES[:, s, k:k + 1],
                                             MODC[:, k, s:s + 1], ALU.mult, ALU.add)
                st(last)
                dve.wait_ge(hhi_ready, ch + 1)
                k4 = slice(4 * q, 4 * q + 4)
                dve.tensor_tensor(H1LO[:, s, k4], TMPW[:, ch % 2], H1HI[:, s, k4].bitcast(F32), ALU.subtract)\
                   .then_inc(hlo_ready, 1)

            def gate_steps(c):
                if c == 4:
                    dve.wait_ge(sem("grow_mm"), 1)
                    dve.wait_ge(sem("bg_in"), 16)
                    for k in range(4):
                        last = dve.tensor_scalar(GROW[:, k], PS[0:HEADS, (4 + k) * NB:(5 + k) * NB], BG[:, k:k + 1],
                                                 None, ALU.add)
                    last.then_inc(sem("grow"), 1)
                    dve.wait_ge(sem("grow"), 1)
                    forget = GROW[:, 1:4:2]
                    dve.scalar_tensor_tensor(GS[:, 0], forget, -1.0, forget, ALU.mult, ALU.max)\
                       .then_inc(sem("gate_abs"), 1)
                if c == 5:
                    forget = GROW[:, 1:4:2]
                    dve.wait_ge(sem("gate_ln"), 1)
                    st(dve.scalar_tensor_tensor(GS[:, 1], forget, 0.0, GS[:, 0], ALU.min, ALU.subtract))
                    one = ONES[0:HEADS, 0:1].broadcast_to([HEADS, 2 * T])
                    dve.wait_ge(sem("ones"), 1)
                    for d in range(2):
                        last = dve.tensor_tensor_scan(GS[:, 0, d], one, GS[:, 1, d], 0.0, ALU.mult, ALU.add)
                    st(last)
                    for d in range(2):
                        last = dve.tensor_tensor(GS[:, 1, d], GROW[:, 2 * d], GS[:, 0, d], ALU.subtract)
                    st(last)
                if c == 6:
                    for d in range(2):
                        last = dve.tensor_tensor_scan(GS[:, 2, d], GS[:, 1, d], GS[:, 1, d], 0.0, ALU.max, ALU.max)
                    st(last)
                    back = slice(2 * T - 1, T - 1, -1)
                    atok = GROW[:, 0:2]
                    dve.tensor_copy(atok[:, 0, 0:T], GS[:, 1, 0, T:2 * T])
                    dve.tensor_copy(atok[:, 0, T:2 * T], GS[:, 1, 0, 0:T])
                    dve.tensor_copy(atok[:, 1, 0:T], GS[:, 1, 1, back])
                    dve.tensor_copy(atok[:, 1, T:2 * T], GS[:, 1, 1, 0:T][:, ::-1])
                    dve.tensor_scalar(NEGM[:, 0], GS[:, 2, 0, T:2 * T], -1.0, None, ALU.mult)
                    dve.tensor_scalar(NEGM[:, 1], GS[:, 2, 1, back], -1.0, None, ALU.mult)
                    dve.tensor_tensor(GROW[:, 2, 0:T], GS[:, 0, 0, T:2 * T], GS[:, 2, 0, T:2 * T], ALU.add)
                    dve.tensor_tensor(GROW[:, 2, T:2 * T], GS[:, 0, 1, back], GS[:, 2, 1, back], ALU.add)\
                       .then_inc(sem("gate_em"), 1)
                    dve.wait_ge(sem("gate_em"), 1)

            def conv_edges(dst, wide_, col0):
                def s1(g, i, b):
                    wait_stage(dve, "a1", g, i, b)
                    ps = (wide if wide_ else narrow)(g.b0 + b)
                    for w, to, frm in ((0, slice(1, T), slice(0, T - 1)), (2, slice(0, T - 1), slice(1, T))):
                        for j in range(4):
                            t = 4 * b + j
                            if wide_:
                                p, o = ps[:, j].rearrange("p (s t) -> p s t", s=2)[:, :, frm], dst[:, t, :, to]
                            else:
                                p, o = ps[:, j, frm], dst[:, t, to]
                            last = dve.scalar_tensor_tensor(o, p, col("conv_qk_w", 16 * w + col0 + t), o, ALU.mult, ALU.add)
                        if w == 0:
                            st(last)
                    last.then_inc(stage_sem["free"], 1)

                def s2(g, i, b):
                    wait_stage(dve, "a2", g, i, b)
                    th = KTH[:] if wide_ else QTH[:]
                    o = dst[:, 4 * b:4 * b + 4]
                    if wide_:
                        o, th = o.rearrange("p j s t -> p (j s t)"), th.rearrange("p j s t -> p (j s t)")
                    else:
                        o, th = o.rearrange("p j t -> p (j t)"), th.rearrange("p j t -> p (j t)")
                    dve.scalar_tensor_tensor(o, th, 1.0, o, ALU.add, ALU.mult).then_inc(stage_sem["d2"], 1)
                return [s1, s2]

            feed(dve, to_lo, G["mk"], conv_edges(MK, True, 8), beside=gate_steps)

            def gate_cols(c):
                if c == 3:
                    dve.wait_ge(sem("a_cols"), 1)
                    dve.tensor_copy(ACOL[:].rearrange("p d j h -> p (d j h)"), bank(6, 64))
                    dve.tensor_copy(EMT[:].rearrange("p d u h -> p (d u h)"), PS[:, 6 * NB + 64:6 * NB + 96])\
                       .then_inc(sem("a_copied"), 1)
                    dve.wait_ge(sem("a_copied"), 1)
                    dve.memset(MV[:, :, :, 128:129], 1.0).then_inc(sem("mv_ones"), 1)
            feed(dve, to_lo, G["mv"], [], beside=gate_cols)
            for name in ("dk", "dv"):
                feed(dve, to_lo, G[name], [])
            mod_sums_out(dve, MOD_REST // 2)
            dve.wait_ge(sem("mod_rest"), MOD_REST // 2 + 1)
            dve.scalar_tensor_tensor(SCALES[:, 3], MODC[:, 64:80, 0], 1.0, col("g_pre_ffn", 0, 16), ALU.add, ALU.mult)
            for n, chunk, gname in ((2, 2, "g_post_mix"), (4, 5, "g_post_ffn")):
                last = dve.tensor_tensor(SCALES[:, n], MODC[:, 16 * chunk:16 * chunk + 16, 0], col(gname, 0, 16), ALU.mult)
            st(last)
            feed(dve, to_lo, G["mq"], conv_edges(MQ, False, 0))
            feed(dve, to_lo, G["dq"], [])

            cos2 = ROPE[:, 0].unsqueeze(1).broadcast_to([P, 2, T])
            sin2 = ROPE[:, 1].unsqueeze(1).broadcast_to([P, 2, T])

            def rope(r):
                v = DK[:, 2 * r:2 * r + 2, 0, :] if r < 4 else DQ[:, 2 * (r - 4):2 * (r - 4) + 2, :]
                dve.wait_ge(sem("rope_in"), 16)
                dve.wait_ge(sem("rot"), r + 1)
                dve.tensor_tensor(RT1[:], v, cos2, ALU.mult)
                st(dve.tensor_tensor(RT2[:], bank(4 + r % 2).rearrange("p (h t) -> p h t", h=2), sin2, ALU.mult))
                dve.tensor_tensor(v, RT1[:], RT2[:], ALU.add).then_inc(sem("roped"), 1)
                dve.wait_ge(sem("roped"), r + 1)
            feed(dve, to_lo, G["mo"], [], beside=lambda c: rope(c - 2) if c >= 2 else None)
            rope(6)
            rope(7)

            wait_stage(dve, "free", G["mo"], 0, 1)
            mo_flat = MO[:].rearrange("p h t -> p (h t)")
            st(dve.tensor_scalar(mo_flat, mo_flat, 1.0, None, ALU.add))
            ST16 = STAT[:, 0:16]
            wait_block(dve, G["mo"], 0, 1)
            dve.memset(MW[:, 0, 1, 0:128], 0.0)
            dve.memset(MW[:, 1, 0, 128:256], 0.0).then_inc(sem("m_zero"), 1)
            dve.wait_ge(sem("m_zero"), 1)

            def m_probs(h):
                for d in range(2):
                    dve.wait_ge(sem("m_w"), 2 * h + d + 1)
                    dve.wait_ge(sem("m_s"), h + 1)
                    if h:
                        dve.wait_ge(sem("m_pv"), 2 * (h - 1) + d + 1)
                    sp_ = PS[:, (h % 2) * 1024:(h % 2) * 1024 + 1024]
                    dve.scalar_tensor_tensor(MP[:, d].rearrange("p j t -> p (j t)"), sp_, 0.25 * 128 ** -0.5,
                                             MW[:, d].rearrange("p j t -> p (j t)"), ALU.mult, ALU.mult)\
                       .then_inc(sem("m_p"), 1)

            def m_norm(half):
                dve.wait_ge(sem("m_num"), 8 * (half + 1))
                if half:
                    dve.wait_ge(sem("m_t"), 1)
                st(dve.scalar_tensor_tensor(STAT[:, 16:32], ST16, -1.0, ST16, ALU.mult, ALU.max))
                den = STAT[:, 16:32].rearrange("p (d u h) -> p d u h", d=2, u=2)
                st(dve.tensor_tensor(den, den, EMT[:, :, :, 4 * half:4 * half + 4], ALU.max))
                st(dve.reciprocal(STAT[:, 16:32], STAT[:, 16:32]))
                for d in range(2):
                    last = dve.tensor_tensor((MH, MSQ)[d][:], NUM[:, d],
                                             den[:, d].unsqueeze(3).broadcast_to([P, TT, 4, P]), ALU.mult)
                st(last)
                st(dve.tensor_tensor(MH[:], MH[:], MSQ[:], ALU.add))
                st(dve.tensor_tensor(MSQ[:], MH[:], MH[:], ALU.mult))
                var8 = STAT[:, 16:24]
                st(dve.reduce_sum(var8.rearrange("p (u h) -> p u h", u=2), MSQ[:], axis=AX.X))
                st(dve.tensor_scalar(var8, var8, 4.0 / P, 4.0 * EPS, ALU.mult, ALU.add))
                dve.reciprocal(var8, var8).then_inc(sem("m_var"), 1)
                dve.wait_ge(sem("m_rstd"), half + 1)
                rs = var8.rearrange("p (u h) -> p u h", u=2).unsqueeze(3).broadcast_to([P, TT, 4, P])
                dve.tensor_tensor(MH[:], MH[:], rs, ALU.mult).then_inc(sem("m_h"), 1)
                dve.wait_ge(sem("m_h"), half + 1)

            def m_mix(half):
                dve.wait_ge(sem("m_t"), half + 1)
                for hh in range(4):
                    h = 4 * half + hh
                    at_ = m_transposed(half) + T * hh
                    last = dve.scalar_tensor_tensor(MIX[:, h], PS[:, at_:at_ + T], col("g_mlstm", h), MO[:, h],
                                                    ALU.mult, ALU.mult)
                last.then_inc(sem("mixm_done"), 1)
                dve.wait_ge(sem("mixm_done"), half + 1)

            def d_max(u):
                par = u % 2
                dve.wait_ge(sem("d_s"), u + 1)
                s8 = STAT[:, 32 + 8 * par:40 + 8 * par]
                st(dve.reduce_max(s8[:, 0:2], PS[:, par * 1024:par * 1024 + 1024].rearrange("p (c k) -> p c k", c=2),
                                  axis=AX.X))
                dve.tensor_scalar(s8[:, 2:4], s8[:, 0:2], -0.125, None, ALU.mult).then_inc(sem("d_nm"), 1)

            def d_prob(u):
                par = u % 2
                s8 = STAT[:, 32 + 8 * par:40 + 8 * par]
                dve.wait_ge(sem("d_e"), u + 1)
                st(dve.reciprocal(s8[:, 6:8], s8[:, 4:6]))
                st(dve.tensor_scalar(s8[:, 7:8], s8[:, 7:8], LAM[:, 5:6], None, ALU.mult))
                st(dve.tensor_scalar(DE[:, par, 1], DE[:, par, 1], s8[:, 7:8], None, ALU.mult))
                if u >= 2:
                    dve.wait_ge(sem("d_t"), u - 1)
                dve.scalar_tensor_tensor(DP[:, par], DE[:, par, 0], s8[:, 6:7], DE[:, par, 1],
                                         ALU.mult, ALU.subtract).then_inc(sem("d_p"), 1)

            for h in range(5):
                m_probs(h)
            m_norm(0)
            m_probs(5)
            m_probs(6)
            m_mix(0)
            m_probs(7)
            U = 2 * HEADS
            d_max(0)
            m_norm(1)
            d_max(1)
            m_mix(1)
            dve.wait_ge(sem("m_pv"), 2 * HEADS)
            for u in range(2, U + 2):
                d_prob(u - 2)
                dve.wait_ge(sem("d_p"), u - 1)
                if u < U:
                    d_max(u)
            dve.wait_ge(sem("d_oc"), U)
            dve.wait_ge(sem("d_p"), U)
            st(dve.tensor_tensor(DSQ[:], DO[:], DO[:], ALU.mult))
            st(dve.reduce_sum(ST16.rearrange("p (u h) -> p u h", u=2), DSQ[:], axis=AX.X))
            st(dve.tensor_scalar(ST16, ST16, 1.0 / (P * 0.64), EPS / 0.64, ALU.mult, ALU.add))
            dve.reciprocal(ST16, ST16).then_inc(sem("d_var"), 1)
            dve.wait_ge(sem("d_rstd"), 1)
            rs = ST16.rearrange("p (u h) -> p u h", u=2).unsqueeze(3).broadcast_to([P, TT, HEADS, P])
            dve.tensor_tensor(DO[:], DO[:], rs, ALU.mult).then_inc(sem("d_on"), 1)
            dve.wait_ge(sem("d_ot"), 1)
            dve.tensor_scalar(MIX[:, 8:16].rearrange("p h t -> p (h t)"), PS[:, 0:2048], col("g_diff"), None, ALU.mult)\
               .then_inc(sem("mixd_done"), 1)
            split(APPLY["mix"], HHI, HLO, MIX)
            feed(dve, to_lo, G["wout"], [])
            dve.wait_ge(sem("x2_in"), 16)
            residual(1, lambda k: SCALES[:, 2, k:k + 1])
            dve.wait_ge(x_new, 4)
            var(2, False)
            wait_block(dve, G["wout"], 0, 3)
            apply(APPLY["ffn"], TMPS["ffn"], 4, TMP, lambda ch, k: X[:, 4 * ch + k],
                  lambda ch, k: SCALES[:, 3, 4 * ch + k:4 * ch + k + 1], lambda ch: RB[:, 0],
                  lambda ch, k: (HHI[:, 4 * ch + k], HLO[:, 4 * ch + k]), lambda ch, k: MODC[:, 48 + 4 * ch + k, 0:1])

            def up_stages(part):
                f0 = FFN_PARTS[part][0]

                def s1(g, i, b):
                    wait_stage(dve, "a1", g, i, b)
                    ps, par = narrow(g.b0 + b), b % 2
                    for w, to, frm in ((0, slice(1, T), slice(0, T - 1)), (2, slice(0, T - 1), slice(1, T))):
                        for j in range(4):
                            t = (j // 2) * FT + j % 2 + 2 * (f0 + b)
                            at_ = COL_AT["conv_ffn_w"][0] + 2 * FT * w + t + mult(i, 4)
                            last = dve.scalar_tensor_tensor(UC[:, par, j, to], ps[:, j, frm], COL[:, bass.ds(at_, 1)],
                                                            UC[:, par, j, to], ALU.mult, ALU.add)
                        if w == 0:
                            st(last)
                    last.then_inc(stage_sem["free"], 1)

                def s2(g, i, b):
                    wait_stage(dve, "a2", g, i, b)
                    par = b % 2
                    st(dve.scalar_tensor_tensor(UTH[:, par], UTH[:, par], 1.0, UC[:, par, 0:2], ALU.add, ALU.mult))
                    dve.scalar_tensor_tensor(UACT[:, par], UTH[:, par], 0.5, UC[:, par, 2:4], ALU.mult, ALU.mult)\
                       .then_inc(stage_sem["d2"], 1)

                def s3(g, i, b):
                    wait_stage(dve, "a3", g, i, b)
                    k = bass.ds(mult(i, 4) + 2 * b, 2)
                    dve.tensor_tensor(ALO[:, k], UACT[:, b % 2], AHI[:, k].bitcast(F32), ALU.subtract)\
                       .then_inc(stage_sem["d3"], 1)
                return [s1, s2, s3]

            def add_y(g, i, b):
                wait_block(dve, g, i, b)
                y = Y[:, 4 * b:4 * b + 4]
                dve.tensor_tensor(y, narrow(g.b0 + b), y, ALU.add).then_inc(stage_sem["free"], 1)

            for part in range(3):
                stages = up_stages(part)
                feed(dve, to_lo, G[f"up{part}"], stages, st, 2, last=1)
                if part == 1:
                    wait_stage(dve, "free", G["down0"], 0, 3)
                if part == 2:
                    wait_stage(dve, "free", G["down1"], 0, 3)
                feed(dve, to_lo, G[f"down{part}"], [add_y] if part else [],
                     beside=lambda c: last_stages(c, G[f"up{part}"], stages))
            wait_stage(dve, "free", G["down2"], 0, 3)
            residual(3, lambda k: SCALES[:, 4, k:k + 1])
            dve.wait_ge(x_new, 8)
            var(4, False)
            wait_block(dve, G["down2"], 0, 3)
            apply(APPLY["mix2"], TMPS["mix2"], 4, TMP, lambda ch, k: X[:, 4 * ch + k],
                  lambda ch, k: col("norm_mix", 4 * ch + k), lambda ch: RB[:, 0],
                  lambda ch, k: (HHI[:, 4 * ch:4 * ch + 4], HLO[:, 4 * ch:4 * ch + 4]))

            def x_taps(g, i, b):
                wait_stage(dve, "a1", g, i, b)
                ps = narrow(g.b0 + b)
                for w in range(3):
                    back_ = 3 - w
                    for j in range(4):
                        t = 4 * b + j
                        o = XC[:, t, back_:T]
                        last = dve.scalar_tensor_tensor(o, ps[:, j, 0:T - back_], col("lru_conv_w", 12 * w + t), o,
                                                        ALU.mult, ALU.add)
                    if w < 2:
                        st(last)
                last.then_inc(stage_sem["free"], 1)

            def y_cube(g, i, b):
                wait_stage(dve, "a1", g, i, b)
                dve.tensor_tensor(YSQ[:], narrow(g.b0 + b), YSQ[:], ALU.mult).then_inc(stage_sem["d1"], 1)

            def y_gelu(g, i, b):
                wait_stage(dve, "a2", g, i, b)
                dve.scalar_tensor_tensor(YG[:, 4 * b:4 * b + 4], YSQ[:], 1.0, narrow(g.b0 + b), ALU.add, ALU.mult)\
                   .then_inc(stage_sem["free"], 1)

            re, im = col("lam_re", 0, 16).unsqueeze(1), col("lam_im", 0, 16).unsqueeze(1)
            MAGIC = 1.5 * 2 ** 23

            def s5(n, m=1):
                return S5S[:, n:n + m]

            def flat(x):
                return x.rearrange("p a s n -> p (a s n)")

            def s5_steps(c):
                z, u_ = HALF[:, 60:72], S5S[:, 16, 0:12]
                if c == 0:
                    dve.wait_ge(sem("sp_e"), 1)
                    dve.tensor_scalar(u_, z, 1.0, None, ALU.add).then_inc(sem("sp_u"), 1)
                if c == 1:
                    dve.wait_ge(sem("sp_u"), 1)
                    s17, s18, s19 = (S5S[:, n, 0:12] for n in (17, 18, 19))
                    st(dve.tensor_scalar(s18, u_, -1.0, None, ALU.add))
                    st(dve.tensor_scalar(s19, s18, 0.0, None, ALU.is_equal))
                    st(dve.tensor_tensor(s18, s18, s19, ALU.add))
                    st(dve.reciprocal(s18, s18))
                    dve.wait_ge(sem("sp_ln"), 1)
                    st(dve.tensor_tensor(s17, s17, s18, ALU.mult))
                    st(dve.tensor_tensor(s17, s17, s19, ALU.add))
                    st(dve.tensor_tensor(s17, s17, z, ALU.mult))
                    st(dve.tensor_scalar(s18, col("lru_lambda", 0, 12), -1.0, 0.0, ALU.mult, ALU.max))
                    st(dve.tensor_tensor(s17, s17, s18, ALU.add))
                    st(dve.tensor_scalar(z, s17, 4.0, None, ALU.mult))
                if c == 2:
                    dve.wait_ge(sem("s5_step"), 1)
                    st(dve.tensor_tensor(s5(2), im, s5(0), ALU.mult))
                    dve.tensor_tensor(s5(1), re, s5(0), ALU.mult)
                    st(dve.tensor_scalar(s5(11), s5(2), 1.0 / (2 * math.pi), MAGIC, ALU.mult, ALU.add))
                    st(dve.tensor_scalar(s5(11), s5(11), MAGIC, None, ALU.subtract))
                    st(dve.scalar_tensor_tensor(s5(3), s5(11), -6.28125, s5(2), ALU.mult, ALU.add))
                    c2 = float(np.float32(2 * math.pi - 6.28125))
                    st(dve.scalar_tensor_tensor(s5(3), s5(11), -c2, s5(3), ALU.mult, ALU.add))
                    pi_ = float(np.nextafter(np.float32(math.pi), np.float32(0)))
                    dve.tensor_scalar(s5(3), s5(3), pi_, -pi_, ALU.min, ALU.max).then_inc(sem("s5_pre"), 1)
                    dve.wait_ge(sem("s5_pre"), 1)
                    st(dve.tensor_scalar(s5(14), s5(3), 1.0 / (2 * math.pi), None, ALU.mult))
                    st(dve.tensor_scalar(s5(15), s5(14), 16.0, None, ALU.mult))
                    st(dve.tensor_scalar(s5(11), s5(15), MAGIC, None, ALU.add))
                    st(dve.tensor_scalar(s5(11), s5(11), MAGIC, None, ALU.subtract))
                    st(dve.tensor_tensor(s5(15), s5(15), s5(11), ALU.subtract))
                    iota = CST[:, C_IOTA:C_IOTA + 16].unsqueeze(1).broadcast_to([P, 16, 16])
                    for w in range(2):
                        last = dve.tensor_tensor(EX[:, 0, w], s5(14 + w).rearrange("p a s -> p (a s)").unsqueeze(2)
                                                 .broadcast_to([P, 16, 16]), iota, ALU.mult)
                    st(last)

                    st(dve.tensor_scalar(flat(EX[:, 1]), flat(EX[:, 0]), 0.25, None, ALU.add))
                    ex, exr = EX[:].rearrange("p f a s n -> p (f a s n)"), EXR[:].rearrange("p f a s n -> p (f a s n)")
                    st(dve.tensor_scalar(exr, ex, MAGIC, None, ALU.add))
                    st(dve.tensor_scalar(exr, exr, MAGIC, None, ALU.subtract))
                    dve.tensor_tensor(ex, ex, exr, ALU.subtract).then_inc(sem("s5_ang"), 1)
                if c == 3:
                    dve.wait_ge(sem("s5_abs"), 1)
                    dve.wait_ge(sem("s5_sin"), 1)
                    st(dve.tensor_tensor(s5(12), s5(5), s5(5), ALU.mult))
                    st(dve.tensor_scalar(s5(12), s5(12), -2.0, 1.0, ALU.mult, ALU.add))
                    dve.tensor_tensor(s5(7), s5(1), s5(4), ALU.mult)
                    st(dve.tensor_tensor(s5(6), s5(1), s5(12), ALU.mult))
                    st(dve.tensor_scalar(s5(6), s5(6), -1.0, None, ALU.add))
                    dve.tensor_tensor(s5(11), re, re, ALU.mult)
                    st(dve.tensor_tensor(s5(12), im, im, ALU.mult))
                    st(dve.tensor_tensor(s5(8), s5(11), s5(12), ALU.add))
                    st(dve.reciprocal(s5(8), s5(8)))
                    dve.tensor_tensor(s5(11), s5(6), re, ALU.mult)
                    st(dve.tensor_tensor(s5(12), s5(7), im, ALU.mult))
                    st(dve.tensor_tensor(s5(9), s5(11), s5(12), ALU.add))
                    dve.tensor_tensor(s5(11), s5(7), re, ALU.mult)
                    st(dve.tensor_tensor(s5(12), s5(6), im, ALU.mult))
                    st(dve.tensor_tensor(s5(10), s5(11), s5(12), ALU.subtract))
                    for n in (9, 10):
                        last = dve.tensor_tensor(s5(n), s5(n), s5(8), ALU.mult)
                    st(last)

            def s5_cosines(kt):
                fine = [ESC[:, f, 0, 4 * kt:4 * kt + 4].unsqueeze(2).broadcast_to([P, 4, 16, 16]) for f in range(2)]
                coarse = [ESC[:, f, 1, 4 * kt:4 * kt + 4].unsqueeze(3).broadcast_to([P, 4, 16, 16]) for f in range(2)]
                e = ECS[:, kt % 2, 0]
                if kt >= 2:
                    dve.wait_ge(sem("s5_s"), 4 * (kt - 1))
                dve.tensor_tensor(e.rearrange("p s (a n) -> p s a n", a=16), coarse[1], fine[1], ALU.mult)
                st(dve.tensor_tensor(ET[:].rearrange("p s (a n) -> p s a n", a=16), coarse[0], fine[0], ALU.mult))
                st(dve.tensor_tensor(e, e, ET[:], ALU.subtract))

            def s5_state(s_):
                kt, a = s_ // 4, s_ % 4
                cs = ECS[:, kt % 2, 0, a].unsqueeze(1).broadcast_to([P, 2, T])
                sn = ECS[:, kt % 2, 1, a].unsqueeze(1).broadcast_to([P, 2, T])
                dve.wait_ge(sem("s5_bu"), s_ + 1)
                dve.wait_ge(sem("s5_sines"), 2 * kt + 2)
                bu = bank(4 + s_ % 2).rearrange("p (f t) -> p f t", f=2)
                dve.tensor_tensor(SM1[:], bu, cs, ALU.mult)
                dve.tensor_tensor(SM2[:], bu, sn, ALU.mult).then_inc(sem("s5_bu_read"), 1)
                dve.wait_ge(sem("s5_bu_read"), s_ + 1)
                dve.tensor_tensor(SM1[:, 0], SM1[:, 0], SM2[:, 1], ALU.add)
                st(dve.tensor_tensor(SM1[:, 1], SM1[:, 1], SM2[:, 0], ALU.subtract))
                if s_ >= 2:
                    dve.wait_ge(sem("s5_s"), s_ - 1)
                r = S5S[:, 1, s_:s_ + 1].broadcast_to([P, T])
                for f in range(2):
                    last = dve.tensor_tensor_scan(SZ[:, s_ % 2, f], r, SM1[:, f], 0.0, ALU.mult, ALU.add)
                last.then_inc(sem("s5_z"), 1)
                dve.wait_ge(sem("s5_z"), s_ + 1)

            def s5_beside(c):
                if c == 0:
                    dve.wait_ge(sem("s5w_in"), 32)
                    cf = [S5S[:, n].unsqueeze(2).broadcast_to([P, ST_TILES, 32]) for n in (9, 10)]

                    def m5(x):
                        return x.rearrange("p a t -> p (a t)").rearrange("p (k n) -> p k n", k=ST_TILES)
                    tmp = (SM1[:], SM2[:], SZ[:, 0], SZ[:, 1])
                    for o, v, f in zip(tmp, (0, 1, 0, 1), (0, 1, 1, 0)):
                        last = dve.tensor_tensor(m5(o), S5C[:, v], cf[f], ALU.mult)
                    st(last)
                    dve.tensor_tensor(S5C[:, 0], m5(tmp[0]), m5(tmp[1]), ALU.subtract)
                    st(dve.tensor_tensor(S5C[:, 1], m5(tmp[2]), m5(tmp[3]), ALU.add))
                    dve.tensor_scalar(S5C[:, 1], S5C[:, 1], -1.0, None, ALU.mult).then_inc(sem("s5_c"), 1)
                    dve.wait_ge(sem("s5_c"), 1)
                if c == 1:
                    dve.wait_ge(sem("s5_esc"), 1)
                    s5_cosines(0)
                s_ = c - 3
                if 0 <= s_ < ST_TILES:
                    s5_state(s_)
                    if s_ % 4 == 1 and s_ < 12:
                        s5_cosines(s_ // 4 + 1)
                if c >= 9 and c % 4 == 1:
                    kt = (c - 9) // 4
                    dve.wait_ge(sem("s5_cy"), 4 * kt + 4)
                    dve.scalar_tensor_tensor(U5[:, kt], U5[:, kt], col("s5_d", kt),
                                             PS[:, (6 + kt % 2) * NB:(6 + kt % 2) * NB + T],
                                             ALU.mult, ALU.add).then_inc(sem("s5_yk"), 1)

            wait_block(dve, G["down2"], 0, 3)
            feed(dve, to_lo, G["in_u"], [], beside=s5_steps)
            feed(dve, to_lo, G["in_x"], [x_taps], beside=s5_beside)
            feed(dve, to_lo, G["in_y"], [y_cube, y_gelu], beside=lambda c: s5_beside(12 + c))

            def lru_log(n):
                dve.wait_ge(sem("lru_ri"), n + 1)
                for h in range(LH):
                    t = n * LH + h
                    last = dve.tensor_scalar(LR[:, h], LR[:, h], 1.0, HALF[:, 60 + t:61 + t], ALU.add, ALU.mult)
                last.then_inc(sem("lru_y"), 1)

            def lru_mult(n):
                xs = XC[:, n * LH:(n + 1) * LH]
                st(dve.scalar_tensor_tensor(LI[:], LI[:], 1.0, xs, ALU.add, ALU.mult))
                dve.wait_ge(sem("lru_th"), n + 1)
                dve.scalar_tensor_tensor(LA[:], LT[:], 1.0, LA[:], ALU.add, ALU.mult).then_inc(sem("lru_m"), 1)

            def lru_scan(n):
                dve.wait_ge(sem("lru_sq"), n + 1)
                st(dve.memset(LA[:, :, 0:1], 1.0))
                st(dve.tensor_tensor(LI[:], LI[:], LA[:], ALU.mult))
                dve.wait_ge(sem("lru_a"), n + 1)
                dve.wait_ge(sem("lru_m"), n + 1)
                for h in range(LH):
                    last = dve.tensor_tensor_scan(LT[:, h], LR[:, h], LI[:, h], 0.0, ALU.mult, ALU.add)
                st(last)
                y = YG[:, n * LH:(n + 1) * LH]
                dve.scalar_tensor_tensor(y, LT[:], 0.25, y, ALU.mult, ALU.mult).then_inc(sem("lru_out"), 1)

            def beside_gates(c):
                if c == 0:
                    dve.wait_ge(sem("s5_yk"), S5_TILES)
                    dve.wait_ge(sem("s5_ysq"), 1)
                    st(dve.tensor_scalar(Y5B[:], Y5B[:], 0.044715, 1.0, ALU.mult, ALU.add))
                    dve.tensor_tensor(Y5B[:], Y5B[:], U5[:], ALU.mult).then_inc(sem("s5_yt"), 1)
                if c == 2:
                    dve.wait_ge(sem("s5_yth"), 1)
                    st(dve.scalar_tensor_tensor(Y5, Y5B[:], 1.0, U5[:], ALU.add, ALU.mult))
                    dve.tensor_scalar(Y5, Y5, 0.5, None, ALU.mult).then_inc(sem("s5_g"), 1)
                if c == 4:
                    dve.wait_ge(sem("s5_ghi"), 1)
                    dve.wait_ge(sem("s5_g"), 1)
                    dve.tensor_tensor(GLO[:], Y5, GHI[:].bitcast(F32), ALU.subtract).then_inc(sem("s5_glo"), 1)
                if c % 3 == 0:
                    lru_log(c // 3)
                elif c % 3 == 1:
                    lru_mult(c // 3)
                elif c % 3 == 2:
                    lru_scan(c // 3)

            def split_mixer(c):
                if c < 4:
                    k4 = slice(4 * ((c + 1) % 4), 4 * ((c + 1) % 4) + 4)
                    dve.wait_ge(hhi_ready, APPLY["lru"] + c + 1)
                    dve.tensor_tensor(ALO[:, k4], OUT5[:, 4 * c:4 * c + 4], AHI[:, k4].bitcast(F32), ALU.subtract)\
                       .then_inc(hlo_ready, 1)

            def proj_out(k):
                def s1(g, i, b):
                    wait_block(dve, g, i, b)
                    wait_stage(dve, "free", G[f"gates{k}"], 0, 1)
                    ps = proj_bank(k)
                    if k:
                        wait_stage(dve, "d2", G[f"proj{k - 1}"], 0, 0)
                    for v in range(2):
                        last = dve.scalar_tensor_tensor(PM[:, v], GT[k % 2][v][:], 1.0, ps[:, :, T * v:T * v + T],
                                                        ALU.add, ALU.mult)
                    last.then_inc(stage_sem["free"], 1)

                def s2(g, i, b):
                    wait_stage(dve, "free", g, i, b)
                    dve.wait_ge(hlo_ready, APPLY["lru"] + 4)
                    dve.tensor_tensor(MG[:, 4 * k:4 * k + 4], PM[:, 0], PM[:, 1], ALU.add)\
                       .then_inc(stage_sem["d2"], 1)
                return [s1, s2]

            feed(dve, to_lo, G["gates0"], [], beside=beside_gates)
            lru_scan(2)
            feed(dve, to_lo, G["glu"], [])
            wait_stage(dve, "free", G["glu"], 0, 0)
            st(dve.scalar_tensor_tensor(Y5, Y5B[:], 1.0, Y5, ALU.add, ALU.mult))
            dve.wait_ge(sem("lru_out"), 3)
            dve.tensor_scalar(Y5, Y5, 0.5, None, ALU.mult).then_inc(sem("s5_out"), 1)
            dve.wait_ge(sem("s5_out"), 1)
            feed(dve, to_lo, G["gates1"], [], beside=split_mixer)
            def split_merged(ch):
                sl = slice(4 * ch, 4 * ch + 4)
                dve.wait_ge(hhi_ready, APPLY["merged"] + ch + 1)
                dve.tensor_tensor(HLO[:, sl], MG[:, sl], HHI[:, sl].bitcast(F32), ALU.subtract).then_inc(hlo_ready, 1)

            for k in range(4):
                feed(dve, to_lo, G[f"proj{k}"], proj_out(k),
                     beside=lambda c: split_merged(c - 1) if k == 3 and c >= 1 else None)
                if k < 2:
                    feed(dve, to_lo, G[f"gates{k + 2}"], [])
            wait_stage(dve, "d2", G["proj3"], 0, 0)
            split_merged(3)

            def add_x(g, i, b):
                wait_block(dve, g, i, b)
                x = X[:, 4 * b:4 * b + 4]
                dve.tensor_tensor(x, narrow(g.b0 + b), x, ALU.add).then_inc(stage_sem["free"], 1)

            def router_lo(c):
                if c == 3:
                    dve.wait_ge(sem("wr_hi"), 1)
                    dve.tensor_tensor(WRL[:], WR[:], WRH[:].bitcast(F32), ALU.subtract).then_inc(sem("wr_lo"), 1)
            def add_half(g, i, b):
                wait_block(dve, g, i, b)
                x = X[:, 4 * b:4 * b + 4]
                dve.scalar_tensor_tensor(x, narrow(g.b0 + b), 0.5, x, ALU.mult, ALU.add).then_inc(stage_sem["free"], 1)
            feed(dve, to_lo, G["out2"], [add_half], beside=router_lo)
            wait_stage(dve, "free", G["out2"], 0, 3)
            var(5, False)
            apply(APPLY["moe"], TMPS["moe"], 4, TMP, lambda ch, k: X[:, 4 * ch + k],
                  lambda ch, k: col("norm_ffn", 4 * ch + k), lambda ch: RB[:, 0],
                  lambda ch, k: (HHI[:, 4 * ch:4 * ch + 4], HLO[:, 4 * ch:4 * ch + 4]))
            lg = RS[:, 0:2].rearrange("p a u e -> p (a u e)")[:, 0:72].rearrange("p (u e) -> p u e", u=2)
            gl = lg[:, :, 0:4]

            def r(n, m):
                return RS[:, n, :, 0:m]

            def first_of(best, values, n, slot, dst):
                it = CST[:, C_IOTA:C_IOTA + n].unsqueeze(1).broadcast_to([P, TT, n])
                st(dve.tensor_tensor(r(slot, n), values, best.broadcast_to([P, TT, n]), ALU.is_equal))
                st(dve.tensor_scalar(r(slot, n), r(slot, n), -1000.0, 1000.0, ALU.mult, ALU.add))
                st(dve.tensor_tensor(r(slot, n), r(slot, n), it, ALU.add))
                st(dve.tensor_reduce(r(slot + 1, 1), r(slot, n), AX.X, ALU.min))
                st(dve.tensor_tensor(dst, it, r(slot + 1, 1).broadcast_to([P, TT, n]), ALU.is_equal))

            def router(c):
                if c == 5:
                    dve.wait_ge(sem("r_cols"), 1)
                    dve.wait_ge(sem("rbias_in"), 16)
                    st(dve.tensor_tensor(lg, bank(7, 72).rearrange("p (u e) -> p u e", u=2),
                                         RBIAS[:].unsqueeze(1).broadcast_to([P, TT, 36]), ALU.add))
                    st(dve.reduce_max(r(4, 1), gl, axis=AX.X))
                    dve.tensor_tensor(r(2, 4), gl, r(4, 1).broadcast_to([P, TT, 4]), ALU.subtract).then_inc(sem("r_shift"), 1)
                    first_of(r(4, 1), gl, 4, 5, r(3, 4))
                if c == 6:
                    dve.wait_ge(sem("r_exp"), 1)
                    st(dve.reduce_sum(r(4, 1), r(2, 4), axis=AX.X))
                    st(dve.reciprocal(r(4, 1), r(4, 1)))
                    el = lg[:, :, 4:36].rearrange("p u (g e) -> p u g e", g=4)
                    for u in range(TT):
                        last = dve.tensor_tensor(RS[:, 7, u].rearrange("p (g e) -> p g e", g=4), el[:, u],
                                                 r(3, 4)[:, u].unsqueeze(2).broadcast_to([P, 4, 8]), ALU.mult)
                    st(last)
                    for u in range(TT):
                        last = dve.reduce_sum(RS[:, 8, u, 0:8], RS[:, 7, u].rearrange("p (g e) -> p e g", g=4), axis=AX.X)
                    st(last)
                    st(dve.reduce_max(r(9, 1), r(8, 8), axis=AX.X))
                    st(dve.tensor_copy(r(10, 1), r(9, 1)))
                    first_of(r(10, 1), r(8, 8), 8, 5, r(11, 8))
                    st(dve.scalar_tensor_tensor(r(8, 8), r(11, 8), -BIG, r(8, 8), ALU.mult, ALU.add))
                    st(dve.reduce_max(r(12, 1), r(8, 8), axis=AX.X))
                    first_of(r(12, 1), r(8, 8), 8, 5, r(13, 8))
                    dve.tensor_tensor(r(9, 1), r(12, 1), r(10, 1), ALU.subtract).then_inc(sem("r_gap"), 1)
                if c == 7:
                    dve.wait_ge(sem("r_gape"), 1)
                    st(dve.tensor_scalar(r(10, 1), r(9, 1), 1.0, None, ALU.add))
                    st(dve.reciprocal(r(10, 1), r(10, 1)))
                    st(dve.tensor_tensor(r(10, 1), r(10, 1), r(4, 1), ALU.mult))
                    st(dve.tensor_tensor(r(9, 1), r(9, 1), r(10, 1), ALU.mult))
                    dve.tensor_tensor(r(11, 8), r(11, 8), r(10, 1).broadcast_to([P, TT, 8]), ALU.mult)
                    st(dve.tensor_tensor(r(13, 8), r(13, 8), r(9, 1).broadcast_to([P, TT, 8]), ALU.mult))
                    st(dve.tensor_tensor(r(11, 8), r(11, 8), r(13, 8), ALU.add))
                    for u in range(TT):
                        last = dve.tensor_tensor(RS[:, 14, u].rearrange("p (g e) -> p g e", g=4),
                                                 r(3, 4)[:, u].unsqueeze(2).broadcast_to([P, 4, 8]),
                                                 r(11, 8)[:, u].unsqueeze(1).broadcast_to([P, 4, 8]), ALU.mult)
                    last.then_inc(sem("r_comb"), 1)

            def moe_first(g, i, b):
                wait_stage(dve, "a2", g, i, b)
                ps = narrow(g.b0 + b)
                st(dve.scalar_tensor_tensor(MS1[:], MTH[:], 1.0, ps[:, 0:2], ALU.add, ALU.mult))
                dve.scalar_tensor_tensor(MF[:, b], MS1[:], 0.5, ps[:, 2:4], ALU.mult, ALU.mult)\
                   .then_inc(stage_sem["free"], 1)
                wait_stage(dve, "free", g, i, b)

            def moe_mid(e0):
                def s2(g, i, b):
                    wait_stage(dve, "a2", g, i, b)
                    ps = narrow(g.b0 + b)
                    st(dve.scalar_tensor_tensor(MS1[:], MTH[:], 1.0, ps[:, 0:2], ALU.add, ALU.mult))
                    dve.scalar_tensor_tensor(MS2[:], MS1[:], 0.5, ps[:, 2:4], ALU.mult, ALU.mult)\
                       .then_inc(stage_sem["free"], 1)
                    wait_stage(dve, "free", g, i, b)
                    cb = CB[:, bass.ds(mult(i, 2) + b + e0, 1)].rearrange("p e t -> p (e t)")\
                        .unsqueeze(1).broadcast_to([P, 2, T])
                    dve.tensor_tensor(MACT[:], MS2[:], cb, ALU.mult).then_inc(stage_sem["d2"], 1)
                return s2

            def moe_lo(off):
                def s3(g, i, b):
                    wait_stage(dve, "a3", g, i, b)
                    wait_stage(dve, "d2", g, i, b)
                    k = bass.ds(mult(i, 4) + 2 * b + off, 2)
                    dve.tensor_tensor(ALO[:, k], MACT[:], AHI[:, k].bitcast(F32), ALU.subtract)\
                       .then_inc(stage_sem["d3"], 1)
                return s3

            feed(dve, to_lo, G["moe_first"], [moe_first], beside=router)
            dve.wait_ge(sem("cb"), 8)
            for b in range(FIRST_EXPERTS):
                dve.tensor_tensor(MF[:, b], MF[:, b], CB[:, b].unsqueeze(1).broadcast_to([P, 2, T]), ALU.mult)\
                   .then_inc(sem("first_act"), 1)
            for b in range(FIRST_EXPERTS):
                dve.wait_ge(sem("first_hi"), b + 1)
                dve.tensor_tensor(ALO[:, 2 * b:2 * b + 2], MF[:, b], AHI[:, 2 * b:2 * b + 2].bitcast(F32),
                                  ALU.subtract).then_inc(sem("first_lo"), 1)
            for part in range(4):
                e0 = 8 * part or FIRST_EXPERTS
                feed(dve, to_lo, G[f"moe_up{part}"], [moe_mid(e0), nothing, moe_lo(0 if part else 2 * FIRST_EXPERTS)],
                     st, 1)
                if part:
                    wait_stage(dve, "free", G[f"moe_down{part - 1}"], 0, 3)
                feed(dve, to_lo, G[f"moe_down{part}"], [add_x])
            var(6, False)
            wait_block(dve, G["moe_down3"], 0, 3)
            for ch in range(4):
                for k in range(4 * ch, 4 * ch + 4):
                    last = dve.scalar_tensor_tensor(OUTB[:, k], X[:, k], col("norm_final", k), RB[:, 0],
                                                    ALU.mult, ALU.mult)
                last.then_inc(sem("out_ready"), 1)

        @block.tensor
        def _(pe):
            pe.sem_inc(slot_used, 2)
            pe.sem_inc(stage_sem["free"], 2)
            ident, rev = CST[:, C_ID:C_ID + P], CST[:, C_REV:C_REV + P]

            def slot(g, i, b, q, products):
                c = b * g.slots + q
                par = (g.m0 + c) % 2
                wait_place(pe, g, i, c, RING)
                last = products(par, q)
                last.then_inc(slot_used, 1)

            def mod_sums(w, free):
                pe.wait_ge(stage_sem["free"], free)
                for mb in range(max(2 * w - 1, 0), min(2 * w + 1, MOD_REST)):
                    pe.wait_ge(lo_done, G["mk"].s0 + (4 * mb + 3) // 2 * 3 + (4 * mb + 3) % 2 + 2 + RING)
                    for j in range(4):
                        at_ = mod_sums_at(w) + 4 * (mb - 2 * w + 1) + j
                        last = pe.matmul(PS[:, at_:at_ + 1], MACC[:, mb % 2, P * j:P * j + P], ONES[:, 0:1],
                                         start=True, stop=True)
                last.then_inc(sem("mod_sums_read"), 1)

            def by_chunk(n):
                return lambda q: pe.wait_ge(hlo_ready, n + q + 1)

            def by_block(up):
                return lambda q: wait_stage(pe, "d3", up, 0, 2 * q + 1)

            def blocks(g, products, beside=None, ready=None):
                def one(i, b):
                    pe.wait_ge(stage_sem["free"], mult(i, 2) + (g.base.get("free", 0) + b + 1))
                    w = (g.m0 - G["mk"].m0) // 4 + b
                    if w and (g.extra or g.name == "mq" and b == 0):
                        pe.wait_ge(sem("mod_rest"), w if g.extra else w + 1)
                    for q in range(g.slots):
                        if ready:
                            ready(q)
                        slot(g, i, b, q, products(g, i, b))
                        if beside:
                            beside(b * g.slots + q)
                        if g.extra and q == 1:
                            mod_sums(w, g.base["free"] + b + 2)
                if g.blocks >= 4 and 2 * g.slots % RING == 0:
                    with pe.Fori(0, g.blocks // 2) as i:
                        one(i, 0)
                        one(i, 1)
                else:
                    for b in range(g.blocks):
                        one(0, b)

            def weights_still(hi, lo, wide_):
                def products(g, i, b):
                    ps = wide(g.b0 + b) if wide_ else narrow(g.b0 + b)

                    def run(par, q):
                        for k in range(SLOT_K):
                            kt = SLOT_K * q + k
                            end = q == g.slots - 1 and k == SLOT_K - 1
                            for j in range(4):
                                out = ps[:, j]
                                first = q == 0 and k == 0 and (wide_ or j % 2 == 0)
                                w = slice(P * j, P * j + P)
                                pe.matmul(out, WHI[:, par, k, w], hi(kt), start=first, stop=False)
                                pe.matmul(out, WHI[:, par, k, w], lo(kt), start=False, stop=False)
                                last = pe.matmul(out, WLO[:, par, k, w], hi(kt), start=False,
                                                 stop=end and (wide_ or j % 2 == 1))
                        return last
                    return run
                return products

            def tokens_still(g, i, b):
                ps = wide(g.b0 + b)

                def run(par, q):
                    for k in range(SLOT_K):
                        kt = SLOT_K * q + k
                        end = q == g.slots - 1 and k == SLOT_K - 1
                        for j in range(4):
                            x = [h[:, j // 2, kt, P * (j % 2):P * (j % 2) + P] for h in (H1HI, H1LO)]
                            pe.matmul(ps[:, j], x[0], WHI[:, par, k], start=q == 0 and k == 0, stop=False)
                            pe.matmul(ps[:, j], x[1], WHI[:, par, k], start=False, stop=False)
                            last = pe.matmul(ps[:, j], x[0], WLO[:, par, k], start=False, stop=end)
                    return last
                return run

            def stats(n):
                for ch in range(4):
                    pe.wait_ge(sq_done, 4 * n + ch + 1)
                    for k in range(4):
                        last = pe.matmul(bank(7, T), ONES[:], SQ[:, ch % 2, k], start=ch == 0 and k == 0,
                                         stop=ch == 3 and k == 3)
                    last.then_inc(ss_done, 1)

            def first_stats(squares, at_, n):
                pe.wait_ge(sq_done, squares)
                for k in range(n):
                    sq = SQW[:, bass.ds(at_ + k, 1)].rearrange("p e s t -> p (e s) t")
                    last = pe.matmul(bank(7).rearrange("p (s t) -> p s t", s=2), ONES[:], sq,
                                     start=isinstance(at_, int) and at_ + k == 0,
                                     stop=isinstance(at_, int) and at_ + k == KT - 1)
                return last

            def mod(g, i, b):
                par_b = b % 2

                def run(par, q):
                    for k in range(SLOT_K):
                        kt = SLOT_K * q + k
                        out = PS[0:4, par_b * NB:par_b * NB + NB]
                        pe.matmul(out, C4[:, kt], WHI[:, par, k], start=q == 0 and k == 0, stop=False)
                        last = pe.matmul(out, C4[:, kt], WLO[:, par, k], start=False,
                                         stop=q == g.slots - 1 and k == SLOT_K - 1)
                    return last
                return run

            def mod_cols(g, i, b):
                wait_stage(pe, "free", g, i, b)
                for j in range(4):
                    at_ = 6 * NB + 8 * b + 2 * j + mult(i, 16)
                    last = pe.matmul(PS[:, bass.ds(at_, 2)], MROW[:, b % 2, P * j:P * j + P],
                                     CST[0:4, C_PAIR:C_PAIR + 2], start=True, stop=True)
                return last

            pe.wait_ge(sem("c_ready"), 2)
            pe.wait_ge(sem("const_in"), 16)
            pe.wait_ge(sem("ones"), 1)
            g = G["mod"]

            def mod_block(i, b):
                pe.wait_ge(stage_sem["free"], mult(i, 2) + (b + 1))
                for q in range(g.slots):
                    slot(g, i, b, q, mod(g, i, b))
            mod_block(0, 0)
            first_stats(1, 0, 2)
            with pe.Fori(0, (g.blocks - 2) // 2) as i:
                mod_block(i, 1)
                mod_cols(g, i, 0)
                mod_block(i, 2)
                mod_cols(g, i, 1)
                first_stats(i + 2, i * 4 + 2, 4).then_inc(ss_done, 1)
            first_stats(4, KT - 2, 2).then_inc(ss_done, 1)
            mod_block(0, g.blocks - 1)
            mod_cols(g, 0, g.blocks - 2)
            mod_cols(g, 0, g.blocks - 1).then_inc(sem("mod_cols"), 1)
            all_free(pe, G["mod"])
            pe.wait_ge(rec_done, 1)

            def gate_rows(c):
                if c == 2:
                    pe.wait_ge(hlo_ready, 8)
                    pe.wait_ge(sem("wg_lo"), 1)
                    for k in range(KT):
                        out = PS[0:4 * HEADS, 6 * NB:7 * NB].rearrange("p (s t) -> p s t", s=2)
                        pe.matmul(out, WGH[:, k], H1HI[:, :, k], start=k == 0, stop=False)
                        pe.matmul(out, WGH[:, k], H1LO[:, :, k], start=False, stop=False)
                        last = pe.matmul(out, WGL[:, k], H1HI[:, :, k], start=False, stop=k == KT - 1)
                    last.then_inc(sem("gate_mm"), 1)
                    pe.wait_ge(sem("gates_copied"), 1)
                    pe.wait_ge(sem("mod_rest"), 1)
                    for kind in range(4):
                        pick = ident[0:4 * HEADS, HEADS * kind:HEADS * kind + HEADS]
                        parts = ([(0, GALL[:, T:2 * T]), (T, GALL[:, 0:T])] if kind < 2 else [(0, GALL[:, ::-1])])
                        for at_, rhs in parts:
                            c0 = (4 + kind) * NB + at_
                            last = pe.matmul(PS[0:HEADS, c0:c0 + rhs.shape[1]], pick, rhs, start=True, stop=True)
                    last.then_inc(sem("grow_mm"), 1)
                if c == 3:
                    pe.wait_ge(sem("grow"), 1)
            blocks(G["mk"], weights_still(lambda k: H1HI[:, :, k], lambda k: H1LO[:, :, k], True), gate_rows,
                   ready=lambda q: pe.wait_ge(hlo_ready, 2 * q + 2))

            def gate_cols(c):
                if c == 1:
                    all_free(pe, G["mk"])
                    pe.wait_ge(sem("gate_emt"), 1)
                    for d in range(2):
                        for j in range(4):
                            at_ = 6 * NB + HEADS * (4 * d + j)
                            pe.matmul(PS[:, at_:at_ + HEADS], GROW[:, d, P * j:P * j + P], ident[0:HEADS, 0:HEADS],
                                      start=True, stop=True)
                        for u in range(TT):
                            at_ = 6 * NB + 64 + HEADS * (2 * d + u)
                            last = pe.matmul(PS[:, at_:at_ + HEADS], GROW[:, 2, T * d + P * u:T * d + P * u + P],
                                             ident[0:HEADS, 0:HEADS], start=True, stop=True)
                    last.then_inc(sem("a_cols"), 1)
                if c == 3:
                    pe.wait_ge(sem("a_copied"), 1)
            blocks(G["mv"], tokens_still, gate_cols)
            blocks(G["dk"], weights_still(lambda k: H1HI[:, :, k], lambda k: H1LO[:, :, k], True))
            blocks(G["dv"], tokens_still)

            mod_sums(MOD_REST // 2, G["mq"].base["free"] + 1)
            latent = weights_still(lambda k: H1HI[:, 0, k], lambda k: H1LO[:, 0, k], False)
            blocks(G["mq"], latent)
            blocks(G["dq"], latent)

            def rotate(r):
                v = DK[:, 2 * r:2 * r + 2, 0, :] if r < 4 else DQ[:, 2 * (r - 4):2 * (r - 4) + 2, :]
                if r == 0:
                    all_free(pe, G["dv"])
                if r == 4:
                    all_free(pe, G["dq"])
                if r >= 2:
                    pe.wait_ge(sem("roped"), r - 1)
                pe.matmul(bank(4 + r % 2).rearrange("p (h t) -> p h t", h=2), CST[:, C_ROT:C_ROT + P], v,
                          start=True, stop=True).then_inc(sem("rot"), 1)
            blocks(G["mo"], latent, rotate)

            all_free(pe, G["mo"])
            wait_stage(pe, "d2", G["mq"], 0, 1)

            def m_scores(h):
                if h >= 2:
                    pe.wait_ge(sem("m_p"), 2 * (h - 1))
                if h == 7:
                    pe.wait_ge(sem("mixm_done"), 1)
                for j in range(4):
                    at_ = (h % 2) * 1024 + T * j
                    last = pe.matmul(PS[:, at_:at_ + T], MK[:, h, j // 2, P * (j % 2):P * (j % 2) + P], MQ[:, h],
                                     start=True, stop=True)
                last.then_inc(sem("m_s"), 1)
                for d in range(2):
                    if h:
                        pe.wait_ge(sem("m_w"), 2 * (h - 1) + d + 1)
                    if h == 0:
                        pe.wait_ge(sem("roped"), 8)
                    pe.matmul(bank(4 + d).rearrange("p (r t) -> p r t", r=2),
                              ident[0:HEADS, h:h + 1].broadcast_to([HEADS, P]),
                              NEGM[:, d].unsqueeze(1).broadcast_to([HEADS, 2, T]), start=True, stop=False)
                    mask = CST[:, C_MF + P * d:C_MF + P * d + P].unsqueeze(1).broadcast_to([P, 2, P])
                    pe.matmul(PS[:, (4 + d) * NB + T:(5 + d) * NB].rearrange("p (r t) -> p r t", r=2),
                              ident, mask, start=False, stop=True).then_inc(sem("m_bc"), 1)

            def m_values(h):
                for d in range(2):
                    pe.wait_ge(sem("m_p"), 2 * h + d + 1)
                    if h:
                        pe.wait_ge(sem("m_num"), 2 * (h - 1) + d + 1)
                    for u in range(TT):
                        keys = [2, 3] + [j for j in range(2) if (j <= u if d == 0 else j >= u)]
                        for j in keys:
                            at_ = (6 + d) * NB + 129 * u
                            last = pe.matmul(PS[:, at_:at_ + 129], MP[:, d, j, P * u:P * u + P], MV[:, j, h],
                                             start=j == keys[0], stop=j == keys[-1])
                    last.then_inc(sem("m_pv"), 1)

            def m_transposes(half):
                pe.wait_ge(sem("m_h"), half + 1)
                for hh in range(4):
                    for u in range(TT):
                        at_ = m_transposed(half) + T * hh + P * u
                        last = pe.transpose(PS[:, at_:at_ + P], MH[:, u, hh], ident)
                last.then_inc(sem("m_t"), 1)

            U = 2 * HEADS

            def d_scores(u):
                pe.wait_ge(sem("m_p"), 2 * HEADS)
                if u >= 2:
                    pe.wait_ge(sem("d_e"), u - 1)
                for c in range(2):
                    half_ = slice(64 * c, 64 * c + 64)
                    last = pe.matmul(bank(2 * (u % 2) + c).rearrange("p (s t) -> p s t", s=2),
                                     DQ[half_, u // 2, P * (u % 2):P * (u % 2) + P], DK[half_, u // 2],
                                     start=True, stop=True)
                last.then_inc(sem("d_s"), 1)

            m_scores(0)
            for h in range(HEADS):
                if h < HEADS - 1:
                    m_scores(h + 1)
                m_values(h)
                if h == 5:
                    m_transposes(0)
            d_scores(0)
            d_scores(1)
            m_transposes(1)

            def d_transposes(u):
                pe.wait_ge(sem("d_p"), u + 1)
                if u >= 2:
                    pe.wait_ge(sem("d_tc"), u - 1)
                for j in range(4):
                    at_ = (4 + u % 2) * NB + P * j
                    last = pe.transpose(PS[:, at_:at_ + P], DP[:, u % 2, P * j:P * j + P], ident)
                last.then_inc(sem("d_t"), 1)

            def d_values(u):
                pe.wait_ge(sem("d_tc"), u + 1)
                if u >= 2:
                    pe.wait_ge(sem("d_oc"), u - 1)
                for j in range(4):
                    last = pe.matmul(bank(6 + u % 2, P), DPT[:, u % 2, j], DV[:, j, u // 2], start=j == 0, stop=j == 3)
                last.then_inc(sem("d_o"), 1)

            pe.wait_ge(sem("mixm_done"), 2)
            for u in range(2, U + 3):
                if u < U:
                    d_scores(u)
                if 2 <= u < U + 2:
                    d_transposes(u - 2)
                if u >= 3:
                    d_values(u - 3)
            pe.wait_ge(sem("d_on"), 1)
            for h in range(HEADS):
                for u in range(TT):
                    at_ = T * h + P * u
                    last = pe.transpose(PS[:, at_:at_ + P], DO[:, u, h], ident)
            last.then_inc(sem("d_ot"), 1)

            here = weights_still(lambda k: HHI[:, k], lambda k: HLO[:, k], False)
            inner = weights_still(lambda k: AHI[:, k], lambda k: ALO[:, k], False)
            blocks(G["wout"], here, ready=by_chunk(APPLY["mix"]))
            stats(1)
            stats(2)
            for part in range(3):
                blocks(G[f"up{part}"], here, ready=None if part else by_chunk(APPLY["ffn"]))
                blocks(G[f"down{part}"], inner, ready=by_block(G[f"up{part}"]))
            stats(3)
            stats(4)
            def s5_in(s):
                a, kt = s % 4, s // 4
                pe.wait_ge(sem("s5w_in"), 32)
                if s >= 2:
                    pe.wait_ge(sem("s5_bu_read"), s - 1)
                rows = slice(32 * a, 32 * a + 32)
                for f in range(2):
                    at_ = (4 + s % 2) * NB + T * f
                    last = pe.matmul(PS[:, at_:at_ + T], S5B[rows, f, kt], U5[rows, kt], start=True, stop=True)
                last.then_inc(sem("s5_bu"), 1)

            def s5_out(s):
                a, kt = s % 4, s // 4
                pe.wait_ge(sem("s5_s"), s + 1)
                pe.wait_ge(sem("s5_c"), 1)
                if kt >= 2 and a == 0:
                    pe.wait_ge(sem("s5_yk"), kt - 1)
                for f in range(2):
                    last = pe.matmul(PS[32 * a:32 * a + 32, (6 + kt % 2) * NB:(6 + kt % 2) * NB + T],
                                     S5C[:, f, s], SST[:, s % 2, f], start=f == 0, stop=f == 1)
                last.then_inc(sem("s5_cy"), 1)

            def lru_gates(n):
                pe.wait_ge(sem("lw_in"), 16 * (n + 1) if n == 2 else 32)
                if n:
                    pe.wait_ge(sem("lru_ri"), n)
                for h in range(LH):
                    for v in range(2):
                        at_ = (4 + h) * NB + T * v
                        last = pe.matmul(PS[:, at_:at_ + T], LW[:, n % 2, v, h], XC[:, n * LH + h], start=True, stop=True)
                    last.then_inc(sem("lru_mm"), 1)

            def s5_beside(c):
                if c == 1:
                    wait_stage(pe, "free", G["in_u"], 0, 0)
                if 0 <= c - 1 < ST_TILES:
                    s5_in(c - 1)
                if 0 <= c - 4 < ST_TILES:
                    s5_out(c - 4)
                if c == 23:
                    pe.wait_ge(sem("s5_yk"), S5_TILES)
                    lru_gates(0)

            blocks(G["in_u"], here, ready=by_chunk(APPLY["mix2"]))
            blocks(G["in_x"], here, s5_beside)
            blocks(G["in_y"], here, lambda c: s5_beside(12 + c))
            blocks(G["gates0"], here, lambda c: lru_gates(1) if c == 2 else lru_gates(2) if c == 5 else None)
            pe.wait_ge(sem("s5_glo"), 1)
            blocks(G["glu"], weights_still(lambda k: GHI[:, k], lambda k: GLO[:, k], False))
            blocks(G["gates1"], here)

            def proj(k):
                def products(g, i, b):
                    ps = proj_bank(k)

                    def run(par, q):
                        for kk in range(SLOT_K):
                            kt = SLOT_K * q + kk
                            end = q == g.slots - 1 and kk == SLOT_K - 1
                            for j in range(4):
                                out, w = ps[:, j, 0:T] if q == 0 else ps[:, j, T:2 * T], slice(P * j, P * j + P)
                                pe.matmul(out, WHI[:, par, kk, w], AHI[:, kt], start=q == 0 and kk == 0, stop=False)
                                pe.matmul(out, WHI[:, par, kk, w], ALO[:, kt], start=False, stop=False)
                                last = pe.matmul(out, WLO[:, par, kk, w], AHI[:, kt], start=False, stop=end)
                        return last
                    return run
                return products

            pe.wait_ge(hlo_ready, APPLY["lru"] + 4)
            pe.wait_ge(sem("lru_ri"), 3)
            for k in range(4):
                if k == 3:
                    wait_stage(pe, "free", G["gates3"], 0, 1)
                blocks(G[f"proj{k}"], proj(k))
                if k < 2:
                    blocks(G[f"gates{k + 2}"], here)
            wait_stage(pe, "free", G["proj3"], 0, 0)
            blocks(G["out2"], here, ready=by_chunk(APPLY["merged"]))
            stats(5)

            def router(c):
                if c == 3:
                    pe.wait_ge(sem("wr_lo"), 1)
                    for k in range(KT):
                        out = PS[0:36, 6 * NB:6 * NB + T]
                        pe.matmul(out, WRH[:, k], HHI[:, k], start=k == 0, stop=False)
                        pe.matmul(out, WRH[:, k], HLO[:, k], start=False, stop=False)
                        last = pe.matmul(out, WRL[:, k], HHI[:, k], start=False, stop=k == KT - 1)
                    last.then_inc(sem("r_mm"), 1)
                if c == 4:
                    pe.wait_ge(sem("r_rows"), 1)
                    pe.wait_ge(rec_done, 6)
                    for u in range(TT):
                        last = pe.matmul(bank(7)[:, 36 * u:36 * u + 36], RLT[:, P * u:P * u + P], ident[0:36, 0:36],
                                         start=True, stop=True)
                    last.then_inc(sem("r_cols"), 1)
                if c == 7:
                    pe.wait_ge(sem("r_comb"), 1)
                    for u in range(TT):
                        at_ = 7 * NB + P * u
                        last = pe.matmul(PS[0:EXPERTS, at_:at_ + P], RS[:, 14, u], ident, start=True, stop=True)
                    last.then_inc(sem("r_combT"), 1)
                    pe.wait_ge(sem("combT"), 1)
                    for q in range(8):
                        if q >= 2:
                            pe.wait_ge(sem("cb"), q - 1)
                        for j in range(4):
                            e = 4 * q + j
                            last = pe.matmul(narrow(q, 2)[:, j], ident[0:EXPERTS, e:e + 1].broadcast_to([EXPERTS, P]),
                                             COMBT[:], start=True, stop=True)
                        last.then_inc(sem("cb_mm"), 1)
            blocks(G["moe_first"], here, router, ready=by_chunk(APPLY["moe"]))

            def first_part(q):
                if q == 0:
                    pe.wait_ge(sem("first_lo"), FIRST_EXPERTS)
                else:
                    wait_stage(pe, "d3", G["moe_up0"], 0, 2 * q + 1 - FIRST_EXPERTS)

            for part in range(4):
                blocks(G[f"moe_up{part}"], here)
                blocks(G[f"moe_down{part}"], inner, ready=by_block(G[f"moe_up{part}"]) if part else first_part)
            stats(6)


def columns(v):
    return np.ascontiguousarray(np.asarray(v).reshape(-1, P).T)


def kernel(**inputs):
    import numpy as _np
    import concourse.bacc as _bacc
    from concourse import mybir as _mybir
    from concourse.bass_utils import run_bass_kernel_spmd as _run

    a = {k: _np.asarray(v) for k, v in inputs.items()}
    cols = {"c": columns(a["c"]), "c_ctx": columns(a["c_ctx"]), "b_mod": columns(a["b_mod"]),
            "norm_mix": columns(a["norm_mix_w_2"]), "norm_ffn": columns(a["norm_ffn_w_2"]),
            "norm_final": columns(a["norm_final_w_2"]), "g_mlstm": columns(a["g_mlstm"]),
            "g_diff": columns(a["g_diff"]), "b_gate2": columns(a["b_gate_2"]),
            "lam_re": columns(a["s5_lam_re_2"]), "lam_im": columns(a["s5_lam_im_2"]),
            "log_step": columns(_np.repeat(a["s5_log_step_2"], 64)),
            "s5_d": columns(a["s5_d_2"]), "b_glu": columns(a["s5_b_glu_2"]),
            "lru_b_a": columns(a["lru_b_a_2"]), "lru_b_x": columns(a["lru_b_x_2"]),
            "lru_lambda": columns(a["lru_lambda_2"]),
            "lru_conv_w": columns(a["lru_conv_w_2"]), "lru_conv_b": columns(a["lru_conv_b_2"])}
    for n in ("g_pre_mix", "g_post_mix", "g_pre_ffn", "g_post_ffn", "conv_qk_w", "conv_qk_b", "conv_ffn_w", "conv_ffn_b"):
        cols[n] = columns(a[n])

    def token_cols(x):
        return _np.ascontiguousarray(x.reshape(T, KT, P).transpose(2, 1, 0).reshape(P, KT * T))

    def rows(w):
        n = w.shape[1]
        return _np.ascontiguousarray(w.reshape(-1, P, n).transpose(1, 0, 2).reshape(P, -1))

    s5_b = _np.zeros((P, 2, 4, P), _np.float32)
    s5_c = _np.zeros((P, 2, ST_TILES, 32), _np.float32)
    for f, (b, c) in enumerate(((a["s5_b_re_2"][0], a["s5_c_re_2"][0]), (a["s5_b_im_2"][0], a["s5_c_im_2"][0]))):
        for g in range(32):
            tile, half = g // 2, g % 2
            at = 32 * (tile % 4) + 16 * half
            s5_b[at:at + 16, f, tile // 4, 64 * half:64 * half + 64] = b[g].T
            s5_c[64 * half:64 * half + 64, f, tile, 16 * half:16 * half + 16] = c[g].T
    lru_w = _np.stack([a["lru_w_a_2"][0], a["lru_w_x_2"][0]]).transpose(2, 0, 1, 3).reshape(P, -1)
    arrays = {
        "cols": _np.concatenate([cols[n] for n, _ in COLS], axis=1),
        "consts": shape_constants(),
        "xT": token_cols(a["x"][0]), "ctxT": token_cols(a["ctx"][0]),
        "lamv": _np.tile(_np.concatenate([a[n].ravel() for n in ("lambda_q1", "lambda_k1", "lambda_q2", "lambda_k2")]), (P, 1)),
        "b_gateT": a["b_gate"][0].T,
        "b_router": _np.tile(_np.concatenate([a["b_router_group_2"][0], a["b_router_expert_2"][0]]), (P, 1)),
        "w_gates": rows(a["w_in"][0][:, 4096:4128]),
        "w_router": rows(_np.concatenate([a["w_router_group_2"][0], a["w_router_expert_2"][0]], axis=1)),
        "s5_b": s5_b.reshape(P, -1), "s5_c": s5_c.reshape(P, -1), "lru_w": lru_w,
        "w_mod": a["w_mod"][0], "w_in": a["w_in"][0], "w_out": a["w_out"][0], "w_up": a["w_up"][0],
        "w_down": a["w_down"][0], "w_in_2": a["w_in_2"][0], "s5_w_glu_2": a["s5_w_glu_2"][0],
        "w_proj_s5_2": a["w_proj_s5_2"][0], "w_proj_lru_2": a["w_proj_lru_2"][0], "w_out_2": a["w_out_2"][0],
        "w_e_gate_2": a["w_e_gate_2"][0].reshape(EXPERTS * D, E_FF),
        "w_e_up_2": a["w_e_up_2"][0].reshape(EXPERTS * D, E_FF),
        "w_e_down_2": a["w_e_down_2"][0].reshape(EXPERTS * E_FF, D),
    }
    arrays = {n: _np.ascontiguousarray(v) for n, v in arrays.items()}
    nc = _bacc.Bacc("TRN2", target_bir_lowering=False, num_devices=1)
    aps = {n: nc.dram_tensor("in_" + n, v.shape, _mybir.dt.from_np(v.dtype), kind="ExternalInput").ap()
           for n, v in arrays.items()}
    aps["out"] = nc.dram_tensor("out_T", (P, KT * T), _mybir.dt.float32, kind="ExternalOutput").ap()
    program(nc, aps)
    r = _run(nc, [{"in_" + n: v for n, v in arrays.items()}], core_ids=[0])
    out = r.results[0]["out_T"]
    return _np.ascontiguousarray(out.reshape(P, KT, T).transpose(2, 1, 0).reshape(1, T, D))
```
